# Optimizing a Trainium2 kernel written in Bass

```python
import math
import jax
import jax.numpy as jnp
from jax import lax
import numpy as np
import jax, jax.numpy as jnp

D_MODEL = 1024
BATCH = 1
SEQ = 512
DEPTH = 1

A_WIDTH = 256
A_GROUPS = 4
A_GDIM = A_WIDTH // A_GROUPS
CHUNK = 128
B_WIDTH = 256
POOL_WINDOWS = (2, 4, 8, 16)
B_GROUPS = len(POOL_WINDOWS)
B_GDIM = B_WIDTH // B_GROUPS
C_HEADS = 4
C_HEAD_DIM = 64
C_VDIM = 2 * C_HEAD_DIM
C_QK_WIDTH = C_HEADS * 2 * C_HEAD_DIM
C_V_WIDTH = C_HEADS * C_VDIM
Q_BLOCK = 128
N_BUCKETS = 32
MAX_EXACT = 16
MAX_DISTANCE = 128
IN_COLS = 2 * A_WIDTH + B_WIDTH + 2 * C_QK_WIDTH + C_V_WIDTH
N_BRANCH = 3
D_FF = 2816
CONV_WIDTH = 3
EPS = 1e-6


def rmsnorm(x, g, eps=EPS):
    xf = x.astype(jnp.float32)
    y = xf * lax.rsqrt(jnp.mean(xf * xf, axis=-1, keepdims=True) + eps)
    return (y * g.astype(jnp.float32)).astype(x.dtype)

def layernorm(x, g, b, eps=1e-5):
    xf = x.astype(jnp.float32)
    mu = jnp.mean(xf, axis=-1, keepdims=True)
    var = jnp.mean(jnp.square(xf - mu), axis=-1, keepdims=True)
    y = (xf - mu) * lax.rsqrt(var + eps)
    return (y * g.astype(jnp.float32) + b.astype(jnp.float32)).astype(x.dtype)

def gmlp_mixer(zuv, ln_g, ln_b, w_s, b_s):
    B, S, _ = zuv.shape
    z = jax.nn.gelu(zuv, approximate=False)
    u, v = z[..., :A_WIDTH], z[..., A_WIDTH:]
    v = layernorm(v, ln_g, ln_b)
    vc = v.reshape(B, S // CHUNK, CHUNK, A_GROUPS, A_GDIM)
    mask = jnp.tril(jnp.ones((CHUNK, CHUNK), dtype=bool))
    ws = jnp.where(mask[None], w_s, jnp.zeros_like(w_s))
    mixed = jnp.einsum('gts,bcsgd->bctgd', ws, vc) + b_s.T[None, None, :, :, None]
    return u * mixed.reshape(B, S, A_WIDTH)

def pool_mixer(xb, pool_w, pool_scale):
    B, S, _ = xb.shape
    xf = xb.astype(jnp.float32)
    cs = jnp.cumsum(xf, axis=1)
    t = jnp.arange(S)
    outs = []
    for gi, w in enumerate(POOL_WINDOWS):
        sl = slice(gi * B_GDIM, (gi + 1) * B_GDIM)
        c = cs[..., sl]
        lag = jnp.pad(c, ((0, 0), (w, 0), (0, 0)))[:, :S]
        cnt = jnp.minimum(t + 1, w).astype(jnp.float32)[None, :, None]
        outs.append((c - lag) / cnt - xf[..., sl])
    p = jnp.stack(outs, axis=2).astype(xb.dtype)
    y = jnp.einsum('bsgc,gcd->bsgd', p, pool_w).reshape(B, S, B_WIDTH)
    return y * pool_scale

def t5_causal_bucket(rel):
    n = jnp.maximum(rel, 0)
    nf = jnp.maximum(n, 1).astype(jnp.float32)
    large = MAX_EXACT + (jnp.log(nf / MAX_EXACT) / math.log(MAX_DISTANCE / MAX_EXACT)
                         * (N_BUCKETS - MAX_EXACT)).astype(jnp.int32)
    large = jnp.minimum(large, N_BUCKETS - 1)
    return jnp.where(n < MAX_EXACT, n, large)

def diff_attention(q, k, v, lam, rel_bias):
    B, S, H, _, dh = q.shape
    nb = S // Q_BLOCK
    scale = dh ** -0.5
    qb = q.reshape(B, nb, Q_BLOCK, H, 2, dh).transpose(1, 0, 2, 3, 4, 5)
    kpos = jnp.arange(S)

    def block(args):
        qi, i = args
        qpos = i * Q_BLOCK + jnp.arange(Q_BLOCK)
        rel = qpos[:, None] - kpos[None, :]
        bias = rel_bias[t5_causal_bucket(rel)].astype(jnp.float32)
        s = jnp.einsum('bqhcd,bkhcd->bhcqk', qi, k).astype(jnp.float32) * scale
        s = s + bias.transpose(2, 0, 1)[None, :, None]
        s = jnp.where((rel >= 0)[None, None, None], s, -1e30)
        p = jax.nn.softmax(s, axis=-1)
        a = p[:, :, 0] - lam * p[:, :, 1]
        return jnp.einsum('bhqk,bkhd->bqhd', a.astype(v.dtype), v)

    out = lax.map(block, (qb, jnp.arange(nb)))
    return out.transpose(1, 0, 2, 3, 4).reshape(B, S, H, v.shape[-1])

def diff_attn_mixer(zq, zk, zv, lam_vecs, subln_g, rel_bias, layer_idx):
    B, S, _ = zq.shape
    q = zq.reshape(B, S, C_HEADS, 2, C_HEAD_DIM)
    k = zk.reshape(B, S, C_HEADS, 2, C_HEAD_DIM)
    v = zv.reshape(B, S, C_HEADS, C_VDIM)
    lam_init = 0.8 - 0.6 * math.exp(-0.3 * layer_idx)
    lv = lam_vecs.astype(jnp.float32)
    lam = jnp.exp(jnp.sum(lv[0] * lv[1])) - jnp.exp(jnp.sum(lv[2] * lv[3])) + lam_init
    o = diff_attention(q, k, v, lam, rel_bias)
    o = rmsnorm(o, subln_g, eps=1e-5) * (1.0 - lam_init)
    return o.reshape(B, S, C_V_WIDTH)

def conv_ffn(h, w_up, conv_w, conv_b, w_down):
    gu = h @ w_up
    gate, up = gu[..., :D_FF], gu[..., D_FF:]
    gate = lax.conv_general_dilated(
        gate, conv_w[:, None, :], window_strides=(1,), padding=[(CONV_WIDTH - 1, 0)],
        dimension_numbers=('NWC', 'WIO', 'NWC'), feature_group_count=D_FF) + conv_b
    return (jax.nn.gelu(gate, approximate=False) * up) @ w_down

def first_inputs(seed: int = 0) -> dict:
    key = jax.random.key(seed)
    ks = jax.random.split(key, 24)
    L, D = DEPTH, D_MODEL

    def nrm(k, shape, scale):
        return jax.random.normal(k, shape, jnp.float32) * scale

    def gain(k, shape):
        return 1.0 + nrm(k, shape, 0.05)

    return {
        'x': nrm(ks[0], (BATCH, SEQ, D), 1.0),
        'attn_norm_g': gain(ks[1], (L, D)),
        'w_in': nrm(ks[2], (L, D, IN_COLS), D ** -0.5),
        'w_gate': nrm(ks[3], (L, D, N_BRANCH * D), D ** -0.5),
        'b_gate': nrm(ks[4], (L, N_BRANCH * D), 0.01),
        'sgu_ln_g': gain(ks[5], (L, A_WIDTH)),
        'sgu_ln_b': nrm(ks[6], (L, A_WIDTH), 0.01),
        'sgu_w': nrm(ks[7], (L, A_GROUPS, CHUNK, CHUNK), CHUNK ** -0.5),
        'sgu_b': gain(ks[8], (L, A_GROUPS, CHUNK)),
        'proj_a': nrm(ks[9], (L, A_WIDTH, D), A_WIDTH ** -0.5),
        'pool_w': nrm(ks[10], (L, B_GROUPS, B_GDIM, B_GDIM), B_GDIM ** -0.5),
        'pool_scale': gain(ks[11], (L, B_WIDTH)),
        'proj_b': nrm(ks[12], (L, B_WIDTH, D), B_WIDTH ** -0.5),
        'diff_lam': nrm(ks[13], (L, 4, C_HEAD_DIM), 0.1),
        'diff_subln_g': gain(ks[14], (L, C_VDIM)),
        'proj_c': nrm(ks[15], (L, C_V_WIDTH, D), C_V_WIDTH ** -0.5),
        'w_out': nrm(ks[16], (L, D, D), D ** -0.5),
        'ffn_norm_g': gain(ks[17], (L, D)),
        'w_up': nrm(ks[18], (L, D, 2 * D_FF), D ** -0.5),
        'conv_w': nrm(ks[19], (L, CONV_WIDTH, D_FF), CONV_WIDTH ** -0.5),
        'conv_b': nrm(ks[20], (L, D_FF), 0.01),
        'w_down': nrm(ks[21], (L, D_FF, D), D_FF ** -0.5),
        'rel_bias': nrm(ks[22], (N_BUCKETS, C_HEADS), 0.5),
        'final_norm_g': gain(ks[23], (D,)),
    }

def first_block(x, attn_norm_g, w_in, w_gate, b_gate, sgu_ln_g, sgu_ln_b, sgu_w, sgu_b,
              proj_a, pool_w, pool_scale, proj_b, diff_lam, diff_subln_g, proj_c, w_out,
              ffn_norm_g, w_up, conv_w, conv_b, w_down, rel_bias, final_norm_g):
    o_a = 2 * A_WIDTH
    o_b = o_a + B_WIDTH
    o_q = o_b + C_QK_WIDTH
    o_k = o_q + C_QK_WIDTH
    for l in range(DEPTH):
        h = rmsnorm(x, attn_norm_g[l])
        z = h @ w_in[l]
        gates = jax.nn.sigmoid(h @ w_gate[l] + b_gate[l])
        y_a = gmlp_mixer(z[..., :o_a], sgu_ln_g[l], sgu_ln_b[l], sgu_w[l], sgu_b[l])
        y_b = pool_mixer(z[..., o_a:o_b], pool_w[l], pool_scale[l])
        y_c = diff_attn_mixer(z[..., o_b:o_q], z[..., o_q:o_k], z[..., o_k:],
                              diff_lam[l], diff_subln_g[l], rel_bias, l)
        g_a = gates[..., :D_MODEL]
        g_b = gates[..., D_MODEL:2 * D_MODEL]
        g_c = gates[..., 2 * D_MODEL:]
        merged = g_a * (y_a @ proj_a[l]) + g_b * (y_b @ proj_b[l]) + g_c * (y_c @ proj_c[l])
        x = x + merged @ w_out[l]
        x = x + conv_ffn(rmsnorm(x, ffn_norm_g[l]), w_up[l], conv_w[l], conv_b[l], w_down[l])
    return rmsnorm(x, final_norm_g)


MEM_LEN = 256
A_HEADS = 8
A_HEAD_DIM = 64
A_WIDTH_2 = A_HEADS * A_HEAD_DIM
MOBA_BLOCK = 256
MOBA_TOPK = 3
G_HEADS = 4
G_WIDTH = D_MODEL - A_WIDTH_2
G_HEAD_V = G_WIDTH // G_HEADS
G_KEY_WIDTH = G_WIDTH // 2
G_HEAD_K = G_KEY_WIDTH // G_HEADS
G_GATE_RANK = 16
G_GATE_NORM = 16.0
G_CHUNK = 64
MIX_WIDTH = A_WIDTH_2 + G_WIDTH
IN_SPLITS = (A_WIDTH_2, A_WIDTH_2, A_WIDTH_2, G_KEY_WIDTH, G_KEY_WIDTH, G_WIDTH, G_GATE_RANK, G_WIDTH)
IN_COLS_2 = 3 * A_WIDTH_2 + 2 * G_KEY_WIDTH + G_WIDTH + G_GATE_RANK + G_WIDTH
X_HEADS = 4
X_HEAD_DIM = D_MODEL // X_HEADS
D_FF_2 = 4 * D_MODEL
RP_BUCKETS = 32
RP_MAX_DIST = 128


def rms_norm(x, g):
    xf = x.astype(jnp.float32)
    y = xf * lax.rsqrt(jnp.mean(xf * xf, axis=-1, keepdims=True) + EPS)
    return (y * g.astype(jnp.float32)).astype(x.dtype)

def rel_bucket(dist):
    max_exact = RP_BUCKETS // 2
    d = jnp.maximum(dist, 0)
    large = max_exact + (jnp.log(jnp.maximum(d, 1).astype(jnp.float32) / max_exact)
                         / math.log(RP_MAX_DIST / max_exact) * (RP_BUCKETS - max_exact)).astype(jnp.int32)
    large = jnp.minimum(large, RP_BUCKETS - 1)
    return jnp.where(d < max_exact, d, large)

def moba_attention(q, k, v, rp_table):
    B, T, H, dh = q.shape
    nb = -(-T // MOBA_BLOCK)
    pad = nb * MOBA_BLOCK - T
    kp = jnp.pad(k, ((0, 0), (0, pad), (0, 0), (0, 0)))
    vp = jnp.pad(v, ((0, 0), (0, pad), (0, 0), (0, 0)))
    kb = kp.reshape(B, nb, MOBA_BLOCK, H, dh).transpose(0, 3, 1, 2, 4)
    vb = vp.reshape(B, nb, MOBA_BLOCK, H, dh).transpose(0, 3, 1, 2, 4)
    nq = T // Q_BLOCK
    qc = q.reshape(B, nq, Q_BLOCK, H, dh).transpose(0, 1, 3, 2, 4).reshape(B * nq, H, Q_BLOCK, dh)
    scale = dh ** -0.5
    n_sel = min(MOBA_TOPK, nb - 1)
    table_t = rp_table.T.astype(jnp.float32)
    key_off = jnp.arange(MOBA_BLOCK, dtype=jnp.int32)
    hidx = jnp.arange(H)[:, None, None]
    b_ids = jnp.repeat(jnp.arange(B, dtype=jnp.int32), nq)
    qb_ids = jnp.tile(jnp.arange(nq, dtype=jnp.int32), B)
    xs = (qc, b_ids, qb_ids)
    if n_sel > 0:
        pos = jnp.arange(T, dtype=jnp.int32)
        q_blk = pos // MOBA_BLOCK
        kmean = jnp.mean(kb.astype(jnp.float32), axis=3)
        gate = jnp.einsum('bthd,bhnd->bhtn', q.astype(jnp.float32), kmean)
        past = jnp.arange(nb)[None, :] < q_blk[:, None]
        gate = jnp.where(past[None, None], gate, -jnp.inf)
        _, sel = lax.top_k(gate, n_sel)
        valid = sel < q_blk[None, None, :, None]
        sel_c = sel.reshape(B, H, nq, Q_BLOCK, n_sel).transpose(0, 2, 1, 3, 4).reshape(B * nq, H, Q_BLOCK, n_sel)
        valid_c = valid.reshape(B, H, nq, Q_BLOCK, n_sel).transpose(0, 2, 1, 3, 4).reshape(B * nq, H, Q_BLOCK, n_sel)
        xs = xs + (sel_c, valid_c)

    def step(args):
        qi, b, qb = args[0], args[1], args[2]
        kb_b = kb[b]
        vb_b = vb[b]
        q_pos = qb * Q_BLOCK + jnp.arange(Q_BLOCK, dtype=jnp.int32)
        own = (qb * Q_BLOCK) // MOBA_BLOCK
        k_own = lax.dynamic_index_in_dim(kb_b, own, axis=1, keepdims=False)
        v_own = lax.dynamic_index_in_dim(vb_b, own, axis=1, keepdims=False)
        d_own = q_pos[:, None] - (own * MOBA_BLOCK + key_off)[None, :]
        s_own = jnp.einsum('hqd,hld->hql', qi, k_own).astype(jnp.float32) * scale + table_t[:, rel_bucket(d_own)]
        s_own = jnp.where(d_own[None] >= 0, s_own, -jnp.inf)
        if n_sel > 0:
            sel_i, valid_i = args[3], args[4]
            k_sel = kb_b[hidx, sel_i]
            v_sel = vb_b[hidx, sel_i]
            d_sel = q_pos[None, :, None, None] - (sel_i[..., None] * MOBA_BLOCK + key_off)
            s_sel = (jnp.einsum('hqd,hqcld->hqcl', qi, k_sel).astype(jnp.float32) * scale
                     + table_t[hidx[..., None], rel_bucket(d_sel)])
            s_sel = jnp.where(valid_i[..., None], s_sel, -jnp.inf)
            s = jnp.concatenate([s_sel.reshape(H, Q_BLOCK, n_sel * MOBA_BLOCK), s_own], axis=-1)
            p = jax.nn.softmax(s, axis=-1).astype(v.dtype)
            p_sel = p[..., :n_sel * MOBA_BLOCK].reshape(H, Q_BLOCK, n_sel, MOBA_BLOCK)
            p_own = p[..., n_sel * MOBA_BLOCK:]
            return jnp.einsum('hqcl,hqcld->hqd', p_sel, v_sel) + jnp.einsum('hql,hld->hqd', p_own, v_own)
        p_own = jax.nn.softmax(s_own, axis=-1).astype(v.dtype)
        return jnp.einsum('hql,hld->hqd', p_own, v_own)

    o = lax.map(step, xs)
    return o.reshape(B, nq, H, Q_BLOCK, dh).transpose(0, 1, 3, 2, 4).reshape(B, T, H * dh)

def gla_chunked(q, k, v, log_a):
    B, T, H, dk = q.shape
    dv = v.shape[-1]
    nc = T // G_CHUNK
    scale = dk ** -0.5

    def to_chunks(t):
        return t.reshape(B, nc, G_CHUNK, H, t.shape[-1]).transpose(1, 0, 3, 2, 4)

    causal = jnp.tril(jnp.ones((G_CHUNK, G_CHUNK), dtype=bool))

    def body(S, inp):
        qi, ki, vi, gi = inp
        qf = qi.astype(jnp.float32) * scale
        kf = ki.astype(jnp.float32)
        vf = vi.astype(jnp.float32)
        b = jnp.cumsum(gi.astype(jnp.float32), axis=2)
        o_inter = jnp.einsum('bhcd,bhde->bhce', qf * jnp.exp(b), S)
        diff = b[:, :, :, None, :] - b[:, :, None, :, :]
        decay = jnp.exp(jnp.where(causal[None, None, :, :, None], diff, -jnp.inf))
        A = jnp.einsum('bhid,bhjd,bhijd->bhij', qf, kf, decay)
        o_intra = jnp.einsum('bhij,bhje->bhie', A, vf)
        b_last = b[:, :, -1:, :]
        S_new = jnp.exp(b_last[:, :, 0, :])[..., None] * S + jnp.einsum('bhcd,bhce->bhde', kf * jnp.exp(b_last - b), vf)
        return S_new, o_inter + o_intra

    S0 = jnp.zeros((B, H, dk, dv), jnp.float32)
    _, o = lax.scan(body, S0, (to_chunks(q), to_chunks(k), to_chunks(v), to_chunks(log_a)))
    return o.transpose(1, 0, 3, 2, 4).reshape(B, T, H, dv).astype(v.dtype)

def second_inputs(seed: int = 0) -> dict:
    key = jax.random.key(seed)
    ks = jax.random.split(key, 20)

    def nrm(k, shape, scale):
        return jax.random.normal(k, shape, jnp.float32) * scale

    def gain(k, shape):
        return 1.0 + 0.05 * jax.random.normal(k, shape, jnp.float32)

    L = DEPTH
    return {
        "x": nrm(ks[0], (BATCH, SEQ, D_MODEL), 1.0),
        "mem": nrm(ks[1], (BATCH, MEM_LEN, D_MODEL), 1.0),
        "rp_table": nrm(ks[2], (RP_BUCKETS, A_HEADS), 0.5),
        "norm_mix": gain(ks[3], (L, D_MODEL)),
        "w_in": nrm(ks[4], (L, D_MODEL, IN_COLS_2), D_MODEL ** -0.5),
        "w_gate_up": nrm(ks[5], (L, G_GATE_RANK, G_KEY_WIDTH), G_GATE_RANK ** -0.5),
        "b_gate": nrm(ks[6], (L, G_KEY_WIDTH), 0.1),
        "g_norm": gain(ks[7], (L, G_HEAD_V)),
        "w_out": nrm(ks[8], (L, MIX_WIDTH, D_MODEL), MIX_WIDTH ** -0.5),
        "norm_xattn": gain(ks[9], (L, D_MODEL)),
        "norm_mem": gain(ks[10], (L, D_MODEL)),
        "w_xq": nrm(ks[11], (L, D_MODEL, D_MODEL), D_MODEL ** -0.5),
        "w_xkv": nrm(ks[12], (L, D_MODEL, 2 * D_MODEL), D_MODEL ** -0.5),
        "w_xo": nrm(ks[13], (L, D_MODEL, D_MODEL), D_MODEL ** -0.5),
        "norm_mlp": gain(ks[14], (L, D_MODEL)),
        "w_up": nrm(ks[15], (L, D_MODEL, D_FF_2), D_MODEL ** -0.5),
        "w_down": nrm(ks[16], (L, D_FF_2, D_MODEL), D_FF_2 ** -0.5),
        "norm_final": gain(ks[17], (D_MODEL,)),
    }

def second_block(x, mem, rp_table, norm_mix, w_in, w_gate_up, b_gate, g_norm, w_out,
              norm_xattn, norm_mem, w_xq, w_xkv, w_xo, norm_mlp, w_up, w_down, norm_final):
    B, T, _ = x.shape
    M = mem.shape[1]
    offsets = [int(o) for o in np.cumsum(IN_SPLITS)[:-1]]
    for l in range(DEPTH):
        h = rms_norm(x, norm_mix[l])
        proj = h @ w_in[l]
        qa, ka, va, qg, kg, vg, glr, rg = jnp.split(proj, offsets, axis=-1)
        o_a = moba_attention(qa.reshape(B, T, A_HEADS, A_HEAD_DIM),
                             ka.reshape(B, T, A_HEADS, A_HEAD_DIM),
                             va.reshape(B, T, A_HEADS, A_HEAD_DIM), rp_table)
        log_a = jax.nn.log_sigmoid((glr @ w_gate_up[l] + b_gate[l]).astype(jnp.float32)) / G_GATE_NORM
        o_g = gla_chunked(qg.reshape(B, T, G_HEADS, G_HEAD_K),
                          kg.reshape(B, T, G_HEADS, G_HEAD_K),
                          vg.reshape(B, T, G_HEADS, G_HEAD_V),
                          log_a.reshape(B, T, G_HEADS, G_HEAD_K))
        o_g = rms_norm(o_g, g_norm[l]).reshape(B, T, G_WIDTH) * jax.nn.silu(rg)
        x = x + jnp.concatenate([o_a, o_g], axis=-1) @ w_out[l]
        h = rms_norm(x, norm_xattn[l])
        m = rms_norm(mem, norm_mem[l])
        qx = (h @ w_xq[l]).reshape(B, T, X_HEADS, X_HEAD_DIM)
        kx, vx = jnp.split(m @ w_xkv[l], 2, axis=-1)
        kx = kx.reshape(B, M, X_HEADS, X_HEAD_DIM)
        vx = vx.reshape(B, M, X_HEADS, X_HEAD_DIM)
        s = jnp.einsum('bthd,bmhd->bhtm', qx, kx).astype(jnp.float32) * (X_HEAD_DIM ** -0.5)
        p = jax.nn.softmax(s, axis=-1).astype(vx.dtype)
        ox = jnp.einsum('bhtm,bmhd->bthd', p, vx).reshape(B, T, D_MODEL)
        x = x + ox @ w_xo[l]
        h = rms_norm(x, norm_mlp[l])
        x = x + jnp.square(jax.nn.relu(h @ w_up[l])) @ w_down[l]
    return rms_norm(x, norm_final)


def setup_inputs(seed=0):
    out = dict(first_inputs(seed))
    for name, value in second_inputs(seed + 1).items():
        if name != "x":
            out[name + "_2"] = value
    return out


def reference(
    x, attn_norm_g, w_in, w_gate, b_gate, sgu_ln_g, sgu_ln_b, sgu_w, sgu_b, proj_a, pool_w,
    pool_scale, proj_b, diff_lam, diff_subln_g, proj_c, w_out, ffn_norm_g, w_up, conv_w, conv_b,
    w_down, rel_bias, final_norm_g, mem_2, rp_table_2, norm_mix_2, w_in_2, w_gate_up_2,
    b_gate_2, g_norm_2, w_out_2, norm_xattn_2, norm_mem_2, w_xq_2, w_xkv_2, w_xo_2, norm_mlp_2,
    w_up_2, w_down_2, norm_final_2,
):
    x = first_block(
        x, attn_norm_g, w_in, w_gate, b_gate, sgu_ln_g, sgu_ln_b, sgu_w, sgu_b, proj_a, pool_w,
        pool_scale, proj_b, diff_lam, diff_subln_g, proj_c, w_out, ffn_norm_g, w_up, conv_w,
        conv_b, w_down, rel_bias, final_norm_g,
    )
    return second_block(
        x, mem_2, rp_table_2, norm_mix_2, w_in_2, w_gate_up_2, b_gate_2, g_norm_2, w_out_2,
        norm_xattn_2, norm_mem_2, w_xq_2, w_xkv_2, w_xo_2, norm_mlp_2, w_up_2, w_down_2,
        norm_final_2,
    )


_drawn_inputs = setup_inputs


def setup_inputs(seed=0):
    import zlib

    import numpy as np

    out = dict(_drawn_inputs(seed))
    spreads = {}
    factors = {'b_gate': 8.0,
     'sgu_ln_g': 3.821,
     'sgu_ln_b': 8.0,
     'sgu_b': 2.968,
     'diff_lam': 6.582,
     'conv_b': 8.0,
     'b_gate_2': 2.76,
     'g_norm_2': 3.052,
     'norm_xattn_2': 8.0,
     'norm_mem_2': 7.251,
     'norm_mlp_2': 5.9}
    for name, (base, spread) in spreads.items():
        noise = np.random.default_rng([zlib.crc32(name.encode()), seed]).standard_normal(out[name].shape)
        drawn = base * np.exp(spread * noise) if base else spread * noise
        out[name] = jnp.asarray(drawn.astype(out[name].dtype))
    for name, factor in factors.items():
        out[name] = (out[name] * factor).astype(out[name].dtype)
    return out
```

```python
import math

import numpy as np

import concourse.bass as bass
from concourse import mybir

F32 = mybir.dt.float32
F32R = mybir.dt.float32r
U32 = mybir.dt.uint32
ALU = mybir.AluOpType
ACT = mybir.ActivationFunctionType
AX_X = mybir.AxisListType.X

P = 128
D = 1024
KT = D // P
T = 512
TT = T // P
RING = 4
AHEAD = 3
FF1 = 2816
FT1 = FF1 // P
DOWN1 = (8, 7, 7)
NB = 32
LINE = 640
NEG = -1.0e30
LAM_INIT = 0.8 - 0.6 * math.exp(0.0)

P_U, P_VA, P_POOL, P_Q, P_K, P_V, P_GATE, P_PROJ, P_WOUT, P_UP, P_DOWN = 0, 2, 4, 6, 10, 14, 18, 42, 50, 58, 102
P_END1 = P_DOWN + 3 * KT
(P_QA, P_KA, P_VA2, P_PAIRS, P_VG, P_GLR, P_XV, P_WOUT2, P_XQ, P_XO, P_UP_A, P_DOWN_A, P_UP_B, P_DOWN_B,
 P_END) = (P_END1 + n for n in (0, 4, 8, 12, 28, 32, 33, 41, 49, 57, 65, 81, 97, 113, 129))
E_U, E_VA, E_POOL, E_Q, E_K, E_V, E_GATE, E_PROJ, E_WOUT, E_UP, E_DOWN = 0, 2, 4, 6, 10, 14, 18, 42, 66, 74, 118
E_END1 = E_DOWN + KT
(E_QA, E_KA, E_VA2, E_PAIRS, E_VG, E_GLR, E_XV, E_WOUT2, E_XQ, E_XO, E_UP_A, E_DOWN_A, E_UP_B, E_DOWN_B,
 E_END) = (E_END1 + n for n in (0, 4, 8, 12, 28, 32, 33, 37, 45, 53, 61, 77, 85, 101, 109))
M = 256
MT = M // P
FF2 = 4096
FH = FF2 // P // 2
CHUNK = 64
NC = T // CHUNK
LEVELS = (32, 16, 8, 4, 2, 1)
XSCALE = 1.0 / 16

VEC = {}


def _vec_columns():
    at = 0
    for name, n in (("attn_norm_g", 8), ("b_gate", 24), ("ffn_norm_g", 8), ("conv0", 22), ("conv1", 22),
                    ("conv2", 22), ("conv_b", 22), ("final_norm_g", 8), ("subln", 1), ("pool_scale", 2),
                    ("norm_mix", 8), ("b_gate2", 2), ("g_norm", 1), ("norm_xattn", 8), ("norm_mem", 8),
                    ("norm_mlp", 8), ("norm_final", 8)):
        VEC[name] = at
        at += n
    return at


NVEC = _vec_columns()


class Panel:

    def __init__(self, first, step=0, i=0):
        self.first, self.step, self.i = first, step, i
        self.slot = first % RING
        self.index = first + step * i if step else first
        self.round = first // RING + 1 + (step // RING) * i if step else first // RING + 1

    def plus(self, n):
        return Panel(self.first + n, self.step, self.i)


class Steps:

    def __init__(self, eng, sem):
        self.eng, self.sem, self.n, self.per, self.i = eng, sem, 0, 0, 0

    def enter(self, i, per):
        self.i, self.per, self.start = i, per, self.n

    def leave(self, count):
        assert self.n - self.start == self.per, (self.n - self.start, self.per)
        self.n = self.start + self.per * count
        self.per = 0

    def mark(self, ins):
        ins.then_inc(self.sem, 1)
        self.n += 1

    def wait(self):
        self.eng.wait_ge(self.sem, self.n + self.per * self.i if self.per else self.n)

    def link(self, ins):
        self.mark(ins)
        self.wait()


def pairs_offset(qb):
    return P * (qb * (qb + 1) // 2)


SCORES = pairs_offset(TT)


def turned_offset(kb):
    return P * (kb * TT - kb * (kb - 1) // 2)


class Names:
    pass


def semaphores(nc):
    s = Names()

    def named(names):
        return [nc.alloc_semaphore(name) for name in names.split()]

    (s.panel_done, s.lo_ready, s.hi_ready, s.evac) = named(
        "panel_done lo_ready hi_ready evac")
    (s.steps, s.vec_in, s.consts_in, s.early_in) = named(
        "steps vec_in consts_in early_in")
    (s.line_in, s.lines_out, s.lines_set, s.line_done) = named(
        "line_in lines_out lines_set line_done")
    (s.line_copied, s.x_hi, s.x_squared, s.h_ready) = named(
        "line_copied x_hi x_squared h_ready")
    (s.sums, s.col_done, s.mean_ready, s.pow_done) = named(
        "sums col_done mean_ready pow_done")
    (s.diag_ready, s.row_done, s.row_ready, s.u_ready) = named(
        "diag_ready row_done row_ready u_ready")
    (s.va_gelu, s.ln_mean, s.ln_pow, s.v_normed) = named(
        "va_gelu ln_mean ln_pow v_normed")
    (s.ws_masked, s.spatial_done, s.pooled, s.poolmm_done) = named(
        "ws_masked spatial_done pooled poolmm_done")
    (s.lam_dots, s.lam_exps, s.v_done, s.qk_hi) = named(
        "lam_dots lam_exps v_done qk_hi")
    (s.qk_ready, s.v_hi, s.v_ready, s.bias_in) = named(
        "qk_ready v_hi v_ready bias_in")
    (s.score_done, s.scored, s.negated, s.exped) = named(
        "score_done scored negated exped")
    (s.blended, s.turned, s.turned_hi, s.turned_ready) = named(
        "blended turned turned_hi turned_ready")
    (s.pv_done, s.o_evac, s.gated, s.o_squared) = named(
        "pv_done o_evac gated o_squared")
    (s.ocol_done, s.omean_ready, s.opow_done, s.odiag_ready) = named(
        "ocol_done omean_ready opow_done odiag_ready")
    (s.orow_done, s.o_normed, s.yc_hi, s.yc_ready) = named(
        "orow_done o_normed yc_hi yc_ready")
    (s.yab_written, s.yab_hi, s.yab_ready, s.m_summed) = named(
        "yab_written yab_hi yab_ready m_summed")
    (s.m_hi, s.m_ready, s.tapped, s.conved) = named(
        "m_hi m_ready tapped conved")
    (s.gelued, s.acted, s.act_hi, s.act_ready) = named(
        "gelued acted act_hi act_ready")
    (s.out_done, s.x_second, s.sums2, s.act_steps) = named(
        "out_done x_second sums2 act_steps")
    (s.pow_a, s.mean_b, s.rowa_done, s.rowa_ready) = named(
        "pow_a mean_b rowa_done rowa_ready")
    (s.mem_in, s.mem_hi, s.mem_sq, s.mem_sums) = named(
        "mem_in mem_hi mem_sq mem_sums")
    (s.mem_ready, s.mcol_done, s.mmean_ready, s.mpow_done) = named(
        "mem_ready mcol_done mmean_ready mpow_done")
    (s.mdiag_ready, s.mrow_done, s.mrow_ready, s.late_in) = named(
        "mdiag_ready mrow_done mrow_ready late_in")
    (s.logit_done, s.logit_abs, s.soft_ready, s.b_ready) = named(
        "logit_done logit_abs soft_ready b_ready")
    (s.b_exped, s.qb_ready, s.kd_shift, s.kd_exped) = named(
        "b_exped qb_ready kd_shift kd_exped")
    (s.kd_ready, s.kd_turned, s.kd_copied, s.last_exped) = named(
        "kd_ready kd_turned kd_copied last_exped")
    (s.updates_done, s.states_ready, s.shifted, s.level_exped) = named(
        "updates_done states_ready shifted level_exped")
    (s.level_ready, s.level_done, s.level_taken, s.og_done) = named(
        "level_ready level_done level_taken og_done")
    (s.og_evac, s.og_squared, s.gcol_done, s.gmean_ready) = named(
        "og_evac og_squared gcol_done gmean_ready")
    (s.gpow_done, s.gdiag_ready, s.grow_done, s.og_normed) = named(
        "gpow_done gdiag_ready grow_done og_normed")
    (s.y_hi, s.y_ready, s.xq_hi, s.xq_ready) = named(
        "y_hi y_ready xq_hi xq_ready")
    (s.xkv_hi, s.xkv_ready, s.xscore_done, s.xneg) = named(
        "xkv_hi xkv_ready xscore_done xneg")
    (s.xexped, s.xblended, s.xturned, s.xturned_hi) = named(
        "xexped xblended xturned xturned_hi")
    (s.xturned_ready, s.xpv_done, s.ox_hi, s.ox_ready) = named(
        "xturned_ready xpv_done ox_hi ox_ready")
    (s.acted2, s.act2_hi, s.act2_ready, s.final_scaled) = named(
        "acted2 act2_hi act2_ready final_scaled")
    (s.mem_scaled, s.diag_a, s.silued) = named(
        "mem_scaled diag_a silued")
    s.load = named(" ".join(f"load{n}" for n in range(RING)))
    s.x_in = named(" ".join(f"x_in{n}" for n in range(4)))
    return s


def build(nc, dram, out):
    s = semaphores(nc)
    b = place(nc)
    scratch = nc.dram_tensor("bias_lines", (12, P * LINE), F32).ap()
    with nc.Block() as block:
        @block.sync
        def _(sp):
            sync_program(nc, sp, s, b, dram, scratch, out)

        @block.scalar
        def _(act):
            scalar_program(nc, act, s, b, dram, scratch)

        @block.vector
        def _(dve):
            vector_program(nc, dve, s, b)

        @block.gpsimd
        def _(pool):
            gpsimd_program(nc, pool, s, b)

        @block.tensor
        def _(pe):
            tensor_program(nc, pe, s, b)


KB = 1024


def place(nc):
    b = Names()
    base = (nc.sbuf_base + 31) // 32 * 32

    def at(name, offset, shape, dt=F32):
        return nc.alloc_sbuf_tensor_at(name, [P] + shape, dt, offset=base + int(offset))

    off = [0]

    def nxt(name, shape, dt=F32):
        start = off[0]
        off[0] += (4 * int(np.prod(shape)) + 31) // 32 * 32
        return at(name, start, shape, dt)

    b.x = nxt("x", [KT, T])
    b.hh = nxt("hh", [KT, T], F32R)
    b.hl = nxt("hl", [KT, T], F32R)
    b.stage = nxt("stage", [RING, D])
    b.wh = nxt("wh", [RING, D], F32R)
    b.wl = nxt("wl", [RING, D], F32R)
    b.rrow = nxt("rrow", [T])
    b.sumsq = nxt("sumsq", [T])
    b.tmp = nxt("tmp", [2, T])
    b.diag = nxt("diag", [2, T])
    b.consts = nxt("consts", [2, P])
    b.vec = nxt("vec", [NVEC])
    b.half_bg = nxt("half_bg", [24])
    b.gg = nxt("gg", [8])
    b.small = nxt("small", [96])
    b.mx = nxt("mx", [8])
    b.neg = nxt("neg", [8])
    b.sums = nxt("sums", [8])
    b.rec = nxt("rec", [8])
    b.turn = nxt("turn", [8])
    b.small2 = nxt("small2", [64])
    r0 = off[0]
    R = lambda kb: r0 + kb * KB
    b.qk = at("qk", R(0), [8, T])
    b.v = at("v", R(16), [TT, 512])
    b.qh = at("qh", R(24), [T], F32R)
    b.ql = at("ql", R(26), [T], F32R)
    b.kh = at("kh", R(28), [T], F32R)
    b.kl = at("kl", R(30), [T], F32R)
    b.vh = at("vh", R(32), [TT, P], F32R)
    b.vl = at("vl", R(34), [TT, P], F32R)
    b.s = at("s", R(36), [2, SCORES])
    b.th = at("th", R(46), [SCORES], F32R)
    b.tl = at("tl", R(51), [SCORES], F32R)
    b.ga = at("ga", R(56), [16, T])
    b.yab = at("yab", R(88), [4, T])
    b.o = at("o", R(96), [4, T])
    b.bias = at("bias", R(104), [T])
    b.lines = at("lines", R(24), [12, LINE])
    b.u = at("u", R(56), [2, T])
    b.va = at("va", R(60), [TT, 256])
    b.early = at("early", R(64), [D])
    b.ws = at("ws", R(68), [4, P])
    b.inv = at("inv", R(70), [2, T])
    b.xb = at("xb", R(74), [2, T + 16])
    b.s1 = at("s1", R(74) + 4 * 2 * (T + 16), [T + 16])
    b.s2 = at("s2", R(74) + 4 * 3 * (T + 16), [T + 16])
    b.poolw = at("poolw", R(74) + 4 * 4 * (T + 16), [2, 64])
    b.pool = at("pool", R(84), [2, T])
    b.onehot = at("onehot", R(96), [T])
    b.tables = at("tables", R(98), [12 * P])
    b.gatec = at("gatec", R(36), [8, T])
    b.osq = at("osq", R(52), [2, T])
    b.yabh = at("yabh", R(0), [4, T], F32R)
    b.yabl = at("yabl", R(8), [4, T], F32R)
    b.ych = at("ych", R(16), [4, T], F32R)
    b.ycl = at("ycl", R(24), [4, T], F32R)
    b.mh = at("mh", R(56), [8, T], F32R)
    b.ml = at("ml", R(72), [8, T], F32R)
    b.ah = at("ah", R(0), [FT1, T], F32R)
    b.al = at("al", R(44), [FT1, T], F32R)
    b.gb = at("gb", R(88), [2, T + 2])
    b.cb = at("cb", R(93), [2, T])
    b.sq2 = at("sq2", R(97), [2, T])
    b.sum2 = at("sum2", R(101), [T])
    b.bias2 = at("bias2", R(56), [2, T])
    b.mem = at("mem", R(60), [KT, M])
    b.oa = at("oa", R(60), [4, T])
    b.zg = at("zg", R(68), [4, T])
    b.rg = at("rg", R(76), [4, T])
    b.memh = at("memh", R(84), [KT, M], F32R)
    b.meml = at("meml", R(92), [KT, M], F32R)
    b.kx = at("kx", R(100), [KT, M])
    b.mrow = at("mrow", R(108), [M])
    b.msum = at("msum", R(109), [M])
    b.rowa = at("rowa", R(110), [T])
    b.vg = at("vg", R(0), [TT, 512])
    b.b = at("b", R(8), [2, T])
    b.reset = at("reset", R(12), [T])
    b.la = at("la", R(14), [2, T])
    b.qe = at("qe", R(14), [2, T])
    b.gsq = at("gsq", R(14), [2, T])
    b.ke = at("ke", R(18), [2, T])
    b.a = at("a", R(22), [2, T])
    b.masks = at("masks", R(26), [len(LEVELS) + 1, P])
    b.kdt = at("kdt", R(30), [TT, P])
    b.states = at("states", R(32), [NC, P])
    b.og = at("og", R(36), [4, T])
    b.vx = at("vx", R(44), [MT, D])
    b.glr = at("glr", R(52), [T])
    b.wgu = at("wgu", R(54), [256])
    b.yh2 = at("yh2", R(68), [KT, T], F32R)
    b.yl2 = at("yl2", R(84), [KT, T], F32R)
    b.qxh = at("qxh", R(0), [2, T], F32R)
    b.qxl = at("qxl", R(4), [2, T], F32R)
    b.kxh = at("kxh", R(8), [2, M], F32R)
    b.kxl = at("kxl", R(10), [2, M], F32R)
    b.vxh = at("vxh", R(12), [MT, 256], F32R)
    b.vxl = at("vxl", R(14), [MT, 256], F32R)
    b.xs = at("xs", R(16), [TT, M])
    b.xth = at("xth", R(20), [MT, T], F32R)
    b.xtl = at("xtl", R(24), [MT, T], F32R)
    b.oxh = at("oxh", R(28), [KT, T], F32R)
    b.oxl = at("oxl", R(52), [KT, T], F32R)
    b.ah2 = at("ah2", R(0), [FH, T], F32R)
    b.al2 = at("al2", R(32), [FH, T], F32R)
    b.ps = nc.alloc_psum_tensor("ps", [P, 8, 512], F32)
    b.ident = b.consts[:, 0, :]
    b.ones = b.consts[:, 1, :]
    sm = b.small
    b.mean = sm[:, 0:4]
    b.rs = sm[:, 4:8]
    b.expo = sm[:, 8:24]
    b.omean = sm[:, 24:40]
    b.ors = sm[:, 40:56]
    b.ln_stats = sm[:, 56:80]
    b.ln_mv = sm[:, 80:88]
    b.lam_e = sm[:, 88:90]
    b.nlam = sm[:, 90:91]
    b.lam_d = sm[:, 92:94]
    b.subln = sm[:, 94:95]
    b.ln_rs = b.omean[:, 0:4]
    b.ln_var = b.omean[:, 4:8]
    b.rsa = b.small2[:, 0:4]
    b.sq_a = b.small2[:, 4:8]
    b.mmean = b.small2[:, 8:10]
    b.mrs = b.small2[:, 10:12]
    b.half_gn = b.small2[:, 12:13]
    b.ebl = b.small2[:, 16:32]
    b.gmean = b.small2[:, 32:48]
    b.grs = b.small2[:, 48:64]
    return b


def f32(ap):
    return ap.bitcast(F32)


def col(b, name, k):
    at = VEC[name]
    return b.vec[:, bass.ds(at + k, 1)] if not isinstance(k, int) else b.vec[:, at + k:at + k + 1]


def sync_program(nc, sp, s, b, dram, scratch, out):
    stream = dram["stream"]
    n = stream.shape[0]
    for p in range(RING):
        sp.dma_start(b.stage[:, p, :], stream[p]).then_inc(s.load[p], 16)
    with sp.Fori(1, n // RING) as g:
        for u in range(RING):
            sp.wait_ge(s.lo_ready, RING * g + u - RING + 1)
            sp.dma_start(b.stage[:, u, :], stream[RING * g + u]).then_inc(s.load[u], 16)
    for p in range(n // RING * RING, n):
        sp.wait_ge(s.lo_ready, p - RING + 1)
        sp.dma_start(b.stage[:, p % RING, :], stream[p]).then_inc(s.load[p % RING], 16)
    for k in range(KT):
        sp.wait_ge(s.final_scaled, k + 1)
        sp.dma_start(out[P * k:P * k + P, :], b.x[:, k, :]).then_inc(s.out_done, 16)
    sp.wait_ge(s.out_done, 16 * KT)


def scalar_program(nc, act, s, b, dram, scratch):
    A = nc.scalar.activation

    def AR(*args, **kw):
        act.wait_ge(s.vec_in, 16)
        return A(*args, **kw)

    act.dma_start(b.vec[:], dram["vec"]).then_inc(s.vec_in, 16)
    for c in range(4):
        act.dma_start(b.x[:, 2 * c:2 * c + 2, :], dram["x"][:, 2 * c:2 * c + 2, :]).then_inc(s.x_in[c], 16)
    act.dma_start(b.consts[:], dram["consts"]).then_inc(s.consts_in, 16)
    act.dma_start(b.early[:], dram["early"]).then_inc(s.early_in, 16)
    act.dma_start(b.ws[:], dram["sgu_w"]).then_inc(s.early_in, 16)
    act.dma_start(b.inv[:], dram["inv_count"]).then_inc(s.early_in, 16)
    act.dma_start(b.poolw[:], dram["pool_w"]).then_inc(s.early_in, 16)
    act.dma_start(b.onehot[0:NB, :], dram["onehot"]).then_inc(s.line_in, 16)
    act.dma_start(b.tables[0:NB, :], dram["tables"]).then_inc(s.line_in, 16)

    def hi(p):
        if isinstance(p.index, int) and p.index >= P_END:
            return
        act.wait_ge(s.load[p.slot], 16 * p.round)
        if p.first >= RING:
            act.wait_ge(s.panel_done, p.index - RING + 1)
        A(b.wh[:, p.slot, :], b.stage[:, p.slot, :], ACT.Copy).then_inc(s.hi_ready, 1)

    def x_parts(k, name, evac, sums=None):
        if sums is not None:
            act.wait_ge(s.sums, sums)
        if evac is not None:
            act.wait_ge(s.evac, evac + 1)
        AR(b.hh[:, k, :], b.x[:, k, :], ACT.Copy, scale=col(b, name, k)).then_inc(s.x_hi, 1)

    def x_square(k, half):
        AR(b.tmp[:, half, :], b.x[:, k, :], ACT.Square).then_inc(s.x_squared, 1)

    def row(n):
        act.wait_ge(s.row_done, n)
        A(b.rrow[:], b.ps[:, 7, :], ACT.Copy).then_inc(s.row_ready, 1)

    hi(Panel(0))
    act.wait_ge(s.vec_in, 16)
    for k in range(KT):
        if k % 2 == 0:
            act.wait_ge(s.x_in[k // 2], 16)
        x_parts(k, "attn_norm_g", None, k if k >= 2 else None)
        x_square(k, k % 2)
        if k in (1, 3, 5):
            hi(Panel((k + 1) // 2))

    hi(Panel(P_U + RING))
    row(1)
    act.wait_ge(s.evac, E_U + 1)
    A(b.u[:, 0, :], b.u[:, 0, :], ACT.Gelu).then_inc(s.u_ready, 1)
    hi(Panel(P_U + 1 + RING))
    act.wait_ge(s.evac, E_U + 2)
    A(b.u[:, 1, :], b.u[:, 1, :], ACT.Gelu).then_inc(s.u_ready, 1)
    hi(Panel(P_VA + RING))
    hi(Panel(P_VA + 1 + RING))
    act.wait_ge(s.evac, E_VA + 2)
    A(b.va[:], b.va[:], ACT.Gelu).then_inc(s.va_gelu, 1)
    hi(Panel(P_POOL + RING))
    for h in range(12):
        act.wait_ge(s.line_done, h + 1)
        A(b.lines[:, h, 0:T], b.ps[:, 4 + h % 2, :], ACT.Copy).then_inc(s.line_copied, 1)
    act.wait_ge(s.lines_set, 1)
    act.wait_ge(s.line_copied, 12)
    act.dma_start(scratch.rearrange("h (p j) -> p h j", p=P), b.lines[:]).then_inc(s.lines_out, 16)
    hi(Panel(P_POOL + 1 + RING))
    act.wait_ge(s.lam_dots, 1)
    A(b.lam_e, b.lam_d, ACT.Exp).then_inc(s.lam_exps, 1)

    with act.Fori(0, 2) as i:
        for u in range(RING):
            hi(Panel(P_Q + u + RING, RING, i))
    for u in range(4):
        hi(Panel(P_V + u + RING))

    act.wait_ge(s.lines_out, 16)

    def gate(g, half, dst, evac):
        act.wait_ge(s.evac, evac + 1)
        bias = b.half_bg[:, g:g + 1] if isinstance(g, int) else b.half_bg[:, bass.ds(g, 1)]
        AR(dst, b.tmp[:, half, :], ACT.Tanh, bias=bias, scale=0.5).then_inc(s.gated, 1)

    with act.Fori(0, 4) as i:
        act.dma_start(b.bias[:], bias_tile(scratch, i)).then_inc(s.bias_in, 16)
        act.wait_ge(s.evac, E_K + 4)
        AR(b.qh[:], b.qk[:, i, :], ACT.Copy, scale=0.125).then_inc(s.qk_hi, 1)
        AR(b.kh[:], b.qk[:, 4 + i, :], ACT.Copy).then_inc(s.qk_hi, 1)
        act.wait_ge(s.evac, E_V + 4)
        AR(b.vh[:], b.v[:, :, bass.ds(P * i, P)], ACT.Copy).then_inc(s.v_hi, 1)
        for u in range(4):
            hi(Panel(P_GATE + u + RING, RING, i))
            gate(4 * i + u, u % 2, b.ga[:, 4 * i + u, :], E_GATE + 4 * i + u)
            if u < 2:
                act.wait_ge(s.negated, 2 * i + u + 1)
                for qb in range(TT):
                    n = 4 * u + qb
                    sc = b.s[:, u, pairs_offset(qb):pairs_offset(qb + 1)]
                    A(sc, sc, ACT.Exp, bias=b.neg[:, n:n + 1], accum_out=b.sums[:, n:n + 1]).then_inc(s.exped, 1)
            if u == 2:
                for kb in range(TT):
                    act.wait_ge(s.turned, 4 * i + kb + 1)
                    w = (TT - kb) * P
                    A(b.th[:, turned_offset(kb):turned_offset(kb) + w], b.ps[:, 5 + kb % 2, 0:w],
                      ACT.Copy).then_inc(s.turned_hi, 1)
        act.wait_ge(s.scored, 8 * i + 8)
        act.wait_ge(s.score_done, 8 * i + 8)
        act.wait_ge(s.pv_done, i + 1)

    def square_head(h):
        act.wait_ge(s.o_evac, h + 1)
        if h >= 2:
            act.wait_ge(s.ocol_done, h - 1)
        A(b.osq[:, h % 2, :], b.o[:, h, :], ACT.Square).then_inc(s.o_squared, 1)

    act.wait_ge(s.pv_done, 4)
    for h in range(4):
        square_head(h)
    for u in range(8):
        hi(Panel(P_GATE + 16 + u + RING))
        gate(16 + u, u % 2, b.gatec[:, u, :], E_GATE + 16 + u)
        if u == 1:
            for k in range(4):
                act.wait_ge(s.yab_written, k + 1)
                A(b.yabh[:, k, :], b.yab[:, k, :], ACT.Copy).then_inc(s.yab_hi, 1)
        if 2 <= u < 6:
            h = u - 2
            act.wait_ge(s.o_normed, h + 1)
            A(b.ych[:, h, :], b.o[:, h, :], ACT.Copy, scale=b.subln).then_inc(s.yc_hi, 1)

    with act.Fori(0, 2) as i:
        for u in range(4):
            hi(Panel(P_PROJ + u + RING, RING, i))
            act.wait_ge(s.m_summed, 4 * i + u + 1)
            AR(b.mh[:, 4 * i + u, :], b.tmp[:, 0, :], ACT.Copy, scale=0.5).then_inc(s.m_hi, 1)

    def residual_loop(p0, e0, name, norm):
        act.wait_ge(s.sums, 9 * norm + 1)
        with act.Fori(0, 2) as i:
            for u in range(4):
                hi(Panel(p0 + u + RING, RING, i))
                x_parts(4 * i + u, name, e0 + 4 * i + u, 9 * norm + 4 * i + u)
                x_square(4 * i + u, u % 2)

    residual_loop(P_WOUT, E_WOUT, "ffn_norm_g", 1)

    def up_body(i, first):
        for a in range(2):
            j = 2 * i + a
            hi(Panel(P_UP + 2 * a + RING, RING, i))
            if first and a == 0:
                row(2)
            act.wait_ge(s.evac, E_UP + 4 * i + 2 * a + 1)
            AR(b.cb[:, a, :], b.gb[:, a, 2:], ACT.Identity, bias=col(b, "conv_b", j),
              scale=col(b, "conv2", j)).then_inc(s.tapped, 1)
            act.wait_ge(s.conved, j + 1)
            A(b.cb[:, a, :], b.cb[:, a, :], ACT.Gelu).then_inc(s.gelued, 1)
            hi(Panel(P_UP + 2 * a + 1 + RING, RING, i))
            act.wait_ge(s.acted, j + 1)
            AR(b.ah[:, j, :], b.tmp[:, a, :], ACT.Copy).then_inc(s.act_hi, 1)

    up_body(0, True)
    with act.Fori(1, FT1 // 2) as i:
        up_body(i, False)

    act.wait_ge(s.sums, 19)
    with act.Fori(0, 2) as i:
        for c in range(4):
            k = 4 * i + c
            for m in range(3):
                p = Panel(P_DOWN + 3 * c + m + RING, 12, i)
                hi(p)
            act.wait_ge(s.sums, 18 + k)
            act.wait_ge(s.sums2, 1 + k)
            act.wait_ge(s.evac, E_DOWN + k + 1)
            AR(b.hh[:, k, :], b.x[:, k, :], ACT.Copy, scale=b.gg[:, bass.ds(k, 1)]).then_inc(s.x_hi, 1)
            x_square(k, c % 2)
            AR(b.sq2[:, c % 2, :], b.x[:, k, :], ACT.Square,
              scale=col(b, "final_norm_g", k)).then_inc(s.x_second, 1)

    block2_scalar(nc, act, s, b, dram, scratch, A, AR, hi, row, x_parts, x_square, residual_loop)


def bias_tile(scratch, h):
    row = scratch[h, P - 1:P - 1 + (LINE - 1) * P]
    return row.rearrange("(p j) -> p j", p=P)[:, 0:T]


def bias_tiles(scratch, h):
    rows = scratch[bass.ds(h, 2), P - 1:P - 1 + (LINE - 1) * P]
    return rows.rearrange("h (p j) -> p h j", p=P)[:, :, 0:T]


def vector_program(nc, dve, s, b):
    V = nc.vector
    st = Steps(dve, s.steps)

    def bank(e):
        return b.ps[:, e % 4, :]

    def lo(p):
        if isinstance(p.index, int) and p.index >= P_END:
            return
        dve.wait_ge(s.hi_ready, p.index + 1)
        V.tensor_tensor(b.wl[:, p.slot, :], b.stage[:, p.slot, :], f32(b.wh[:, p.slot, :]),
                        ALU.subtract).then_inc(s.lo_ready, 1)

    def evac_row(p, e, dst, slot):
        dve.wait_ge(s.panel_done, p.index + 1)
        V.tensor_tensor(dst, b.ps[:, slot, :], b.rrow[:], ALU.mult).then_inc(s.evac, 1)

    def x_rest(k, name, count, seq):
        dve.wait_ge(s.x_hi, count)
        scale = b.gg[:, bass.ds(k, 1)] if name == "gg" else col(b, name, k)
        V.scalar_tensor_tensor(b.hl[:, k, :], b.x[:, k, :], scale, f32(b.hh[:, k, :]),
                               ALU.mult, ALU.subtract).then_inc(s.h_ready, 1)

    def x_sum(half, count, sums):
        dve.wait_ge(s.x_squared, count)
        dve.wait_ge(s.sums, sums)
        V.tensor_tensor(b.sumsq[:], b.sumsq[:], b.tmp[:, half, :], ALU.add).then_inc(s.sums, 1)

    def mean(n, width=D, eps=1e-6):
        dve.wait_ge(s.col_done, n)
        V.tensor_scalar(b.mean, b.ps[:, 7, 0:4], 1.0 / width, eps, ALU.mult, ALU.add).then_inc(s.mean_ready, 1)

    def diagonal(dst, r):
        return V.tensor_tensor(dst.rearrange("p (a q) -> p a q", a=TT),
                               b.ident.unsqueeze(1).to_broadcast([P, TT, P]),
                               r.unsqueeze(2).to_broadcast([P, TT, P]), ALU.mult)

    st.mark(V.memset(b.expo, -0.5))
    V.memset(b.sumsq[:], 0.0).then_inc(s.sums, 1)
    for buf in (b.xb[:, 0, 0:16], b.xb[:, 1, 0:16], b.s1[:, 0:16], b.s2[:, 0:16]):
        st.mark(V.memset(buf, 0.0))
    lo(Panel(0))
    dve.wait_ge(s.vec_in, 16)
    for k in range(KT):
        if k % 2 == 0:
            dve.wait_ge(s.x_in[k // 2], 16)
        x_rest(k, "attn_norm_g", k + 1, 0)
        x_sum(k % 2, k + 1, k + 1)
        if k in (1, 3, 5):
            lo(Panel((k + 1) // 2))
    st.mark(V.tensor_scalar(b.half_bg[:], b.vec[:, VEC["b_gate"]:VEC["b_gate"] + 24], 0.5, None, ALU.mult))
    st.mark(V.tensor_scalar(b.subln, col(b, "subln", 0), 1.0 - LAM_INIT, None, ALU.mult))
    st.mark(V.tensor_tensor(b.gg[:], b.vec[:, VEC["final_norm_g"]:VEC["final_norm_g"] + 8],
                            b.vec[:, VEC["norm_mix"]:VEC["norm_mix"] + 8], ALU.mult))
    dve.wait_ge(s.early_in, 64)
    lam = b.early[:, 768:1024].rearrange("p (a c d) -> p a c d", a=2, c=2)
    prod = b.tmp[:, 0, 0:128].rearrange("p (a d) -> p a d", a=2)
    st.link(V.tensor_tensor(prod, lam[:, :, 0, :], lam[:, :, 1, :], ALU.mult))
    V.tensor_reduce(b.lam_d, prod, AX_X, ALU.add).then_inc(s.lam_dots, 1)
    dve.wait_ge(s.consts_in, 16)

    mean(1)
    dve.wait_ge(s.pow_done, 1)
    diagonal(b.diag[:, 0, :], b.rs).then_inc(s.diag_ready, 1)
    dve.wait_ge(s.row_ready, 1)
    evac_row(Panel(P_U), E_U, b.u[:, 0, :], 0)
    lo(Panel(P_U + RING))
    evac_row(Panel(P_U + 1), E_U + 1, b.u[:, 1, :], 1)
    lo(Panel(P_U + 1 + RING))
    lo(Panel(P_VA + RING))
    dve.wait_ge(s.panel_done, P_VA + 2)
    for t in range(TT):
        ins = V.tensor_scalar(b.va[:, t, :], b.ps[:, 2 + t // 2, 256 * (t % 2):256 * (t % 2) + 256],
                              b.rs[:, t:t + 1], None, ALU.mult)
        if t % 2:
            ins.then_inc(s.evac, 1)
    lo(Panel(P_VA + 1 + RING))
    evac_row(Panel(P_POOL), E_POOL, b.xb[:, 0, 16:], 0)
    lo(Panel(P_POOL + RING))
    dve.wait_ge(s.va_gelu, 1)
    for t in range(TT):
        st.link(V.bn_stats(b.ln_stats[:, 6 * t:6 * t + 6], b.va[:, t, :]))
        st.link(V.bn_aggr(b.ln_mv[:, 2 * t:2 * t + 2], b.ln_stats[:, 6 * t:6 * t + 6]))
    var = b.ln_mv.rearrange("p (t c) -> p t c", c=2)
    V.tensor_scalar(b.ln_var, var[:, :, 1], 1e-5, None, ALU.add).then_inc(s.ln_mean, 1)
    evac_row(Panel(P_POOL + 1), E_POOL + 1, b.xb[:, 1, 16:], 1)
    lo(Panel(P_POOL + 1 + RING))
    dve.wait_ge(s.ln_pow, 1)
    for t in range(TT):
        st.mark(V.tensor_scalar(b.va[:, t, :], b.va[:, t, :], b.ln_mv[:, 2 * t:2 * t + 1], b.ln_rs[:, t:t + 1],
                                ALU.subtract, ALU.mult))
    st.wait()
    st.link(V.tensor_tensor(b.va[:], b.va[:], b.early[:, 256:512].unsqueeze(1).to_broadcast([P, TT, 256]),
                            ALU.mult))
    V.tensor_tensor(b.va[:], b.va[:], b.early[:, 512:768].unsqueeze(1).to_broadcast([P, TT, 256]),
                    ALU.add).then_inc(s.v_normed, 1)

    def wsum(dst, src, shift, parts):
        st.link(V.tensor_tensor(dst[parts, 16:], src[parts, 16:], src[parts, 16 - shift:16 + T - shift], ALU.add))

    every, high, low = slice(0, P), slice(64, P), slice(0, 64)
    x0, x1 = b.xb[:, 0, :], b.xb[:, 1, :]
    dve.wait_ge(s.evac, E_POOL + 2)
    wsum(b.s1, x0, 1, every)
    wsum(b.s2, b.s1, 2, high)
    for parts, src in ((low, b.s1), (high, b.s2)):
        st.mark(V.tensor_tensor(b.pool[parts, 0, :], src[parts, 16:], b.inv[parts, 0, :], ALU.mult))
    st.wait()
    V.tensor_tensor(b.pool[:, 0, :], b.pool[:, 0, :], x0[:, 16:], ALU.subtract).then_inc(s.pooled, 1)
    wsum(b.s1, x1, 1, every)
    wsum(b.s2, b.s1, 2, every)
    wsum(b.s1, b.s2, 4, every)
    wsum(b.s2, b.s1, 8, high)
    for parts, src in ((low, b.s1), (high, b.s2)):
        st.mark(V.tensor_tensor(b.pool[parts, 1, :], src[parts, 16:], b.inv[parts, 1, :], ALU.mult))
    st.wait()
    V.tensor_tensor(b.pool[:, 1, :], b.pool[:, 1, :], x1[:, 16:], ALU.subtract).then_inc(s.pooled, 1)

    dve.wait_ge(s.lam_exps, 1)
    st.link(V.tensor_tensor(b.nlam, b.lam_e[:, 1:2], b.lam_e[:, 0:1], ALU.subtract))
    st.link(V.tensor_scalar(b.nlam, b.nlam, -LAM_INIT, None, ALU.add))

    with dve.Fori(0, 2) as i:
        for u in range(RING):
            e = E_Q + u
            evac_row(Panel(P_Q + u, RING, i), e, b.qk[:, 4 * i + u, :], e % 4)
            lo(Panel(P_Q + u + RING, RING, i))

    for f in range(2):
        dve.wait_ge(s.spatial_done, f + 1)
        dve.wait_ge(s.u_ready, 2)
        y = b.yab[:, f, :]
        st.link(V.tensor_tensor(y.rearrange("p (c t) -> p c t", c=TT),
                                b.ps[:, 4 + f, :].rearrange("p (c t) -> p c t", c=TT),
                                b.early[:, P * f:P * f + P].unsqueeze(1).to_broadcast([P, TT, P]), ALU.add))
        V.tensor_tensor(y, y, b.u[:, f, :], ALU.mult).then_inc(s.yab_written, 1)
    for f in range(2):
        dve.wait_ge(s.poolmm_done, f + 1)
        V.tensor_scalar(b.yab[:, 2 + f, :], b.ps[:, 6 + f, :], col(b, "pool_scale", f), None,
                        ALU.mult).then_inc(s.yab_written, 1)

    for u in range(3):
        dve.wait_ge(s.panel_done, P_V + u + 1)
        lo(Panel(P_V + u + RING))
    for t in range(TT):
        if t < TT - 1:
            dve.wait_ge(s.v_done, t + 1)
        else:
            dve.wait_ge(s.panel_done, P_V + 4)
        V.tensor_scalar(b.v[:, t, :], bank(E_V + t), b.rs[:, t:t + 1], None, ALU.mult).then_inc(s.evac, 1)
    lo(Panel(P_V + 3 + RING))

    def gate(p, g, half, slot):
        if isinstance(g, int):
            if g >= 2:
                dve.wait_ge(s.gated, g - 1)
        evac_row(p, 0, b.tmp[:, half, :], slot)

    def score_rows(i, c, before, bias):
        for qb in range(TT):
            n = 4 * c + qb
            w = P * (qb + 1)
            dve.wait_ge(s.score_done, 8 * i + 8 * before + n + 1)
            V.memset(b.turn[:, n:n + 1], 0.0)
            V.tensor_tensor_reduce(b.s[:, c, pairs_offset(qb):pairs_offset(qb + 1)],
                                   b.ps[:, 4 + n % 2, 0:w], bias[:, (TT - 1 - qb) * P:T], 1.0, -3.0e38,
                                   ALU.add, ALU.max, b.mx[:, n:n + 1]).then_inc(s.scored, 1)
        dve.wait_ge(s.scored, 8 * i + 8 * before + 4 * c + 4)
        V.tensor_scalar(b.neg[:, 4 * c:4 * c + 4], b.mx[:, 4 * c:4 * c + 4], -1.0, None,
                        ALU.mult).then_inc(s.negated, 1)

    HEAD_STEPS = 1 + 4 + 2
    with dve.Fori(0, 4) as i:
        st.enter(i, HEAD_STEPS)
        dve.wait_ge(s.qk_hi, 2 * i + 2)
        V.scalar_tensor_tensor(b.ql[:], b.qk[:, i, :], 0.125, f32(b.qh[:]), ALU.mult, ALU.subtract)
        V.tensor_tensor(b.kl[:], b.qk[:, 4 + i, :], f32(b.kh[:]), ALU.subtract).then_inc(s.qk_ready, 1)
        dve.wait_ge(s.v_hi, i + 1)
        V.tensor_tensor(b.vl[:], b.v[:, :, bass.ds(P * i, P)], f32(b.vh[:]), ALU.subtract).then_inc(s.v_ready, 1)
        for u in range(4):
            if u >= 2:
                dve.wait_ge(s.gated, 4 * i + u - 1)
            evac_row(Panel(P_GATE + u, RING, i), 0, b.tmp[:, u % 2, :], (E_GATE + u) % 4)
            lo(Panel(P_GATE + u + RING, RING, i))
            if u == 0:
                dve.wait_ge(s.bias_in, 16 * i + 16)
            if u < 2:
                score_rows(i, u, 0, b.bias)
            if u == 1:
                dve.wait_ge(s.exped, 8 * i + 4)
                st.link(V.reciprocal(b.rec[:, 0:4], b.sums[:, 0:4]))
                for qb in range(TT):
                    sc = b.s[:, 0, pairs_offset(qb):pairs_offset(qb + 1)]
                    st.mark(V.tensor_scalar(sc, sc, b.rec[:, qb:qb + 1], None, ALU.mult))
                dve.wait_ge(s.exped, 8 * i + 8)
                st.link(V.reciprocal(b.rec[:, 4:8], b.sums[:, 4:8]))
                st.link(V.tensor_scalar(b.rec[:, 4:8], b.rec[:, 4:8], b.nlam, None, ALU.mult))
                for qb in range(TT):
                    c0 = b.s[:, 0, pairs_offset(qb):pairs_offset(qb + 1)]
                    c1 = b.s[:, 1, pairs_offset(qb):pairs_offset(qb + 1)]
                    V.scalar_tensor_tensor(c0, c1, b.rec[:, 4 + qb:5 + qb], c0, ALU.mult,
                                           ALU.add).then_inc(s.blended, 1)
            if u == 2:
                for kb in range(TT):
                    w = (TT - kb) * P
                    at = turned_offset(kb)
                    dve.wait_ge(s.turned_hi, 4 * i + kb + 1)
                    V.tensor_tensor(b.tl[:, at:at + w], b.ps[:, 5 + kb % 2, 0:w], f32(b.th[:, at:at + w]),
                                    ALU.subtract).then_inc(s.turned_ready, 1)
        dve.wait_ge(s.pv_done, i + 1)
        V.tensor_copy(b.o[:, i, :], b.ps[:, 4, :]).then_inc(s.o_evac, 1)
        dve.wait_ge(s.gated, 4 * i + 4)
    st.leave(4)

    for u in range(8):
        gate(Panel(P_GATE + 16 + u), 16 + u, u % 2, (E_GATE + 16 + u) % 4)
        lo(Panel(P_GATE + 16 + u + RING))
        if u == 1:
            dve.wait_ge(s.ocol_done, 4)
            V.tensor_scalar(b.omean, b.ps[:, 7, 0:16], 1.0 / P, 1e-5, ALU.mult, ALU.add).then_inc(s.omean_ready, 1)
            for k in range(4):
                dve.wait_ge(s.yab_hi, k + 1)
                V.tensor_tensor(b.yabl[:, k, :], b.yab[:, k, :], f32(b.yabh[:, k, :]),
                                ALU.subtract).then_inc(s.yab_ready, 1)
        if 2 <= u < 6:
            h = u - 2
            if h == 0:
                dve.wait_ge(s.opow_done, 1)
            diagonal(b.diag[:, h % 2, :], b.ors[:, 4 * h:4 * h + 4]).then_inc(s.odiag_ready, 1)
            dve.wait_ge(s.orow_done, h + 1)
            V.tensor_tensor(b.o[:, h, :], b.o[:, h, :], b.ps[:, 4 + h, :], ALU.mult).then_inc(s.o_normed, 1)
            dve.wait_ge(s.yc_hi, h + 1)
            V.scalar_tensor_tensor(b.ycl[:, h, :], b.o[:, h, :], b.subln, f32(b.ych[:, h, :]),
                                   ALU.mult, ALU.subtract).then_inc(s.yc_ready, 1)

    with dve.Fori(0, 2) as i:
        st.enter(i, 4)
        for u in range(4):
            j = 4 * i + u
            p = Panel(P_PROJ + u, RING, i)
            dve.wait_ge(s.gated, 24)
            dve.wait_ge(s.panel_done, p.index + 1)

            def branch(r, gates, dst):
                ins = V.scalar_tensor_tensor(dst, gates, 1.0, b.ps[:, (E_PROJ + 3 * u + r) % 4, :],
                                             ALU.add, ALU.mult)
                ins.then_inc(s.evac, 1)
            branch(0, b.ga[:, j, :], b.tmp[:, 0, :])
            branch(1, b.ga[:, 8 + j, :], b.tmp[:, 1, :])
            dve.wait_ge(s.evac, E_PROJ + 12 * i + 3 * u + 2)
            st.link(V.tensor_tensor(b.tmp[:, 0, :], b.tmp[:, 0, :], b.tmp[:, 1, :], ALU.add))
            branch(2, b.gatec[:, j, :], b.tmp[:, 1, :])
            dve.wait_ge(s.evac, E_PROJ + 12 * i + 3 * u + 3)
            V.tensor_tensor(b.tmp[:, 0, :], b.tmp[:, 0, :], b.tmp[:, 1, :], ALU.add).then_inc(s.m_summed, 1)
            lo(Panel(P_PROJ + u + RING, RING, i))
            dve.wait_ge(s.m_hi, j + 1)
            dve.wait_ge(s.m_summed, j + 1)
            V.scalar_tensor_tensor(b.ml[:, j, :], b.tmp[:, 0, :], 0.5, f32(b.mh[:, j, :]), ALU.mult,
                                   ALU.subtract).then_inc(s.m_ready, 1)
            dve.wait_ge(s.m_ready, j + 1)
    st.leave(2)

    def residual_loop(p0, e0, name, norm):
        V.memset(b.sumsq[:], 0.0).then_inc(s.sums, 1)
        with dve.Fori(0, 2) as i:
            for u in range(4):
                k = 4 * i + u
                p = Panel(p0 + u, RING, i)
                dve.wait_ge(s.panel_done, p.index + 1)
                V.tensor_tensor(b.x[:, k, :], b.x[:, k, :], b.ps[:, (e0 + u) % 4, :], ALU.add).then_inc(s.evac, 1)
                lo(p.plus(RING))
                dve.wait_ge(s.evac, e0 + k + 1)
                x_rest(k, name, 8 * norm + k + 1, 0)
                x_sum(u % 2, 8 * norm + k + 1, 9 * norm + 1 + k)

    residual_loop(P_WOUT, E_WOUT, "ffn_norm_g", 1)

    for a in range(2):
        st.link(V.memset(b.gb[:, a, 0:2], 0.0))
    mean(2)
    dve.wait_ge(s.pow_done, 2)
    diagonal(b.diag[:, 0, :], b.rs).then_inc(s.diag_ready, 1)
    dve.wait_ge(s.row_ready, 2)
    with dve.Fori(0, FT1 // 2) as i:
        st.enter(i, 2)
        for a in range(2):
            j = 2 * i + a
            gate_p, up_p = Panel(P_UP + 2 * a, RING, i), Panel(P_UP + 2 * a + 1, RING, i)
            evac_row(gate_p, 0, b.gb[:, a, 2:], (E_UP + 2 * a) % 4)
            if a == 1:
                act_rest(nc, dve, s, b, 2 * i, 0)
            lo(gate_p.plus(RING))
            dve.wait_ge(s.tapped, j + 1)
            dve.wait_ge(s.evac, E_UP + 4 * i + 2 * a + 1)
            st.link(V.scalar_tensor_tensor(b.cb[:, a, :], b.gb[:, a, 1:T + 1], col(b, "conv1", j), b.cb[:, a, :],
                                           ALU.mult, ALU.add))
            V.scalar_tensor_tensor(b.cb[:, a, :], b.gb[:, a, 0:T], col(b, "conv0", j), b.cb[:, a, :],
                                   ALU.mult, ALU.add).then_inc(s.conved, 1)
            evac_row(up_p, 0, b.tmp[:, a, :], (E_UP + 2 * a + 1) % 4)
            lo(up_p.plus(RING))
            dve.wait_ge(s.gelued, j + 1)
            dve.wait_ge(s.evac, E_UP + 4 * i + 2 * a + 2)
            V.tensor_tensor(b.tmp[:, a, :], b.tmp[:, a, :], b.cb[:, a, :], ALU.mult).then_inc(s.acted, 1)
            if a == 1:
                act_rest(nc, dve, s, b, 2 * i + 1, 1)
    st.leave(FT1 // 2)

    V.memset(b.sumsq[:], 0.0).then_inc(s.sums, 1)
    V.memset(b.sum2[:], 0.0).then_inc(s.sums2, 1)
    with dve.Fori(0, 2) as i:
        for c in range(4):
            k = 4 * i + c
            for m in range(3):
                p = Panel(P_DOWN + 3 * c + m, 12, i)
                dve.wait_ge(s.panel_done, p.index + 1)
                if m == 2:
                    V.tensor_tensor(b.x[:, k, :], b.x[:, k, :], b.ps[:, (E_DOWN + c) % 4, :],
                                    ALU.add).then_inc(s.evac, 1)
                lo(p.plus(RING))
            dve.wait_ge(s.evac, E_DOWN + k + 1)
            x_rest(k, "gg", 16 + k + 1, 0)
            x_sum(c % 2, 16 + k + 1, 18 + 1 + k)
            dve.wait_ge(s.x_second, k + 1)
            dve.wait_ge(s.sums2, k + 1)
            V.tensor_tensor(b.sum2[:], b.sum2[:], b.sq2[:, c % 2, :], ALU.add).then_inc(s.sums2, 1)

    block2_vector(nc, dve, s, b, st, lo, evac_row, mean, diagonal, x_rest, x_sum, residual_loop,
                  score_rows)


def act_rest(nc, dve, s, b, j, half):
    dve.wait_ge(s.act_hi, j + 1)
    dve.wait_ge(s.acted, j + 1)
    nc.vector.tensor_tensor(b.al[:, j, :], b.tmp[:, half, :], f32(b.ah[:, j, :]),
                            ALU.subtract).then_inc(s.act_ready, 1)


def gpsimd_program(nc, pool, s, b):
    G = nc.gpsimd
    G.memset(b.lines[:, :, T:LINE], NEG).then_inc(s.lines_set, 1)
    pool.wait_ge(s.early_in, 64)
    G.affine_select(out=b.ws[:], in_=b.ws[:], compare_op=ALU.is_ge, fill=0.0, base=0,
                    pattern=[[0, 4], [1, P]], channel_multiplier=-1).then_inc(s.ws_masked, 1)

    def power(n):
        pool.wait_ge(s.mean_ready, n)
        G.tensor_tensor(b.rs, b.mean, b.expo[:, 0:4], ALU.pow).then_inc(s.pow_done, 1)

    power(1)
    pool.wait_ge(s.ln_mean, 1)
    G.tensor_tensor(b.ln_rs, b.ln_var, b.expo[:, 0:4], ALU.pow).then_inc(s.ln_pow, 1)
    pool.wait_ge(s.omean_ready, 1)
    G.tensor_tensor(b.ors, b.omean, b.expo, ALU.pow).then_inc(s.opow_done, 1)
    power(2)
    pool.wait_ge(s.mean_ready, 3)
    G.tensor_tensor(b.rsa, b.mean, b.expo[:, 0:4], ALU.pow).then_inc(s.pow_a, 1)
    pool.wait_ge(s.mean_b, 1)
    G.tensor_tensor(b.rs, b.mean, b.expo[:, 0:4], ALU.pow).then_inc(s.pow_done, 1)
    pool.wait_ge(s.mmean_ready, 1)
    G.tensor_tensor(b.mrs, b.mmean, b.expo[:, 0:MT], ALU.pow).then_inc(s.mpow_done, 1)
    pool.wait_ge(s.gmean_ready, 1)
    G.tensor_tensor(b.grs, b.gmean, b.expo, ALU.pow).then_inc(s.gpow_done, 1)
    for n in (4, 5, 6):
        power(n)


def tensor_program(nc, pe, s, b):
    MM = nc.tensor.matmul

    def three(out, wh, wl, xh, xl, start, stop):
        MM(out, wh, xh, start=start, stop=False, skip_group_check=True)
        MM(out, wh, xl, start=False, stop=False, skip_group_check=True)
        return MM(out, wl, xh, start=False, stop=stop, skip_group_check=True)

    def begin(p, e):
        pe.wait_ge(s.lo_ready, p.index + 1)
        if e is not None:
            pe.wait_ge(s.evac, e - 3)

    def w(p, a, n=P):
        return b.wh[:, p.slot, a:a + n], b.wl[:, p.slot, a:a + n]

    def features(p, e, slot, xh=None, xl=None, tiles=range(KT), last=KT, width=T, ready=None, middle=None,
                 late=None):
        xh, xl = (b.hh, b.hl) if xh is None else (xh, xl)
        begin(p, e)
        for n, k in enumerate(tiles):
            if middle and n == 4:
                middle()
            if late and n == 6:
                late()
            if ready:
                ready(k)
            wh, wl = w(p, P * n)
            ins = three(b.ps[:, slot, 0:width], wh, wl, xh[:, k, 0:width], xl[:, k, 0:width], k == 0, k == last - 1)
        ins.then_inc(s.panel_done, 1)

    def column_sums(n, sums):
        pe.wait_ge(s.sums, sums)
        if n > 1:
            pe.wait_ge(s.row_ready, n - 1)
        for t in range(TT):
            ins = MM(b.ps[:, 7, t:t + 1], b.sumsq[:, P * t:P * t + P], b.ones[:, 0:1], start=True, stop=True)
        ins.then_inc(s.col_done, 1)

    def row(n):
        pe.wait_ge(s.diag_ready, n)
        MM(b.ps[:, 7, :], b.ones, b.diag[:, 0, :], start=True, stop=True).then_inc(s.row_done, 1)

    def x_ready(base):
        return lambda k: pe.wait_ge(s.h_ready, base + k + 1)

    features(Panel(P_U), None, 0, ready=x_ready(0))
    pe.wait_ge(s.consts_in, 16)
    column_sums(1, 9)
    features(Panel(P_U + 1), None, 1, middle=lambda: row(1))
    for m in range(2):
        p = Panel(P_VA + m)
        begin(p, None)
        for k in range(4 * m, 4 * m + 4):
            wh, wl = w(p, 256 * (k - 4 * m), 256)
            for t in range(TT):
                tok = slice(P * t, P * t + P)
                ins = three(b.ps[:, 2 + t // 2, 256 * (t % 2):256 * (t % 2) + 256],
                            b.hh[:, k, tok], b.hl[:, k, tok], wh, wl, k == 0 and t % 2 == 0, k == KT - 1)
        ins.then_inc(s.panel_done, 1)
    for u in range(2):
        features(Panel(P_POOL + u), E_POOL + u, u)
    pe.wait_ge(s.line_in, 32)
    for h in range(12):
        if h >= 2:
            pe.wait_ge(s.line_copied, h - 1)
        MM(b.ps[:, 4 + h % 2, :], b.tables[0:NB, P * h:P * h + P], b.onehot[0:NB, :], start=True,
           stop=True).then_inc(s.line_done, 1)

    with pe.Fori(0, 2) as i:
        for u in range(RING):
            features(Panel(P_Q + u, RING, i), E_Q + u + RING * i, (E_Q + u) % 4)

    pe.wait_ge(s.v_normed, 1)
    pe.wait_ge(s.ws_masked, 1)
    pe.wait_ge(s.line_copied, 12)
    for f in range(2):
        for c in range(TT):
            for g in range(2):
                ins = MM(b.ps[64 * g:64 * g + 64, 4 + f, P * c:P * c + P],
                         b.va[:, c, 64 * (2 * f + g):64 * (2 * f + g) + 64], b.ws[:, 2 * f + g, :],
                         start=True, stop=True)
        ins.then_inc(s.spatial_done, 1)
    pe.wait_ge(s.pooled, 2)
    for g in range(2):
        part = slice(64 * g, 64 * g + 64)
        for f in range(2):
            ins = MM(b.ps[part, 6 + f, :], b.poolw[part, f, :], b.pool[part, f, :], start=True, stop=True)
            if g:
                ins.then_inc(s.poolmm_done, 1)

    def tokens(first, e0, done, wait_banks=True):
        for m in range(4):
            p = Panel(first + m)
            begin(p, None)
            for t in range(TT):
                if m == 0:
                    pe.wait_ge(s.evac, e0 + t - 3)
                for n in range(2):
                    k = 2 * m + n
                    wh, wl = w(p, 512 * n, 512)
                    tok = slice(P * t, P * t + P)
                    ins = three(b.ps[:, (e0 + t) % 4, :], b.hh[:, k, tok], b.hl[:, k, tok], wh, wl,
                                k == 0, k == KT - 1)
                if m == 3 and t < TT - 1:
                    ins.then_inc(done, 1)
            ins.then_inc(s.panel_done, 1)

    tokens(P_V, E_V, s.v_done)

    def scores(i, c):
        part = slice(64 * c, 64 * c + 64)
        for qb in range(TT):
            n = 4 * c + qb
            if n >= 2:
                pe.wait_ge(s.scored, 8 * i + n - 1)
            width = P * (qb + 1)
            tok = slice(P * qb, P * qb + P)
            three(b.ps[:, 4 + n % 2, 0:width], b.qh[part, tok], b.ql[part, tok], b.kh[part, 0:width],
                  b.kl[part, 0:width], True, True).then_inc(s.score_done, 1)

    def turn(n, c=0):
        pe.wait_ge(s.blended, 4 * n + 4)
        for kb in range(TT):
            if kb >= 2:
                pe.wait_ge(s.turned_ready, 4 * n + kb - 1)
            for qb in range(kb, TT):
                at = pairs_offset(qb) + P * kb
                ins = nc.tensor.transpose(b.ps[:, 5 + kb % 2, P * (qb - kb):P * (qb - kb) + P],
                                          b.s[:, c, at:at + P], b.ident)
            ins.then_inc(s.turned, 1)

    def values(n, pair, bank):
        pe.wait_ge(s.v_ready, pair + 1)
        for kb in range(TT):
            pe.wait_ge(s.turned_ready, 4 * n + kb + 1)
            at, width = turned_offset(kb), (TT - kb) * P
            ins = three(b.ps[:, bank, kb * P:T], b.vh[:, kb, :], b.vl[:, kb, :], b.th[:, at:at + width],
                        b.tl[:, at:at + width], kb == 0, kb == TT - 1)
        ins.then_inc(s.pv_done, 1)

    with pe.Fori(0, 4) as i:
        for u in range(4):
            p = Panel(P_GATE + u, RING, i)
            middle = (lambda: turn(i)) if u == 3 else None
            features(p, E_GATE + u + RING * i, (E_GATE + u) % 4, middle=middle)
            if u == 0:
                pe.wait_ge(s.qk_ready, i + 1)
                pe.wait_ge(s.yab_written, 4)
            if u < 2:
                scores(i, u)
        values(i, i, 4)

    for u in range(8):
        p = Panel(P_GATE + 16 + u)
        features(p, E_GATE + 16 + u, (E_GATE + 16 + u) % 4)
        if u < 2:
            for h in (2 * u, 2 * u + 1):
                pe.wait_ge(s.o_squared, h + 1)
                for t in range(TT):
                    ins = MM(b.ps[:, 7, 4 * h + t:4 * h + t + 1], b.osq[:, h % 2, P * t:P * t + P],
                             b.ones[:, 0:1], start=True, stop=True)
                ins.then_inc(s.ocol_done, 1)
        if 2 <= u < 6:
            h = u - 2
            pe.wait_ge(s.odiag_ready, h + 1)
            MM(b.ps[:, 4 + h, :], b.ones, b.diag[:, h % 2, :], start=True, stop=True).then_inc(s.orow_done, 1)

    pe.wait_ge(s.yab_ready, 4)
    pe.wait_ge(s.yc_ready, 4)
    with pe.Fori(0, 2) as i:
        for u in range(4):
            p = Panel(P_PROJ + u, RING, i)
            begin(p, None)
            n = 0
            for r, (xh, xl, ks) in enumerate(((b.yabh, b.yabl, (0, 1)), (b.yabh, b.yabl, (2, 3)),
                                              (b.ych, b.ycl, (0, 1, 2, 3)))):
                e = E_PROJ + 3 * u + r
                pe.wait_ge(s.evac, e - 3 + 12 * i)
                for k in ks:
                    wh, wl = w(p, P * n)
                    ins = three(b.ps[:, e % 4, :], wh, wl, xh[:, k, :], xl[:, k, :], k == ks[0], k == ks[-1])
                    n += 1
            ins.then_inc(s.panel_done, 1)

    def chunk_loop(p0, e0, xh, xl, ready=None):
        with pe.Fori(0, 2) as i:
            for u in range(4):
                features(Panel(p0 + u, RING, i), e0 + u + RING * i, (e0 + u) % 4, xh=xh, xl=xl,
                         ready=ready if u == 0 else None)

    chunk_loop(P_WOUT, E_WOUT, b.mh, b.ml, lambda k: pe.wait_ge(s.m_ready, k + 1))

    def up(i, first):
        for u in range(4):
            features(Panel(P_UP + u, RING, i), E_UP + u + RING * i, (E_UP + u) % 4,
                     ready=x_ready(8) if first and u == 0 else None,
                     middle=(lambda: row(2)) if first and u == 1 else None)
            if first and u == 0:
                column_sums(2, 18)

    up(0, True)
    with pe.Fori(1, FT1 // 2) as i:
        up(i, False)

    with pe.Fori(0, 2) as i:
        for c in range(4):
            first = 0
            for m, n in enumerate(DOWN1):
                p = Panel(P_DOWN + 3 * c + m, 12, i)
                ready = (lambda k: pe.wait_ge(s.act_ready, k + 1)) if c == 0 else None
                features(p, E_DOWN + c + 4 * i if m == 0 else None, (E_DOWN + c) % 4, xh=b.ah, xl=b.al,
                         tiles=range(first, first + n), last=FT1, ready=ready)
                first += n

    block2_tensor(nc, pe, s, b, MM, three, begin, w, features, column_sums, row, x_ready, tokens, scores, turn,
                  values, chunk_loop)



def level_views(b, ap, size):
    v = ap.rearrange("p (n w) -> p n w", w=2 * size)
    return v, v[:, :, 0:size], v[:, :, size:2 * size]


def block2_scalar(nc, act, s, b, dram, scratch, A, AR, hi, row, x_parts, x_square, residual_loop):
    hi(Panel(P_QA + RING))
    act.dma_start(b.mem[:], dram["mem"]).then_inc(s.mem_in, 16)
    hi(Panel(P_QA + 1 + RING))
    row(3)
    act.wait_ge(s.rowa_done, 1)
    A(b.rowa[:], b.ps[:, 6, :], ACT.Copy).then_inc(s.rowa_ready, 1)
    hi(Panel(P_QA + 2 + RING))
    act.wait_ge(s.mem_in, 16)
    act.wait_ge(s.sums2, 9)
    A(b.kx[:], b.mem[:], ACT.Square).then_inc(s.mem_sq, 1)
    hi(Panel(P_QA + 3 + RING))
    act.wait_ge(s.mem_scaled, 1)
    A(b.memh[:], b.mem[:], ACT.Copy).then_inc(s.mem_hi, 1)
    for u in range(3):
        hi(Panel(P_KA + u + RING))
    act.wait_ge(s.mrow_done, 1)
    A(b.mrow[:], b.ps[:, 5, 0:M], ACT.Copy).then_inc(s.mrow_ready, 1)
    hi(Panel(P_KA + 3 + RING))
    for u in range(4):
        hi(Panel(P_VA2 + u + RING))

    with act.Fori(0, 4) as i:
        act.wait_ge(s.scored, 8 * i + 32)
        act.dma_start(b.bias2[:], bias_tiles(scratch, 4 + 2 * i)).then_inc(s.bias_in, 16)
        act.wait_ge(s.score_done, 8 * i + 32)
        act.wait_ge(s.evac, E_KA + 4)
        AR(b.qh[:], b.qk[:, i, :], ACT.Copy, scale=0.125).then_inc(s.qk_hi, 1)
        AR(b.kh[:], b.qk[:, 4 + i, :], ACT.Copy).then_inc(s.qk_hi, 1)
        act.wait_ge(s.evac, E_VA2 + 4)
        act.wait_ge(s.pv_done, 2 * i + 4)
        AR(b.vh[:], b.v[:, :, bass.ds(P * i, P)], ACT.Copy).then_inc(s.v_hi, 1)
        for u in range(4):
            hi(Panel(P_PAIRS + u + RING, RING, i))
            if u < 2:
                act.wait_ge(s.negated, 2 * i + 8 + u + 1)
                for qb in range(TT):
                    n = 4 * u + qb
                    sc = b.s[:, u, pairs_offset(qb):pairs_offset(qb + 1)]
                    A(sc, sc, ACT.Exp, bias=b.neg[:, n:n + 1], accum_out=b.sums[:, n:n + 1]).then_inc(s.exped, 1)
            if u == 1:
                act.wait_ge(s.silued, i + 1)
                act.wait_ge(s.evac, 4 * i + E_PAIRS + 2)
                AR(b.tmp[:, 0, :], b.rg[:, i, :], ACT.Tanh, scale=0.5).then_inc(s.gated, 1)
            if u == 2:
                for c in range(2):
                    if c:
                        act.wait_ge(s.pv_done, 2 * i + 4 + c)
                    for kb in range(TT):
                        act.wait_ge(s.turned, 8 * i + 16 + 4 * c + kb + 1)
                        w = (TT - kb) * P
                        A(b.th[:, turned_offset(kb):turned_offset(kb) + w], b.ps[:, 5 + kb % 2, 0:w],
                          ACT.Copy).then_inc(s.turned_hi, 1)

    act.wait_ge(s.score_done, 64)
    act.wait_ge(s.pv_done, 12)
    act.wait_ge(s.turned_ready, 48)
    act.dma_start(b.masks[:], dram["late"].rearrange("p (l q) -> p l q", q=P)).then_inc(s.late_in, 16)
    act.dma_start(b.wgu[0:16, :], dram["wgu"]).then_inc(s.late_in, 16)
    for u in range(4):
        hi(Panel(P_VG + u + RING))
    hi(Panel(P_GLR + RING))
    for r in range(2):
        act.wait_ge(s.logit_done, r + 1)
        A(b.la[:, r, :], b.ps[:, 6 + r, :], ACT.Abs, bias=col(b, "b_gate2", r)).then_inc(s.logit_abs, 1)
    act.wait_ge(s.logit_abs, 2)
    A(b.la[:], b.la[:], ACT.Exp, scale=-1.0).then_inc(s.act_steps, 1)
    hi(Panel(P_XV + RING))
    act.wait_ge(s.act_steps, 1)
    A(b.la[:], b.la[:], ACT.Ln, bias=b.ones[:, 0:1]).then_inc(s.soft_ready, 1)
    hi(Panel(P_XV + 1 + RING))
    m = 2
    for r in range(2):
        act.wait_ge(s.b_ready, 2)
        if r:
            act.wait_ge(s.og_done, 2)
            act.wait_ge(s.states_ready, 7)
        A(b.ebl[:, 8 * r:8 * r + 8], b.b[:, r, CHUNK - 1::CHUNK], ACT.Exp, scale=1.0 / 16).then_inc(s.last_exped, 1)
        A(b.diag[:, 0, :], b.b[:, r, :], ACT.Exp, scale=1.0 / 16).then_inc(s.b_exped, 1)
        act.wait_ge(s.kd_shift, r + 1)
        A(b.diag[:, 1, :], b.diag[:, 1, :], ACT.Exp, scale=1.0 / 16).then_inc(s.kd_exped, 1)
        act.wait_ge(s.kd_turned, r + 1)
        if r:
            act.wait_ge(s.updates_done, 1)
        A(b.kdt[:], b.ps[:, 6, :].rearrange("p (t k) -> p t k", t=TT), ACT.Copy).then_inc(s.kd_copied, 1)
        hi(Panel(P_XV + m + RING))
        m += 1
        for n, size in enumerate(LEVELS):
            act.wait_ge(s.shifted, 6 * r + n + 1)
            _, first, second = level_views(b, b.tmp[:, n % 2, :], size)
            A(second, second, ACT.Exp, scale=1.0 / 16).then_inc(s.level_exped, 1)
            A(first, first, ACT.Exp, scale=-1.0 / 16).then_inc(s.level_exped, 1)
            if n in (1, 3, 5) and m < 8:
                hi(Panel(P_XV + m + RING))
                m += 1
        for a in range(2):
            act.wait_ge(s.og_done, 2 * r + a + 1)
            A(b.og[:, 2 * r + a, :], b.ps[:, 6 + a, :], ACT.Copy).then_inc(s.og_evac, 1)

    for h in range(4):
        act.wait_ge(s.og_evac, h + 1)
        act.wait_ge(s.level_done, 28)
        if h >= 2:
            act.wait_ge(s.gcol_done, h - 1)
        A(b.gsq[:, h % 2, :], b.og[:, h, :], ACT.Square).then_inc(s.og_squared, 1)
    act.wait_ge(s.o_evac, 12)
    act.wait_ge(s.level_ready, 12)
    for k in range(4):
        A(b.yh2[:, k, :], b.oa[:, k, :], ACT.Copy).then_inc(s.y_hi, 1)
    for h in range(4):
        act.wait_ge(s.og_normed, h + 1)
        A(b.yh2[:, 4 + h, :], b.og[:, h, :], ACT.Copy, scale=b.half_gn).then_inc(s.y_hi, 1)

    residual_loop(P_WOUT2, E_WOUT2, "norm_xattn", 3)

    def head_parts(h):
        if h:
            act.wait_ge(s.xscore_done, 4 * h)
        A(b.kxh[:], b.kx[:, 2 * h:2 * h + 2, :], ACT.Copy).then_inc(s.xkv_hi, 1)
        if h:
            act.wait_ge(s.xpv_done, 2 * h)
        else:
            act.wait_ge(s.evac, E_XV + 4)
        A(b.vxh[:], b.vx[:, :, 256 * h:256 * h + 256], ACT.Copy).then_inc(s.xkv_hi, 1)

    def xq(j):
        act.wait_ge(s.evac, E_XQ + j + 1)
        if j >= 2:
            act.wait_ge(s.xscore_done, 4 * (j // 2))
        A(b.qxh[:, j % 2, :], b.tmp[:, j % 2, :], ACT.Copy, scale=XSCALE).then_inc(s.xq_hi, 1)

    def exps(h):
        act.wait_ge(s.xneg, h + 1)
        if h:
            act.wait_ge(s.xturned, 2 * h)
        for qb in range(TT):
            A(b.xs[:, qb, :], b.ps[:, 4 + qb // 2, M * (qb % 2):M * (qb % 2) + M], ACT.Exp,
              bias=b.neg[:, qb:qb + 1], accum_out=b.sums[:, qb:qb + 1]).then_inc(s.xexped, 1)

    def turned_parts(h):
        if h:
            act.wait_ge(s.xpv_done, 2 * h)
        for mt in range(MT):
            act.wait_ge(s.xturned, 2 * h + mt + 1)
            A(b.xth[:, mt, :], b.ps[:, 6 + mt, :], ACT.Copy).then_inc(s.xturned_hi, 1)

    def out_parts(h):
        for d in range(2):
            act.wait_ge(s.xpv_done, 2 * h + d + 1)
            A(b.oxh[:, 2 * h + d, :], b.ps[:, 6 + d, :], ACT.Copy).then_inc(s.ox_hi, 1)

    act.wait_ge(s.panel_done, P_XQ + 1)
    for h in range(4):
        hi(Panel(P_XQ + 2 * h + RING))
        if h == 0:
            row(4)
            head_parts(0)
        else:
            turned_parts(h - 1)
        xq(2 * h)
        hi(Panel(P_XQ + 2 * h + 1 + RING))
        if h:
            out_parts(h - 1)
            head_parts(h)
        xq(2 * h + 1)
        exps(h)
    turned_parts(3)
    out_parts(3)

    residual_loop(P_XO, E_XO, "norm_mlp", 4)

    def up_body(p0, i, first, base):
        for u in range(4):
            hi(Panel(p0 + u + RING, RING, i))
            if first and u == 0:
                row(5)
            act.wait_ge(s.acted2, base + 4 * i + u + 1)
            AR(b.ah2[:, 4 * i + u, :], b.tmp[:, u % 2, :], ACT.Copy).then_inc(s.act2_hi, 1)

    def down_loop(p0, e0, last):
        if last:
            act.wait_ge(s.sums, 46)
        def body(i):
            for c in range(4):
                k = 4 * i + c
                for m in range(2):
                    hi(Panel(p0 + 2 * c + m + RING, 8, i))
                if last:
                    act.wait_ge(s.sums, 45 + k)
                    act.wait_ge(s.evac, e0 + k + 1)
                    x_square(k, c % 2)

        if last:
            body(0)
            body(1)
        else:
            with act.Fori(0, 2) as i:
                body(i)

    up_body(P_UP_A, 0, True, 0)
    with act.Fori(1, FH // 4) as i:
        up_body(P_UP_A, i, False, 0)
    down_loop(P_DOWN_A, E_DOWN_A, False)
    with act.Fori(0, FH // 4) as i:
        up_body(P_UP_B, i, False, FH)
    down_loop(P_DOWN_B, E_DOWN_B, True)
    row(6)


def block2_vector(nc, dve, s, b, st, lo, evac_row, mean, diagonal, x_rest, x_sum, residual_loop, score_rows):
    V = nc.vector

    def bank(e):
        return b.ps[:, e % 4, :]

    def evac_tokens(first, e0, base, dst):
        for u in range(3):
            dve.wait_ge(s.panel_done, first + u + 1)
            lo(Panel(first + u + RING))
        for t in range(TT):
            if t < TT - 1:
                dve.wait_ge(s.v_done, base + t + 1)
            else:
                dve.wait_ge(s.panel_done, first + 4)
            V.tensor_scalar(dst[:, t, :], bank(e0 + t), b.rs[:, t:t + 1], None, ALU.mult).then_inc(s.evac, 1)
        lo(Panel(first + 3 + RING))

    mean(3)
    V.tensor_scalar(b.sq_a, b.ps[:, 7, 4:8], 1.0 / D, None, ALU.mult).then_inc(s.steps, 1)
    st.n += 1
    lo(Panel(P_QA + RING))
    dve.wait_ge(s.pow_a, 1)
    st.wait()
    st.link(V.tensor_tensor(b.mean, b.rsa, b.sq_a, ALU.mult))
    st.link(V.tensor_tensor(b.mean, b.mean, b.rsa, ALU.mult))
    V.tensor_scalar(b.mean, b.mean, 1e-6, None, ALU.add).then_inc(s.mean_b, 1)
    diagonal(b.diag[:, 1, :], b.rsa).then_inc(s.diag_a, 1)
    dve.wait_ge(s.pow_done, 3)
    st.link(V.tensor_tensor(b.rs, b.rs, b.rsa, ALU.mult))
    diagonal(b.diag[:, 0, :], b.rs).then_inc(s.diag_ready, 1)
    lo(Panel(P_QA + 1 + RING))
    dve.wait_ge(s.row_ready, 3)
    for u in range(8):
        evac_row(Panel(P_QA + u), 0, b.qk[:, u, :], (E_QA + u) % 4)
        if u >= 2:
            lo(Panel(P_QA + u + RING))
        if u == 3:
            dve.wait_ge(s.mem_sq, 1)
            V.tensor_reduce(b.msum[:], b.kx[:].rearrange("p k m -> p m k"), AX_X, ALU.add).then_inc(s.mem_sums, 1)
            g = b.vec[:, VEC["norm_mem"]:VEC["norm_mem"] + KT]
            V.tensor_tensor(b.mem[:], b.mem[:], g.unsqueeze(2).to_broadcast([P, KT, M]),
                            ALU.mult).then_inc(s.mem_scaled, 1)
        if u == 5:
            dve.wait_ge(s.mcol_done, 1)
            V.tensor_scalar(b.mmean, b.ps[:, 5, 0:MT], 1.0 / D, 1e-6, ALU.mult, ALU.add).then_inc(s.mmean_ready, 1)
            dve.wait_ge(s.mem_hi, 1)
            dve.wait_ge(s.mem_scaled, 1)
            V.tensor_tensor(b.meml[:], b.mem[:], f32(b.memh[:]), ALU.subtract).then_inc(s.mem_ready, 1)
            dve.wait_ge(s.mpow_done, 1)
            dve.wait_ge(s.rowa_done, 1)
            V.tensor_tensor(b.diag[:, 1, 0:M].rearrange("p (a q) -> p a q", a=MT),
                            b.ident.unsqueeze(1).to_broadcast([P, MT, P]),
                            b.mrs.unsqueeze(2).to_broadcast([P, MT, P]), ALU.mult).then_inc(s.mdiag_ready, 1)
    evac_tokens(P_VA2, E_VA2, 3, b.v)
    V.tensor_scalar(b.half_gn, col(b, "g_norm", 0), 0.5, None, ALU.mult).then_inc(s.silued, 1)

    PAIR_STEPS = 2
    dve.wait_ge(s.mrow_ready, 1)
    with dve.Fori(0, 4) as i:
        st.enter(i, PAIR_STEPS)
        dve.wait_ge(s.qk_hi, 2 * i + 10)
        V.scalar_tensor_tensor(b.ql[:], b.qk[:, i, :], 0.125, f32(b.qh[:]), ALU.mult, ALU.subtract)
        V.tensor_tensor(b.kl[:], b.qk[:, 4 + i, :], f32(b.kh[:]), ALU.subtract).then_inc(s.qk_ready, 1)
        dve.wait_ge(s.v_hi, i + 5)
        V.tensor_tensor(b.vl[:], b.v[:, :, bass.ds(P * i, P)], f32(b.vh[:]), ALU.subtract).then_inc(s.v_ready, 1)

        def normalise(c):
            dve.wait_ge(s.exped, 8 * i + 32 + 4 * c + 4)
            st.link(V.reciprocal(b.rec[:, 4 * c:4 * c + 4], b.sums[:, 4 * c:4 * c + 4]))
            for qb in range(TT):
                sc = b.s[:, c, pairs_offset(qb):pairs_offset(qb + 1)]
                V.tensor_scalar(sc, sc, b.rec[:, 4 * c + qb:4 * c + qb + 1], None, ALU.mult).then_inc(s.blended, 1)

        def turned_rest(c):
            for kb in range(TT):
                w = (TT - kb) * P
                at = turned_offset(kb)
                dve.wait_ge(s.turned_hi, 8 * i + 16 + 4 * c + kb + 1)
                V.tensor_tensor(b.tl[:, at:at + w], b.ps[:, 5 + kb % 2, 0:w], f32(b.th[:, at:at + w]),
                                ALU.subtract).then_inc(s.turned_ready, 1)

        def out(c):
            dve.wait_ge(s.pv_done, 2 * i + 4 + c + 1)
            part = slice(64 * c, 64 * c + 64)
            V.tensor_copy(b.oa[part, i, :], b.ps[part, 7 if c else 4, :]).then_inc(s.o_evac, 1)

        for u in range(4):
            p = Panel(P_PAIRS + u, RING, i)
            slot = (E_PAIRS + u) % 4
            if u == 0:
                evac_row(p, 0, b.zg[:, i, :], slot)
            elif u == 1:
                evac_row(p, 0, b.rg[:, i, :], slot)
            else:
                dve.wait_ge(s.panel_done, p.index + 1)
                V.tensor_tensor(b.kx[:, 2 * i + u - 2, :], b.ps[:, slot, 0:M], b.mrow[:],
                                ALU.mult).then_inc(s.evac, 1)
            lo(Panel(P_PAIRS + u + RING, RING, i))
            if u == 0:
                dve.wait_ge(s.bias_in, 16 * i + 80)
            if u < 2:
                score_rows(i, u, 4, b.bias2[:, u, :])
            if u == 1:
                normalise(0)
            if u == 2:
                normalise(1)
                turned_rest(0)
                out(0)
                turned_rest(1)
            if u == 3:
                out(1)
                dve.wait_ge(s.gated, i + 25)
                dve.wait_ge(s.evac, 4 * i + E_PAIRS + 2)
                V.scalar_tensor_tensor(b.rg[:, i, :], b.tmp[:, 0, :], 1.0, b.rg[:, i, :], ALU.add,
                                       ALU.mult).then_inc(s.silued, 1)
    st.leave(4)

    dve.wait_ge(s.evac, E_PAIRS + 16)
    for r in range(2):
        st.mark(V.tensor_scalar(b.zg[:, r, :], b.zg[:, r, :], 0.125, None, ALU.mult))
    evac_tokens(P_VG, E_VG, 6, b.vg)
    dve.wait_ge(s.score_done, 64)
    st.link(V.memset(b.reset[:], 1.0))
    st.mark(V.memset(b.reset[:, 0::CHUNK], 0.0))
    st.mark(V.memset(b.ke[:], 0.0))
    dve.wait_ge(s.rowa_ready, 1)
    for k in range(KT):
        st.mark(V.scalar_tensor_tensor(b.x[:, k, :], b.x[:, k, :], col(b, "final_norm_g", k), b.rowa[:],
                                       ALU.mult, ALU.mult))
    evac_row(Panel(P_GLR), 0, b.glr[:], E_GLR % 4)
    lo(Panel(P_GLR + RING))

    def xv_slot(m):
        dve.wait_ge(s.panel_done, P_XV + m + 1)
        if m % 4 == 3:
            for t in range(MT):
                V.tensor_scalar(b.vx[:, t, 512 * (m // 4):512 * (m // 4) + 512], bank(E_XV + 2 * (m // 4) + t),
                                b.mrs[:, t:t + 1], None, ALU.mult).then_inc(s.evac, 1)
        lo(Panel(P_XV + m + RING))

    for r in range(2):
        dve.wait_ge(s.logit_abs, r + 1)
        st.mark(V.tensor_scalar(b.b[:, r, :], b.ps[:, 6 + r, :], col(b, "b_gate2", r), 0.0, ALU.add, ALU.min))
    xv_slot(0)
    dve.wait_ge(s.soft_ready, 1)
    st.wait()
    st.link(V.tensor_tensor(b.b[:], b.b[:], b.la[:], ALU.subtract))
    st.mark(V.memset(b.qe[:], 0.0))
    for r in range(2):
        V.tensor_tensor_scan(b.b[:, r, :], b.reset[:], b.b[:, r, :], 0.0, ALU.mult, ALU.add).then_inc(s.b_ready, 1)
    xv_slot(1)
    m = 2
    for r in range(2):
        q, k, run = b.zg[:, r, :], b.zg[:, 2 + r, :], b.b[:, r, :]
        dve.wait_ge(s.b_ready, 2)
        chunks = run.rearrange("p (c t) -> p c t", c=NC)
        if r:
            dve.wait_ge(s.kd_turned, 1)
        else:
            dve.wait_ge(s.mrow_done, 1)
        V.tensor_tensor(b.diag[:, 1, :].rearrange("p (c t) -> p c t", c=NC),
                        chunks[:, :, CHUNK - 1:CHUNK].to_broadcast([P, NC, CHUNK]), chunks,
                        ALU.subtract).then_inc(s.kd_shift, 1)
        dve.wait_ge(s.b_exped, r + 1)
        V.tensor_tensor(b.diag[:, 0, :], b.diag[:, 0, :], q, ALU.mult).then_inc(s.qb_ready, 1)
        dve.wait_ge(s.kd_exped, r + 1)
        V.tensor_tensor(b.diag[:, 1, :], b.diag[:, 1, :], k, ALU.mult).then_inc(s.kd_ready, 1)

        def shift(n):
            if r or n >= 2:
                dve.wait_ge(s.level_ready, 6 * r + max(n - 1, 0))
            v, _, _ = level_views(b, run, LEVELS[n])
            d, _, _ = level_views(b, b.tmp[:, n % 2, :], LEVELS[n])
            ref = v[:, :, LEVELS[n] - 1:LEVELS[n]].to_broadcast([P, T // (2 * LEVELS[n]), 2 * LEVELS[n]])
            V.tensor_tensor(d, v, ref, ALU.subtract).then_inc(s.shifted, 1)

        def apply(n):
            level = n + 1
            dve.wait_ge(s.level_exped, 12 * r + 2 * n + 2)
            if level >= 2:
                dve.wait_ge(s.level_done, 14 * r + 2 * level - 2)
            _, _, e2 = level_views(b, b.tmp[:, n % 2, :], LEVELS[n])
            _, _, q2 = level_views(b, q, LEVELS[n])
            _, _, qe2 = level_views(b, b.qe[:, level % 2, :], LEVELS[n])
            st.mark(V.tensor_tensor(qe2, q2, e2, ALU.mult))
            _, e1, _ = level_views(b, b.tmp[:, n % 2, :], LEVELS[n])
            _, k1, _ = level_views(b, k, LEVELS[n])
            _, ke1, _ = level_views(b, b.ke[:, level % 2, :], LEVELS[n])
            st.wait()
            V.tensor_tensor(ke1, k1, e1, ALU.mult).then_inc(s.level_ready, 1)

        def take(level):
            for a in range(2):
                dve.wait_ge(s.level_done, 14 * r + 2 * level + a + 1)
                if level:
                    dve.wait_ge(s.level_taken, 14 * r + 2 * level + a - 1)
                mask = b.masks[:, level, :].bitcast(U32).unsqueeze(1).to_broadcast([P, TT, P])
                src = b.ps[:, (6 if level % 2 else 4) + a, :].rearrange("p (t q) -> p t q", t=TT)
                V.copy_predicated(b.a[:, a, :].rearrange("p (t q) -> p t q", t=TT), mask,
                                  src).then_inc(s.level_taken, 1)

        xv_slot(m)
        m += 1
        shift(0)
        if r:
            dve.wait_ge(s.og_done, 2)
        else:
            dve.wait_ge(s.late_in, 32)
        st.mark(V.memset(b.a[:], 0.0))
        dve.wait_ge(s.updates_done, r + 1)
        dve.wait_ge(s.last_exped, r + 1)
        for c in range(NC - 1):
            upd = b.ps[:, 6 + c % 2, P * (c // 2):P * (c // 2) + P]
            if c == 0:
                ins = V.tensor_copy(b.states[:, 1, :], upd)
            else:
                dve.wait_ge(s.states_ready, 7 * r + c)
                ins = V.scalar_tensor_tensor(b.states[:, c + 1, :], b.states[:, c, :],
                                             b.ebl[:, 8 * r + c:8 * r + c + 1], upd, ALU.mult, ALU.add)
            ins.then_inc(s.states_ready, 1)
        st.wait()
        take(0)
        apply(0)
        for n in range(len(LEVELS)):
            if n + 1 < len(LEVELS):
                shift(n + 1)
            take(n + 1)
            if n % 2 == 0 and m < 8:
                xv_slot(m)
                m += 1
            if n + 1 < len(LEVELS):
                apply(n + 1)

    for k in range(4):
        dve.wait_ge(s.y_hi, k + 1)
        V.tensor_tensor(b.yl2[:, k, :], b.oa[:, k, :], f32(b.yh2[:, k, :]), ALU.subtract).then_inc(s.y_ready, 1)
        if k == 0:
            dve.wait_ge(s.gcol_done, 4)
            V.tensor_scalar(b.gmean, b.ps[:, 7, 0:16], 1.0 / P, 1e-6, ALU.mult, ALU.add).then_inc(s.gmean_ready, 1)
    dve.wait_ge(s.gpow_done, 1)
    for h in range(4):
        if h >= 2:
            dve.wait_ge(s.grow_done, h - 1)
        diagonal(b.diag[:, h % 2, :], b.grs[:, 4 * h:4 * h + 4]).then_inc(s.gdiag_ready, 1)
    st.wait()
    for h in range(4):
        dve.wait_ge(s.grow_done, h + 1)
        st.link(V.tensor_tensor(b.og[:, h, :], b.og[:, h, :], b.ps[:, 4 + h, :], ALU.mult))
        V.tensor_tensor(b.og[:, h, :], b.og[:, h, :], b.rg[:, h, :], ALU.mult).then_inc(s.og_normed, 1)
    for h in range(4):
        dve.wait_ge(s.y_hi, 4 + h + 1)
        V.scalar_tensor_tensor(b.yl2[:, 4 + h, :], b.og[:, h, :], b.half_gn, f32(b.yh2[:, 4 + h, :]),
                               ALU.mult, ALU.subtract).then_inc(s.y_ready, 1)

    residual_loop(P_WOUT2, E_WOUT2, "norm_xattn", 3)

    def norm_row(n):
        mean(n)
        dve.wait_ge(s.pow_done, n)
        diagonal(b.diag[:, 0, :], b.rs).then_inc(s.diag_ready, 1)

    def head_rest(h):
        dve.wait_ge(s.xkv_hi, 2 * h + 1)
        st.mark(V.tensor_tensor(b.kxl[:], b.kx[:, 2 * h:2 * h + 2, :], f32(b.kxh[:]), ALU.subtract))
        dve.wait_ge(s.xkv_hi, 2 * h + 2)
        V.tensor_tensor(b.vxl[:], b.vx[:, :, 256 * h:256 * h + 256], f32(b.vxh[:]), ALU.subtract).then_inc(
            s.xkv_ready, 1)

    def q_chunk(j):
        if j >= 2:
            dve.wait_ge(s.xq_ready, j - 1)
        evac_row(Panel(P_XQ + j), 0, b.tmp[:, j % 2, :], (E_XQ + j) % 4)
        lo(Panel(P_XQ + j + RING))

    def q_rest(j):
        dve.wait_ge(s.xq_hi, j + 1)
        dve.wait_ge(s.evac, E_XQ + j + 1)
        V.scalar_tensor_tensor(b.qxl[:, j % 2, :], b.tmp[:, j % 2, :], XSCALE, f32(b.qxh[:, j % 2, :]),
                               ALU.mult, ALU.subtract).then_inc(s.xq_ready, 1)

    def maxima(h):
        for half in range(2):
            dve.wait_ge(s.xscore_done, 4 * h + 2 * half + 2)
            if h:
                dve.wait_ge(s.xneg, h)
            st.mark(V.tensor_reduce(b.mx[:, 2 * half:2 * half + 2],
                                    b.ps[:, 4 + half, :].rearrange("p (a m) -> p a m", a=2), AX_X, ALU.max))
        st.wait()
        V.tensor_scalar(b.neg[:, 0:4], b.mx[:, 0:4], -1.0, None, ALU.mult).then_inc(s.xneg, 1)

    def normalise_x(h):
        dve.wait_ge(s.xexped, 4 * h + 4)
        st.link(V.reciprocal(b.rec[:, 0:4], b.sums[:, 0:4]))
        for qb in range(TT):
            V.tensor_scalar(b.xs[:, qb, :], b.xs[:, qb, :], b.rec[:, qb:qb + 1], None,
                            ALU.mult).then_inc(s.xblended, 1)

    def turned_rest_x(h):
        for mt in range(MT):
            dve.wait_ge(s.xturned_hi, 2 * h + mt + 1)
            V.tensor_tensor(b.xtl[:, mt, :], b.ps[:, 6 + mt, :], f32(b.xth[:, mt, :]),
                            ALU.subtract).then_inc(s.xturned_ready, 1)

    def out_rest(h):
        for d in range(2):
            dve.wait_ge(s.ox_hi, 2 * h + d + 1)
            V.tensor_tensor(b.oxl[:, 2 * h + d, :], b.ps[:, 6 + d, :], f32(b.oxh[:, 2 * h + d, :]),
                            ALU.subtract).then_inc(s.ox_ready, 1)

    norm_row(4)
    dve.wait_ge(s.row_ready, 4)
    for h in range(4):
        q_chunk(2 * h)
        if h:
            turned_rest_x(h - 1)
        else:
            head_rest(0)
        q_rest(2 * h)
        q_chunk(2 * h + 1)
        if h:
            out_rest(h - 1)
            head_rest(h)
        q_rest(2 * h + 1)
        maxima(h)
        normalise_x(h)
    turned_rest_x(3)
    out_rest(3)

    residual_loop(P_XO, E_XO, "norm_mlp", 4)

    def rest(j, half, base):
        dve.wait_ge(s.act2_hi, base + j + 1)
        dve.wait_ge(s.acted2, base + j + 1)
        V.tensor_tensor(b.al2[:, j, :], b.tmp[:, half, :], f32(b.ah2[:, j, :]), ALU.subtract).then_inc(
            s.act2_ready, 1)

    def up_body(p0, e0, i, base):
        for u in range(4):
            j = 4 * i + u
            evac_row(Panel(p0 + u, RING, i), 0, b.tmp[:, u % 2, :], (e0 + u) % 4)
            lo(Panel(p0 + u + RING, RING, i))
            dve.wait_ge(s.evac, e0 + j + 1)
            V.scalar_tensor_tensor(b.tmp[:, u % 2, :], b.tmp[:, u % 2, :], 0.0, b.tmp[:, u % 2, :], ALU.max,
                                   ALU.mult).then_inc(s.acted2, 1)
            rest(j, u % 2, base)

    def down_loop(p0, e0, last):
        def body(i):
            for c in range(4):
                k = 4 * i + c
                for m in range(2):
                    p = Panel(p0 + 2 * c + m, 8, i)
                    dve.wait_ge(s.panel_done, p.index + 1)
                    if m == 1:
                        V.tensor_tensor(b.x[:, k, :], b.x[:, k, :], b.ps[:, (e0 + c) % 4, :],
                                        ALU.add).then_inc(s.evac, 1)
                    lo(p.plus(RING))
                if last:
                    x_sum(c % 2, 40 + k + 1, 46 + k)

        if last:
            body(0)
            body(1)
        else:
            with dve.Fori(0, 2) as i:
                body(i)

    norm_row(5)
    dve.wait_ge(s.row_ready, 5)
    with dve.Fori(0, FH // 4) as i:
        up_body(P_UP_A, E_UP_A, i, 0)
    down_loop(P_DOWN_A, E_DOWN_A, False)
    with dve.Fori(0, FH // 4) as i:
        up_body(P_UP_B, E_UP_B, i, FH)
    V.memset(b.sumsq[:], 0.0).then_inc(s.sums, 1)
    down_loop(P_DOWN_B, E_DOWN_B, True)

    norm_row(6)
    dve.wait_ge(s.row_ready, 6)
    dve.wait_ge(s.evac, E_END)
    for k in range(KT):
        V.scalar_tensor_tensor(b.x[:, k, :], b.x[:, k, :], col(b, "norm_final", k), b.rrow[:], ALU.mult,
                               ALU.mult).then_inc(s.final_scaled, 1)


def block2_tensor(nc, pe, s, b, MM, three, begin, w, features, column_sums, row, x_ready, tokens, scores, turn,
                  values, chunk_loop):
    def norm_rows():
        row(3)
        pe.wait_ge(s.diag_a, 1)
        MM(b.ps[:, 6, :], b.ones, b.diag[:, 1, :], start=True, stop=True).then_inc(s.rowa_done, 1)

    def memory_row():
        pe.wait_ge(s.mdiag_ready, 1)
        MM(b.ps[:, 5, 0:M], b.ones, b.diag[:, 1, 0:M], start=True, stop=True).then_inc(s.mrow_done, 1)

    for u in range(8):
        features(Panel(P_QA + u), E_QA + u, (E_QA + u) % 4, ready=x_ready(16) if u == 0 else None,
                 middle={2: norm_rows, 7: memory_row}.get(u))
        if u == 0:
            pe.wait_ge(s.sums2, 9)
            pe.wait_ge(s.row_ready, 2)
            for t in range(TT):
                MM(b.ps[:, 7, 4 + t:5 + t], b.sum2[:, P * t:P * t + P], b.ones[:, 0:1], start=True, stop=True)
            column_sums(3, 27)
        if u == 4:
            pe.wait_ge(s.mem_sums, 1)
            for t in range(MT):
                ins = MM(b.ps[:, 5, t:t + 1], b.msum[:, P * t:P * t + P], b.ones[:, 0:1], start=True, stop=True)
            ins.then_inc(s.mcol_done, 1)
    tokens(P_VA2, E_VA2, s.v_done)

    pe.wait_ge(s.mem_ready, 1)
    pe.wait_ge(s.mrow_ready, 1)
    pe.wait_ge(s.rowa_ready, 1)
    with pe.Fori(0, 4) as i:
        def between():
            values(4 + 2 * i, 4 + i, 4)
            turn(5 + 2 * i, 1)

        for u in range(4):
            moving = {} if u < 2 else {"xh": b.memh, "xl": b.meml, "width": M}
            features(Panel(P_PAIRS + u, RING, i), E_PAIRS + u + RING * i, (E_PAIRS + u) % 4,
                     middle=between if u == 3 else None, **moving)
            if u == 0:
                pe.wait_ge(s.qk_ready, i + 5)
                pe.wait_ge(s.o_evac, 2 * i + 4)
            if u < 2:
                scores(4 + i, u)
            if u == 2:
                pe.wait_ge(s.scored, 8 * i + 40)
                turn(4 + 2 * i, 0)
        values(5 + 2 * i, 4 + i, 7)

    tokens(P_VG, E_VG, s.v_done)
    features(Panel(P_GLR), E_GLR, E_GLR % 4)
    pe.wait_ge(s.late_in, 32)
    pe.wait_ge(s.evac, E_GLR + 1)
    pe.wait_ge(s.o_evac, 12)
    pe.wait_ge(s.turned_ready, 48)
    for r in range(2):
        MM(b.ps[:, 6 + r, :], b.wgu[0:16, P * r:P * r + P], b.glr[0:16, :], start=True,
           stop=True).then_inc(s.logit_done, 1)

    def xv(m):
        p = Panel(P_XV + m)
        begin(p, None)
        half = m // 4
        for t in range(MT):
            e = E_XV + 2 * half + t
            if m % 4 == 0:
                pe.wait_ge(s.evac, e - 3)
            for n in range(2):
                k = 2 * (m % 4) + n
                wh, wl = w(p, 512 * n, 512)
                tok = slice(P * t, P * t + P)
                ins = three(b.ps[:, e % 4, :], b.memh[:, k, tok], b.meml[:, k, tok], wh, wl, k == 0, k == KT - 1)
        ins.then_inc(s.panel_done, 1)

    xv(0)
    xv(1)
    m = 2
    for r in range(2):
        pe.wait_ge(s.kd_ready, r + 1)
        if r:
            pe.wait_ge(s.og_evac, 2)
        else:
            pe.wait_ge(s.b_ready, 2)
        for t in range(TT):
            ins = nc.tensor.transpose(b.ps[:, 6, P * t:P * t + P], b.diag[:, 1, P * t:P * t + P], b.ident)
        ins.then_inc(s.kd_turned, 1)
        xv(m)
        m += 1
        pe.wait_ge(s.kd_copied, r + 1)
        pe.wait_ge(s.evac, E_VG + 4)
        for c in range(NC - 1):
            rows = slice(64 * (c % 2), 64 * (c % 2) + 64)
            for a in range(2):
                head = 2 * r + a
                ins = MM(b.ps[64 * a:64 * a + 64, 6 + c % 2, P * (c // 2):P * (c // 2) + P],
                         b.kdt[rows, c // 2, 64 * a:64 * a + 64], b.vg[rows, c // 2, P * head:P * head + P],
                         start=True, stop=True, skip_group_check=True)
        ins.then_inc(s.updates_done, 1)
        for level in range(len(LEVELS) + 1):
            if level:
                pe.wait_ge(s.level_ready, 6 * r + level)
                q, k = b.qe[:, level % 2, :], b.ke[:, level % 2, :]
            else:
                q, k = b.zg[:, r, :], b.zg[:, 2 + r, :]
            for a in range(2):
                if level == 0 and r:
                    pe.wait_ge(s.level_taken, 14)
                elif level == 1:
                    pe.wait_ge(s.states_ready, 7 * r + 7)
                elif level >= 2:
                    pe.wait_ge(s.level_taken, 14 * r + 2 * level - 3 + a)
                part = slice(64 * a, 64 * a + 64)
                for t in range(TT):
                    tok = slice(P * t, P * t + P)
                    ins = MM(b.ps[:, (6 if level % 2 else 4) + a, tok], k[part, tok], q[part, tok], start=True,
                             stop=True)
                ins.then_inc(s.level_done, 1)
            if level in (1, 3, 5) and m < 8:
                xv(m)
                m += 1
        pe.wait_ge(s.level_taken, 14 * r + 14)
        pe.wait_ge(s.qb_ready, r + 1)
        for a in range(2):
            head = 2 * r + a
            for t in range(TT):
                tok = slice(P * t, P * t + P)
                MM(b.ps[:, 6 + a, tok], b.vg[:, t, P * head:P * head + P], b.a[:, a, tok], start=t == 0,
                   stop=False, skip_group_check=True)
            part = slice(64 * a, 64 * a + 64)
            for c in range(1, NC):
                tok = slice(CHUNK * c, CHUNK * c + CHUNK)
                ins = MM(b.ps[:, 6 + a, tok], b.states[part, c, :], b.diag[part, 0, tok], start=False,
                         stop=c == NC - 1, skip_group_check=True)
            ins.then_inc(s.og_done, 1)

    for h in range(4):
        pe.wait_ge(s.og_squared, h + 1)
        for t in range(TT):
            ins = MM(b.ps[:, 7, 4 * h + t:4 * h + t + 1], b.gsq[:, h % 2, P * t:P * t + P], b.ones[:, 0:1],
                     start=True, stop=True)
        ins.then_inc(s.gcol_done, 1)
    for h in range(4):
        pe.wait_ge(s.gdiag_ready, h + 1)
        MM(b.ps[:, 4 + h, :], b.ones, b.diag[:, h % 2, :], start=True, stop=True).then_inc(s.grow_done, 1)

    chunk_loop(P_WOUT2, E_WOUT2, b.yh2, b.yl2, lambda k: pe.wait_ge(s.y_ready, k + 1))

    def xscores(h):
        pe.wait_ge(s.xkv_ready, h + 1)
        pe.wait_ge(s.xq_ready, 2 * h + 2)
        if h:
            pe.wait_ge(s.xexped, 4 * h)
        for qb in range(TT):
            tok = slice(P * qb, P * qb + P)
            for d in range(2):
                ins = three(b.ps[:, 4 + qb // 2, M * (qb % 2):M * (qb % 2) + M], b.qxh[:, d, tok], b.qxl[:, d, tok],
                            b.kxh[:, d, :], b.kxl[:, d, :], d == 0, d == 1)
            ins.then_inc(s.xscore_done, 1)

    def xturn(h):
        pe.wait_ge(s.xblended, 4 * h + 4)
        if h:
            pe.wait_ge(s.ox_ready, 2 * h)
        for mt in range(MT):
            for qb in range(TT):
                ins = nc.tensor.transpose(b.ps[:, 6 + mt, P * qb:P * qb + P], b.xs[:, qb, P * mt:P * mt + P], b.ident)
            ins.then_inc(s.xturned, 1)

    def xvalues(h):
        pe.wait_ge(s.xturned_ready, 2 * h + 2)
        for d in range(2):
            for mt in range(MT):
                ins = three(b.ps[:, 6 + d, :], b.vxh[:, mt, P * d:P * d + P], b.vxl[:, mt, P * d:P * d + P],
                            b.xth[:, mt, :], b.xtl[:, mt, :], mt == 0, mt == MT - 1)
            ins.then_inc(s.xpv_done, 1)

    for j in range(8):
        h = j // 2
        features(Panel(P_XQ + j), E_XQ + j, (E_XQ + j) % 4, ready=x_ready(24) if j == 0 else None,
                 middle=(lambda: row(4)) if j == 1 else None)
        if j == 0:
            column_sums(4, 36)
        if j % 2 == 0 and h:
            xturn(h - 1)
        if j % 2:
            if h:
                xvalues(h - 1)
            xscores(h)

    for k in range(KT):
        features(Panel(P_XO + k), E_XO + k, (E_XO + k) % 4, xh=b.oxh, xl=b.oxl,
                 ready=(lambda d: pe.wait_ge(s.ox_ready, d + 1)) if k == 0 else None,
                 middle=(lambda: xturn(3)) if k == 0 else None, late=(lambda: xvalues(3)) if k == 0 else None)

    def up_body(p0, e0, i, first):
        for u in range(4):
            features(Panel(p0 + u, RING, i), e0 + u + RING * i, (e0 + u) % 4,
                     ready=x_ready(32) if first and u == 0 else None,
                     middle=(lambda: row(5)) if first and u == 1 else None)
            if first and u == 0:
                column_sums(5, 45)

    def down_loop(p0, e0, base):
        with pe.Fori(0, 2) as i:
            for c in range(4):
                for m in range(2):
                    features(Panel(p0 + 2 * c + m, 8, i), e0 + c + 4 * i if m == 0 else None, (e0 + c) % 4,
                             xh=b.ah2, xl=b.al2, tiles=range(KT * m, KT * m + KT), last=FH,
                             ready=(lambda k: pe.wait_ge(s.act2_ready, base + k + 1)) if c == 0 else None)

    up_body(P_UP_A, E_UP_A, 0, True)
    with pe.Fori(1, FH // 4) as i:
        up_body(P_UP_A, E_UP_A, i, False)
    down_loop(P_DOWN_A, E_DOWN_A, 0)
    with pe.Fori(0, FH // 4) as i:
        up_body(P_UP_B, E_UP_B, i, False)
    down_loop(P_DOWN_B, E_DOWN_B, FH)
    column_sums(6, 54)
    row(6)


def tiles(w):
    return w.reshape(-1, P, w.shape[1])


def chunk_panels(w):
    k, n = w.shape
    return w.reshape(k // P, P, n // P, P).transpose(2, 1, 0, 3).reshape(n // P, P, -1)


def row_panels(w):
    k, n = w.shape
    return w.reshape(k * n // (P * D), D // n, P, n).transpose(0, 2, 1, 3).reshape(-1, P, D)


def down_panels(w, parts):
    per = chunk_panels(w).reshape(w.shape[1] // P, P, -1, P)
    out = np.zeros((per.shape[0], len(parts), P, KT, P), w.dtype)
    at = 0
    for m, n in enumerate(parts):
        out[:, m, :, :n] = per[:, :, at:at + n]
        at += n
    return out.reshape(-1, P, D)


def vector(v):
    return v.reshape(-1, P).T


def shape_constants():
    consts = np.stack([np.eye(P, dtype=np.float32), np.ones((P, P), np.float32)], 1)
    windows = np.repeat(np.array([2, 4, 8, 16]), 64).reshape(2, P).T
    t = np.arange(T)
    inv = (1.0 / np.minimum(t[None, None] + 1, windows[:, :, None])).astype(np.float32)
    rel = T - 1 - np.arange(T)
    large = 16 + (np.log(np.maximum(rel, 1) / 16) / np.log(8) * 16).astype(int)
    bucket = np.where(rel < 16, rel, np.minimum(large, NB - 1))
    onehot = (bucket[None] == np.arange(NB)[:, None]).astype(np.float32)
    return consts, inv, onehot


def level_masks():
    j, i = np.arange(P)[:, None], np.arange(P)[None]
    masks = [j == i]
    for n in LEVELS:
        masks.append((j // (2 * n) == i // (2 * n)) & (j // n % 2 == 0) & (i // n % 2 == 1))
    return np.stack(masks, 1).astype(np.float32)


def layout(a):
    w_in, gate, up = a["w_in"][0], a["w_gate"][0], a["w_up"][0]
    gate_up = np.stack([chunk_panels(up[:, :FF1]), chunk_panels(up[:, FF1:])], 1).reshape(-1, P, D)
    projections = np.concatenate([a["proj_a"][0], a["proj_b"][0], a["proj_c"][0]], 0)
    stream = [chunk_panels(w_in[:, 0:256]), row_panels(w_in[:, 256:512]), chunk_panels(w_in[:, 512:768]),
              chunk_panels(w_in[:, 768:1792]), row_panels(w_in[:, 1792:2304]), chunk_panels(gate),
              chunk_panels(projections), chunk_panels(a["w_out"][0]), gate_up, down_panels(a["w_down"][0], DOWN1)]
    w2, xkv = a["w_in_2"][0], a["w_xkv_2"][0]
    glr = chunk_panels(w2[:, 2560:2560 + P])
    qk_g = chunk_panels(w2[:, 1536:2048])
    r_g = chunk_panels(w2[:, 2576:3088])
    xk = chunk_panels(xkv[:, 0:D])
    pairs = np.stack([qk_g, r_g, xk[0::2], xk[1::2]], 1).reshape(-1, P, D)
    w_up2, w_down2 = a["w_up_2"][0], a["w_down_2"][0]
    half = FF2 // 2
    stream += [chunk_panels(w2[:, 0:1024]), row_panels(w2[:, 1024:1536]), pairs, row_panels(w2[:, 2048:2560]),
               glr, row_panels(xkv[:, D:D + 512]), row_panels(xkv[:, D + 512:2 * D]), chunk_panels(a["w_out_2"][0]),
               chunk_panels(a["w_xq_2"][0]), chunk_panels(a["w_xo_2"][0])]
    for n in range(2):
        stream += [chunk_panels(w_up2[:, half * n:half * n + half]),
                   down_panels(w_down2[half * n:half * n + half], (KT, KT))]
    vec = [a["attn_norm_g"][0], a["b_gate"][0], a["ffn_norm_g"][0], a["conv_w"][0, 0], a["conv_w"][0, 1],
           a["conv_w"][0, 2], a["conv_b"][0], a["final_norm_g"], a["diff_subln_g"][0], a["pool_scale"][0],
           a["norm_mix_2"][0], a["b_gate_2"][0], a["g_norm_2"][0], a["norm_xattn_2"][0], a["norm_mem_2"][0],
           a["norm_mlp_2"][0], a["norm_final_2"]]
    consts, inv, onehot = shape_constants()
    sgu_b = np.repeat(a["sgu_b"][0].reshape(2, 2, P), 64, axis=1).transpose(1, 0, 2).reshape(P, 256)
    wide = np.concatenate([a["sgu_ln_g"][0], a["sgu_ln_b"][0], a["diff_lam"][0].reshape(-1)])
    early = np.concatenate([sgu_b, np.broadcast_to(wide, (P, wide.size))], 1)
    tables = np.concatenate([a["rel_bias"], a["rp_table_2"]], 1)
    return {
        "stream": np.concatenate(stream, 0),
        "late": np.concatenate([level_masks().reshape(P, -1)], 1),
        "wgu": a["w_gate_up_2"][0],
        "mem": a["mem_2"][0].T.reshape(KT, P, M).transpose(1, 0, 2),
        "x": a["x"][0].T.reshape(KT, P, T).transpose(1, 0, 2),
        "vec": np.concatenate([vector(v) for v in vec], 1),
        "consts": consts, "inv_count": inv, "onehot": onehot, "early": early,
        "tables": np.repeat(tables, P, axis=1),
        "sgu_w": a["sgu_w"][0].transpose(2, 0, 1),
        "pool_w": a["pool_w"][0].reshape(2, P, 64).transpose(1, 0, 2),
    }


def kernel(**inputs):
    import concourse.bacc as bacc
    from concourse.bass_utils import run_bass_kernel_spmd

    arrays = {f"{k}_dram": np.ascontiguousarray(v) for k, v in layout({k: np.asarray(v) for k, v in inputs.items()}).items()}
    nc = bacc.Bacc("TRN2", target_bir_lowering=False, num_devices=1, dynamic_dma_scratch_size=1024)
    dram = {k[:-5]: nc.dram_tensor(k, v.shape, mybir.dt.from_np(v.dtype), kind="ExternalInput").ap()
            for k, v in arrays.items()}
    out = nc.dram_tensor("out_dram", (D, T), F32, kind="ExternalOutput").ap()
    build(nc, dram, out)
    got = run_bass_kernel_spmd(nc, [arrays], core_ids=[0]).results[0]["out_dram"]
    return np.ascontiguousarray(got.T).reshape(1, T, D)
```

```python
import math

import numpy as np

import concourse.bass as bass
from concourse import mybir

F32 = mybir.dt.float32
F32R = mybir.dt.float32r
U32 = mybir.dt.uint32
ALU = mybir.AluOpType
ACT = mybir.ActivationFunctionType
AX_X = mybir.AxisListType.X

P = 128
D = 1024
KT = D // P
T = 512
TT = T // P
RING = 4
AHEAD = 3
FF1 = 2816
FT1 = FF1 // P
DOWN1 = (8, 7, 7)
NB = 32
LINE = 640
NEG = -1.0e30
LAM_INIT = 0.8 - 0.6 * math.exp(0.0)

P_U, P_VA, P_POOL, P_Q, P_K, P_V, P_GATE, P_PROJ, P_WOUT, P_UP, P_DOWN = 0, 2, 4, 6, 10, 14, 18, 42, 50, 58, 102
P_END1 = P_DOWN + 3 * KT
(P_QA, P_KA, P_VA2, P_PAIRS, P_GLR, P_VG, P_XV, P_WOUT2, P_XQ, P_XO, P_UP_A, P_DOWN_A, P_UP_B, P_DOWN_B,
 P_END) = (P_END1 + n for n in (0, 4, 8, 12, 28, 29, 33, 41, 49, 57, 65, 81, 97, 113, 129))
E_U, E_VA, E_POOL, E_Q, E_K, E_V, E_GATE, E_PROJ, E_WOUT, E_UP, E_DOWN = 0, 2, 4, 6, 10, 14, 18, 42, 66, 74, 118
E_END1 = E_DOWN + KT
(E_QA, E_KA, E_VA2, E_PAIRS, E_GLR, E_VG, E_XV, E_WOUT2, E_XQ, E_XO, E_UP_A, E_DOWN_A, E_UP_B, E_DOWN_B,
 E_END) = (E_END1 + n for n in (0, 4, 8, 12, 28, 29, 33, 37, 45, 53, 61, 77, 85, 101, 109))
M = 256
MT = M // P
FF2 = 4096
FH = FF2 // P // 2
CHUNK = 128
NC = T // CHUNK
LEVELS = (64, 32, 16, 8, 4, 2, 1)
HEAD_ORDER = (2, 3, 0, 1)
XSCALE = 1.0 / 16

VEC = {}


def _vec_columns():
    at = 0
    for name, n in (("attn_norm_g", 8), ("b_gate", 24), ("ffn_norm_g", 8), ("conv0", 22), ("conv1", 22),
                    ("conv2", 22), ("conv_b", 22), ("final_norm_g", 8), ("subln", 1), ("pool_scale", 2),
                    ("norm_mix", 8), ("b_gate2", 2), ("g_norm", 1), ("norm_xattn", 8), ("norm_mem", 8),
                    ("norm_mlp", 8), ("norm_final", 8)):
        VEC[name] = at
        at += n
    return at


NVEC = _vec_columns()


class Panel:

    def __init__(self, first, step=0, i=0):
        self.first, self.step, self.i = first, step, i
        self.slot = first % RING
        self.index = first + step * i if step else first
        self.round = first // RING + 1 + (step // RING) * i if step else first // RING + 1

    def plus(self, n):
        return Panel(self.first + n, self.step, self.i)


class Steps:

    def __init__(self, eng, sem):
        self.eng, self.sem, self.n, self.per, self.i = eng, sem, 0, 0, 0

    def enter(self, i, per):
        self.i, self.per, self.start = i, per, self.n

    def leave(self, count):
        assert self.n - self.start == self.per, (self.n - self.start, self.per)
        self.n = self.start + self.per * count
        self.per = 0

    def mark(self, ins):
        ins.then_inc(self.sem, 1)
        self.n += 1

    def wait(self):
        self.eng.wait_ge(self.sem, self.n + self.per * self.i if self.per else self.n)

    def link(self, ins):
        self.mark(ins)
        self.wait()


def pairs_offset(qb):
    return P * (qb * (qb + 1) // 2)


SCORES = pairs_offset(TT)


def turned_offset(kb):
    return P * (kb * TT - kb * (kb - 1) // 2)


class Names:
    pass


def semaphores(nc):
    s = Names()

    def named(names):
        return [nc.alloc_semaphore(name) for name in names.split()]

    (s.panel_done, s.lo_ready, s.hi_ready, s.evac) = named(
        "panel_done lo_ready hi_ready evac")
    (s.steps, s.vec_in, s.consts_in, s.early_in) = named(
        "steps vec_in consts_in early_in")
    (s.line_in, s.lines_out, s.lines_set, s.line_done) = named(
        "line_in lines_out lines_set line_done")
    (s.line_copied, s.x_hi, s.x_squared, s.h_ready) = named(
        "line_copied x_hi x_squared h_ready")
    (s.sums, s.col_done, s.mean_ready, s.pow_done) = named(
        "sums col_done mean_ready pow_done")
    (s.diag_ready, s.row_done, s.row_ready, s.u_ready) = named(
        "diag_ready row_done row_ready u_ready")
    (s.va_gelu, s.ln_mean, s.ln_pow, s.v_normed) = named(
        "va_gelu ln_mean ln_pow v_normed")
    (s.ws_masked, s.spatial_done, s.pooled, s.poolmm_done) = named(
        "ws_masked spatial_done pooled poolmm_done")
    (s.lam_dots, s.lam_exps, s.v_done, s.qk_hi) = named(
        "lam_dots lam_exps v_done qk_hi")
    (s.qk_ready, s.v_hi, s.v_ready, s.bias_in) = named(
        "qk_ready v_hi v_ready bias_in")
    (s.score_done, s.scored, s.negated, s.exped) = named(
        "score_done scored negated exped")
    (s.blended, s.turned, s.turned_hi, s.turned_ready) = named(
        "blended turned turned_hi turned_ready")
    (s.pv_done, s.o_evac, s.gated, s.o_squared) = named(
        "pv_done o_evac gated o_squared")
    (s.ocol_done, s.omean_ready, s.opow_done, s.odiag_ready) = named(
        "ocol_done omean_ready opow_done odiag_ready")
    (s.orow_done, s.o_normed, s.yc_hi, s.yc_ready) = named(
        "orow_done o_normed yc_hi yc_ready")
    (s.yab_written, s.yab_hi, s.yab_ready, s.m_summed) = named(
        "yab_written yab_hi yab_ready m_summed")
    (s.m_hi, s.m_ready, s.tapped, s.conved) = named(
        "m_hi m_ready tapped conved")
    (s.gelued, s.acted, s.act_hi, s.act_ready) = named(
        "gelued acted act_hi act_ready")
    (s.out_done, s.x_second, s.sums2, s.act_steps) = named(
        "out_done x_second sums2 act_steps")
    (s.pow_a, s.mean_b, s.rowa_done, s.rowa_ready) = named(
        "pow_a mean_b rowa_done rowa_ready")
    (s.mem_in, s.mem_hi, s.mem_sq, s.mem_sums) = named(
        "mem_in mem_hi mem_sq mem_sums")
    (s.mem_ready, s.mcol_done, s.mmean_ready, s.mpow_done) = named(
        "mem_ready mcol_done mmean_ready mpow_done")
    (s.mdiag_ready, s.mrow_done, s.mrow_ready, s.late_in) = named(
        "mdiag_ready mrow_done mrow_ready late_in")
    (s.logit_done, s.logit_abs, s.soft_ready, s.b_ready) = named(
        "logit_done logit_abs soft_ready b_ready")
    (s.b_exped, s.qb_ready, s.kd_shift, s.kd_exped) = named(
        "b_exped qb_ready kd_shift kd_exped")
    (s.kd_ready, s.kd_turned, s.kd_copied, s.last_exped) = named(
        "kd_ready kd_turned kd_copied last_exped")
    (s.updates_done, s.states_ready, s.shifted, s.level_exped) = named(
        "updates_done states_ready shifted level_exped")
    (s.level_ready, s.level_done, s.level_taken, s.og_done) = named(
        "level_ready level_done level_taken og_done")
    (s.og_evac, s.og_squared, s.gcol_done, s.gmean_ready) = named(
        "og_evac og_squared gcol_done gmean_ready")
    (s.gpow_done, s.gdiag_ready, s.grow_done, s.og_normed) = named(
        "gpow_done gdiag_ready grow_done og_normed")
    (s.y_hi, s.y_ready, s.xq_hi, s.xq_ready) = named(
        "y_hi y_ready xq_hi xq_ready")
    (s.xscore_done, s.xneg) = named(
        "xscore_done xneg")
    (s.xexped, s.xblended, s.xturned, s.xturned_hi) = named(
        "xexped xblended xturned xturned_hi")
    (s.xturned_ready, s.xpv_done, s.ox_hi, s.ox_ready) = named(
        "xturned_ready xpv_done ox_hi ox_ready")
    (s.acted2, s.act2_hi, s.act2_ready, s.final_scaled) = named(
        "acted2 act2_hi act2_ready final_scaled")
    (s.mem_scaled, s.diag_a, s.silued) = named(
        "mem_scaled diag_a silued")
    s.a_cleared, s.ke_cleared, s.q_scaled, s.qk_product = named("a_cleared ke_cleared q_scaled qk_product")
    (s.xk_hi, s.xk_ready, s.xv_hi, s.xv_ready) = named(
        "xk_hi xk_ready xv_hi xv_ready")
    s.load = named(" ".join(f"load{n}" for n in range(RING)))
    s.x_in = named(" ".join(f"x_in{n}" for n in range(4)))
    return s


def build(nc, dram, out):
    s = semaphores(nc)
    b = place(nc)
    scratch = nc.dram_tensor("bias_lines", (12, P * LINE), F32).ap()
    with nc.Block() as block:
        @block.sync
        def _(sp):
            sync_program(nc, sp, s, b, dram, scratch, out)

        @block.scalar
        def _(act):
            scalar_program(nc, act, s, b, dram, scratch)

        @block.vector
        def _(dve):
            vector_program(nc, dve, s, b)

        @block.gpsimd
        def _(pool):
            gpsimd_program(nc, pool, s, b)

        @block.tensor
        def _(pe):
            tensor_program(nc, pe, s, b)


KB = 1024


def place(nc):
    b = Names()
    base = (nc.sbuf_base + 31) // 32 * 32

    def at(name, offset, shape, dt=F32):
        return nc.alloc_sbuf_tensor_at(name, [P] + shape, dt, offset=base + int(offset))

    off = [0]

    def nxt(name, shape, dt=F32):
        start = off[0]
        off[0] += (4 * int(np.prod(shape)) + 31) // 32 * 32
        return at(name, start, shape, dt)

    b.x = nxt("x", [KT, T])
    b.hh = nxt("hh", [KT, T], F32R)
    b.hl = nxt("hl", [KT, T], F32R)
    b.stage = nxt("stage", [RING, D])
    b.wh = nxt("wh", [RING, D], F32R)
    b.wl = nxt("wl", [RING, D], F32R)
    b.rrow = nxt("rrow", [T])
    b.sumsq = nxt("sumsq", [T])
    b.tmp = nxt("tmp", [2, T])
    b.diag = nxt("diag", [2, T])
    b.consts = nxt("consts", [2, P])
    b.vec = nxt("vec", [NVEC])
    b.half_bg = nxt("half_bg", [24])
    b.gg = nxt("gg", [8])
    b.small = nxt("small", [96])
    b.mx = nxt("mx", [8])
    b.neg = nxt("neg", [8])
    b.sums = nxt("sums", [8])
    b.rec = nxt("rec", [8])
    b.turn = nxt("turn", [8])
    b.small2 = nxt("small2", [64])
    r0 = off[0]
    R = lambda kb: r0 + kb * KB
    b.qk = at("qk", R(0), [8, T])
    b.v = at("v", R(16), [TT, 512])
    b.qh = at("qh", R(24), [T], F32R)
    b.ql = at("ql", R(26), [T], F32R)
    b.kh = at("kh", R(28), [T], F32R)
    b.kl = at("kl", R(30), [T], F32R)
    b.vh = at("vh", R(32), [TT, P], F32R)
    b.vl = at("vl", R(34), [TT, P], F32R)
    b.s = at("s", R(36), [2, SCORES])
    b.th = at("th", R(46), [SCORES], F32R)
    b.tl = at("tl", R(51), [SCORES], F32R)
    b.ga = at("ga", R(56), [16, T])
    b.yab = at("yab", R(88), [4, T])
    b.o = at("o", R(96), [4, T])
    b.bias = at("bias", R(104), [T])
    b.lines = at("lines", R(24), [12, LINE])
    b.u = at("u", R(56), [2, T])
    b.va = at("va", R(60), [TT, 256])
    b.early = at("early", R(64), [D])
    b.ws = at("ws", R(68), [4, P])
    b.inv = at("inv", R(70), [2, T])
    b.xb = at("xb", R(74), [2, T + 16])
    b.s1 = at("s1", R(74) + 4 * 2 * (T + 16), [T + 16])
    b.s2 = at("s2", R(74) + 4 * 3 * (T + 16), [T + 16])
    b.poolw = at("poolw", R(74) + 4 * 4 * (T + 16), [2, 64])
    b.pool = at("pool", R(84), [2, T])
    b.onehot = at("onehot", R(96), [T])
    b.tables = at("tables", R(98), [12 * P])
    b.gatec = at("gatec", R(36), [8, T])
    b.osq = at("osq", R(52), [2, T])
    b.yabh = at("yabh", R(0), [4, T], F32R)
    b.yabl = at("yabl", R(8), [4, T], F32R)
    b.ych = at("ych", R(16), [4, T], F32R)
    b.ycl = at("ycl", R(24), [4, T], F32R)
    b.mh = at("mh", R(56), [8, T], F32R)
    b.ml = at("ml", R(72), [8, T], F32R)
    b.ah = at("ah", R(0), [FT1, T], F32R)
    b.al = at("al", R(44), [FT1, T], F32R)
    b.gb = at("gb", R(88), [2, T + 2])
    b.cb = at("cb", R(93), [2, T])
    b.sq2 = at("sq2", R(97), [2, T])
    b.sum2 = at("sum2", R(101), [T])
    b.bias2 = at("bias2", R(56), [2, T])
    b.mem = at("mem", R(60), [KT, M])
    b.oa = at("oa", R(60), [4, T])
    b.zg = at("zg", R(68), [4, T])
    b.rg = at("rg", R(76), [4, T])
    b.memh = at("memh", R(84), [KT, M], F32R)
    b.meml = at("meml", R(92), [KT, M], F32R)
    b.kx = at("kx", R(100), [KT, M])
    b.mrow = at("mrow", R(108), [M])
    b.msum = at("msum", R(109), [M])
    b.rowa = at("rowa", R(110), [T])
    b.vg = at("vg", R(0), [TT, 512])
    b.b = at("b", R(8), [2, T])
    b.reset = at("reset", R(12), [T])
    b.la = at("la", R(14), [2, T])
    b.qe = at("qe", R(36), [2, 2 * TT, 2, 64])
    b.a = at("a", R(18), [2, TT, 2, P])
    b.masks = at("masks", R(26), [len(LEVELS) + 1, P])
    b.gsq = at("gsq", 16 * KB, [4, T])
    parts = 16 * KB
    b.ke = at("ke", parts, [2, 2 * T])
    b.ee = at("ee", parts + 8 * KB, [2, 2 * T])
    b.states = at("states", parts + 16 * KB, [2, NC, P])
    b.qb = at("qb", parts + 24 * KB, [2, T])
    b.kdt = at("kdt", parts + 28 * KB, [2, TT, P])
    b.og = at("og", R(36), [4, T])
    b.vx = at("vx", R(44), [MT, D])
    b.glr = at("glr", R(52), [T])
    b.wgu = at("wgu", R(54), [256])
    b.yh2 = at("yh2", R(68), [KT, T], F32R)
    b.yl2 = at("yl2", R(84), [KT, T], F32R)
    b.qxh = at("qxh", R(0), [2, T], F32R)
    b.qxl = at("qxl", R(4), [2, T], F32R)
    b.kxh = at("kxh", R(8), [2, M], F32R)
    b.kxl = at("kxl", R(10), [2, M], F32R)
    b.vxh = at("vxh", R(12), [MT, 256], F32R)
    b.vxl = at("vxl", R(14), [MT, 256], F32R)
    b.xs = at("xs", R(16), [TT, M])
    b.xth = at("xth", R(20), [MT, T], F32R)
    b.xtl = at("xtl", R(24), [MT, T], F32R)
    b.oxh = at("oxh", R(28), [KT, T], F32R)
    b.oxl = at("oxl", R(52), [KT, T], F32R)
    b.ah2 = at("ah2", R(0), [FH, T], F32R)
    b.al2 = at("al2", R(32), [FH, T], F32R)
    b.ps = nc.alloc_psum_tensor("ps", [P, 8, 512], F32)
    b.ident = b.consts[:, 0, :]
    b.ones = b.consts[:, 1, :]
    sm = b.small
    b.mean = sm[:, 0:4]
    b.rs = sm[:, 4:8]
    b.expo = sm[:, 8:24]
    b.omean = sm[:, 24:40]
    b.ors = sm[:, 40:56]
    b.ln_stats = sm[:, 56:80]
    b.ln_mv = sm[:, 80:88]
    b.lam_e = sm[:, 88:90]
    b.nlam = sm[:, 90:91]
    b.lam_d = sm[:, 92:94]
    b.subln = sm[:, 94:95]
    b.ln_rs = b.omean[:, 0:4]
    b.ln_var = b.omean[:, 4:8]
    b.rsa = b.small2[:, 0:4]
    b.sq_a = b.small2[:, 4:8]
    b.mmean = b.small2[:, 8:10]
    b.mrs = b.small2[:, 10:12]
    b.half_gn = b.small2[:, 12:13]
    b.ebl = b.small2[:, 16:16 + 2 * NC]
    b.gmean = b.small2[:, 32:48]
    b.grs = b.small2[:, 48:64]
    return b


def f32(ap):
    return ap.bitcast(F32)


def col(b, name, k):
    at = VEC[name]
    return b.vec[:, bass.ds(at + k, 1)] if not isinstance(k, int) else b.vec[:, at + k:at + k + 1]


def sync_program(nc, sp, s, b, dram, scratch, out):
    stream = dram["stream"]
    n = stream.shape[0]
    for p in range(RING):
        sp.dma_start(b.stage[:, p, :], stream[p]).then_inc(s.load[p], 16)
    sp.dma_start(b.consts[:], dram["consts"]).then_inc(s.consts_in, 16)
    sp.dma_start(b.early[:], dram["early"]).then_inc(s.early_in, 16)
    sp.dma_start(b.ws[:], dram["sgu_w"]).then_inc(s.early_in, 16)
    sp.dma_start(b.inv[:], dram["inv_count"]).then_inc(s.early_in, 16)
    sp.dma_start(b.poolw[:], dram["pool_w"]).then_inc(s.early_in, 16)
    sp.dma_start(b.onehot[0:NB, :], dram["onehot"]).then_inc(s.line_in, 16)
    sp.dma_start(b.tables[0:NB, :], dram["tables"]).then_inc(s.line_in, 16)
    with sp.Fori(1, n // RING) as g:
        for u in range(RING):
            sp.wait_ge(s.lo_ready, RING * g + u - RING + 1)
            sp.dma_start(b.stage[:, u, :], stream[RING * g + u]).then_inc(s.load[u], 16)
    for p in range(n // RING * RING, n):
        sp.wait_ge(s.lo_ready, p - RING + 1)
        sp.dma_start(b.stage[:, p % RING, :], stream[p]).then_inc(s.load[p % RING], 16)
    for k in range(KT):
        sp.wait_ge(s.final_scaled, k + 1)
        sp.dma_start(out[P * k:P * k + P, :], b.x[:, k, :]).then_inc(s.out_done, 16)
    sp.wait_ge(s.out_done, 16 * KT)


def scalar_program(nc, act, s, b, dram, scratch):
    A = nc.scalar.activation

    def AR(*args, **kw):
        act.wait_ge(s.vec_in, 16)
        return A(*args, **kw)

    act.dma_start(b.vec[:], dram["vec"]).then_inc(s.vec_in, 16)
    for c in range(4):
        act.dma_start(b.x[:, 2 * c:2 * c + 2, :], dram["x"][:, 2 * c:2 * c + 2, :]).then_inc(s.x_in[c], 16)

    def hi(p):
        if isinstance(p.index, int) and p.index >= P_END:
            return
        act.wait_ge(s.load[p.slot], 16 * p.round)
        if p.first >= RING:
            act.wait_ge(s.panel_done, p.index - RING + 1)
        A(b.wh[:, p.slot, :], b.stage[:, p.slot, :], ACT.Copy).then_inc(s.hi_ready, 1)

    def x_parts(k, name, evac, sums=None):
        if sums is not None:
            act.wait_ge(s.sums, sums)
        if evac is not None:
            act.wait_ge(s.evac, evac + 1)
        AR(b.hh[:, k, :], b.x[:, k, :], ACT.Copy, scale=col(b, name, k)).then_inc(s.x_hi, 1)

    def x_square(k, half):
        AR(b.tmp[:, half, :], b.x[:, k, :], ACT.Square).then_inc(s.x_squared, 1)

    def row(n):
        act.wait_ge(s.row_done, n)
        A(b.rrow[:], b.ps[:, 7, :], ACT.Copy).then_inc(s.row_ready, 1)

    act.wait_ge(s.steps, 1)
    A(b.mx[:, 0:1], b.expo[:, 0:1], ACT.Copy)
    hi(Panel(0))
    act.wait_ge(s.vec_in, 16)
    for k in range(KT):
        if k % 2 == 0:
            act.wait_ge(s.x_in[k // 2], 16)
        x_parts(k, "attn_norm_g", None)
        if k in (1, 3, 5):
            hi(Panel((k + 1) // 2))
    for k in range(KT):
        if k >= 2:
            act.wait_ge(s.sums, k)
        x_square(k, k % 2)

    hi(Panel(P_U + RING))
    row(1)
    act.wait_ge(s.evac, E_U + 1)
    A(b.u[:, 0, :], b.u[:, 0, :], ACT.Gelu).then_inc(s.u_ready, 1)
    hi(Panel(P_U + 1 + RING))
    act.wait_ge(s.evac, E_U + 2)
    A(b.u[:, 1, :], b.u[:, 1, :], ACT.Gelu).then_inc(s.u_ready, 1)
    hi(Panel(P_VA + RING))
    hi(Panel(P_VA + 1 + RING))
    act.wait_ge(s.evac, E_VA + 2)
    A(b.va[:], b.va[:], ACT.Gelu).then_inc(s.va_gelu, 1)
    hi(Panel(P_POOL + RING))
    for h in range(12):
        act.wait_ge(s.line_done, h + 1)
        A(b.lines[:, h, 0:T], b.ps[:, 4 + h % 2, :], ACT.Copy).then_inc(s.line_copied, 1)
    act.wait_ge(s.lines_set, 1)
    act.wait_ge(s.line_copied, 12)
    act.dma_start(scratch.rearrange("h (p j) -> p h j", p=P), b.lines[:]).then_inc(s.lines_out, 16)
    hi(Panel(P_POOL + 1 + RING))
    act.wait_ge(s.lam_dots, 1)
    A(b.lam_e, b.lam_d, ACT.Exp).then_inc(s.lam_exps, 1)

    with act.Fori(0, 2) as i:
        for u in range(RING):
            hi(Panel(P_Q + u + RING, RING, i))
    for u in range(4):
        hi(Panel(P_V + u + RING))

    act.wait_ge(s.lines_out, 16)

    def gate(g, half, dst, evac):
        act.wait_ge(s.evac, evac + 1)
        bias = b.half_bg[:, g:g + 1] if isinstance(g, int) else b.half_bg[:, bass.ds(g, 1)]
        AR(dst, b.tmp[:, half, :], ACT.Tanh, bias=bias, scale=0.5).then_inc(s.gated, 1)

    with act.Fori(0, 4) as i:
        act.dma_start(b.bias[:], bias_tile(scratch, i)).then_inc(s.bias_in, 16)
        act.wait_ge(s.evac, E_K + 4)
        AR(b.qh[:], b.qk[:, i, :], ACT.Copy, scale=0.125).then_inc(s.qk_hi, 1)
        AR(b.kh[:], b.qk[:, 4 + i, :], ACT.Copy).then_inc(s.qk_hi, 1)
        act.wait_ge(s.evac, E_V + 4)
        AR(b.vh[:], b.v[:, :, bass.ds(P * i, P)], ACT.Copy).then_inc(s.v_hi, 1)
        for u in range(4):
            hi(Panel(P_GATE + u + RING, RING, i))
            if u != 2:
                gate(4 * i + u, u % 2, b.ga[:, 4 * i + u, :], E_GATE + 4 * i + u)
            if u < 2:
                act.wait_ge(s.negated, 2 * i + u + 1)
                for qb in range(TT):
                    n = 4 * u + qb
                    sc = b.s[:, u, pairs_offset(qb):pairs_offset(qb + 1)]
                    A(sc, sc, ACT.Exp, bias=b.neg[:, n:n + 1], accum_out=b.sums[:, n:n + 1]).then_inc(s.exped, 1)
            if u == 2:
                for kb in range(TT):
                    if kb == 2:
                        gate(4 * i + u, u % 2, b.ga[:, 4 * i + u, :], E_GATE + 4 * i + u)
                    act.wait_ge(s.turned, 4 * i + kb + 1)
                    w = (TT - kb) * P
                    A(b.th[:, turned_offset(kb):turned_offset(kb) + w], b.ps[:, 5 + kb % 2, 0:w],
                      ACT.Copy).then_inc(s.turned_hi, 1)
        act.wait_ge(s.scored, 8 * i + 8)
        act.wait_ge(s.score_done, 8 * i + 8)
        act.wait_ge(s.pv_done, i + 1)

    def square_head(h):
        act.wait_ge(s.o_evac, h + 1)
        if h >= 2:
            act.wait_ge(s.ocol_done, h - 1)
        A(b.osq[:, h % 2, :], b.o[:, h, :], ACT.Square).then_inc(s.o_squared, 1)

    act.wait_ge(s.pv_done, 4)
    for h in range(4):
        square_head(h)
    for u in range(8):
        hi(Panel(P_GATE + 16 + u + RING))
        gate(16 + u, u % 2, b.gatec[:, u, :], E_GATE + 16 + u)
        if u == 1:
            for k in range(4):
                act.wait_ge(s.yab_written, k + 1)
                A(b.yabh[:, k, :], b.yab[:, k, :], ACT.Copy).then_inc(s.yab_hi, 1)
        if 3 <= u < 7:
            h = u - 3
            act.wait_ge(s.o_normed, h + 1)
            A(b.ych[:, h, :], b.o[:, h, :], ACT.Copy, scale=b.subln).then_inc(s.yc_hi, 1)

    with act.Fori(0, 2) as i:
        for u in range(4):
            hi(Panel(P_PROJ + u + RING, RING, i))
            act.wait_ge(s.m_summed, 4 * i + u + 1)
            AR(b.mh[:, 4 * i + u, :], b.tmp[:, 0, :], ACT.Copy, scale=0.5).then_inc(s.m_hi, 1)

    def residual_loop(p0, e0, name, norm):
        act.wait_ge(s.sums, 9 * norm + 1)
        with act.Fori(0, 2) as i:
            for u in range(4):
                hi(Panel(p0 + u + RING, RING, i))
                x_parts(4 * i + u, name, e0 + 4 * i + u, 9 * norm + 4 * i + u)
                x_square(4 * i + u, u % 2)

    residual_loop(P_WOUT, E_WOUT, "ffn_norm_g", 1)

    def up_body(i, first):
        for a in range(2):
            j = 2 * i + a
            hi(Panel(P_UP + 2 * a + RING, RING, i))
            if first and a == 0:
                row(2)
            act.wait_ge(s.evac, E_UP + 4 * i + 2 * a + 1)
            AR(b.cb[:, a, :], b.gb[:, a, 2:], ACT.Identity, bias=col(b, "conv_b", j),
              scale=col(b, "conv2", j)).then_inc(s.tapped, 1)
            act.wait_ge(s.conved, j + 1)
            A(b.cb[:, a, :], b.cb[:, a, :], ACT.Gelu).then_inc(s.gelued, 1)
            hi(Panel(P_UP + 2 * a + 1 + RING, RING, i))
            act.wait_ge(s.acted, j + 1)
            AR(b.ah[:, j, :], b.tmp[:, a, :], ACT.Copy).then_inc(s.act_hi, 1)

    up_body(0, True)
    with act.Fori(1, FT1 // 2) as i:
        up_body(i, False)

    act.wait_ge(s.sums, 19)
    with act.Fori(0, 2) as i:
        for c in range(4):
            k = 4 * i + c
            for m in range(3):
                p = Panel(P_DOWN + 3 * c + m + RING, 12, i)
                hi(p)
            act.wait_ge(s.sums, 18 + k)
            act.wait_ge(s.sums2, 1 + k)
            act.wait_ge(s.evac, E_DOWN + k + 1)
            AR(b.hh[:, k, :], b.x[:, k, :], ACT.Copy, scale=b.gg[:, bass.ds(k, 1)]).then_inc(s.x_hi, 1)
            x_square(k, c % 2)
            AR(b.sq2[:, c % 2, :], b.x[:, k, :], ACT.Square,
              scale=col(b, "final_norm_g", k)).then_inc(s.x_second, 1)

    block2_scalar(nc, act, s, b, dram, scratch, A, AR, hi, row, x_parts, x_square, residual_loop)


def bias_tile(scratch, h):
    row = scratch[h, P - 1:P - 1 + (LINE - 1) * P]
    return row.rearrange("(p j) -> p j", p=P)[:, 0:T]


def bias_tiles(scratch, h):
    rows = scratch[bass.ds(h, 2), P - 1:P - 1 + (LINE - 1) * P]
    return rows.rearrange("h (p j) -> p h j", p=P)[:, :, 0:T]


def vector_program(nc, dve, s, b):
    V = nc.vector
    st = Steps(dve, s.steps)

    def bank(e):
        return b.ps[:, e % 4, :]

    def lo(p):
        if isinstance(p.index, int) and p.index >= P_END:
            return
        dve.wait_ge(s.hi_ready, p.index + 1)
        V.tensor_tensor(b.wl[:, p.slot, :], b.stage[:, p.slot, :], f32(b.wh[:, p.slot, :]),
                        ALU.subtract).then_inc(s.lo_ready, 1)

    def evac_row(p, e, dst, slot):
        dve.wait_ge(s.panel_done, p.index + 1)
        V.tensor_tensor(dst, b.ps[:, slot, :], b.rrow[:], ALU.mult).then_inc(s.evac, 1)

    def x_rest(k, name, count):
        dve.wait_ge(s.x_hi, count)
        scale = b.gg[:, bass.ds(k, 1)] if name == "gg" else col(b, name, k)
        V.scalar_tensor_tensor(b.hl[:, k, :], b.x[:, k, :], scale, f32(b.hh[:, k, :]),
                               ALU.mult, ALU.subtract).then_inc(s.h_ready, 1)

    def x_sum(half, count, sums):
        dve.wait_ge(s.x_squared, count)
        dve.wait_ge(s.sums, sums)
        V.tensor_tensor(b.sumsq[:], b.sumsq[:], b.tmp[:, half, :], ALU.add).then_inc(s.sums, 1)

    def mean(n, width=D, eps=1e-6):
        dve.wait_ge(s.col_done, n)
        V.tensor_scalar(b.mean, b.ps[:, 7, 0:4], 1.0 / width, eps, ALU.mult, ALU.add).then_inc(s.mean_ready, 1)

    def diagonal(dst, r):
        return V.tensor_tensor(dst.rearrange("p (a q) -> p a q", a=TT),
                               b.ident.unsqueeze(1).to_broadcast([P, TT, P]),
                               r.unsqueeze(2).to_broadcast([P, TT, P]), ALU.mult)

    st.mark(V.memset(b.expo, -0.5))
    V.memset(b.sumsq[:], 0.0).then_inc(s.sums, 1)
    for buf in (b.xb[:, 0, 0:16], b.xb[:, 1, 0:16], b.s1[:, 0:16], b.s2[:, 0:16]):
        st.mark(V.memset(buf, 0.0))
    lo(Panel(0))
    dve.wait_ge(s.vec_in, 16)
    for k in range(KT):
        if k % 2 == 0:
            dve.wait_ge(s.x_in[k // 2], 16)
        x_rest(k, "attn_norm_g", k + 1)
        if k in (1, 3, 5):
            lo(Panel((k + 1) // 2))
    for k in range(KT):
        x_sum(k % 2, k + 1, k + 1)
    st.mark(V.tensor_scalar(b.half_bg[:], b.vec[:, VEC["b_gate"]:VEC["b_gate"] + 24], 0.5, None, ALU.mult))
    st.mark(V.tensor_scalar(b.subln, col(b, "subln", 0), 1.0 - LAM_INIT, None, ALU.mult))
    st.mark(V.tensor_tensor(b.gg[:], b.vec[:, VEC["final_norm_g"]:VEC["final_norm_g"] + 8],
                            b.vec[:, VEC["norm_mix"]:VEC["norm_mix"] + 8], ALU.mult))
    dve.wait_ge(s.early_in, 64)
    lam = b.early[:, 768:1024].rearrange("p (a c d) -> p a c d", a=2, c=2)
    prod = b.tmp[:, 0, 0:128].rearrange("p (a d) -> p a d", a=2)
    st.link(V.tensor_tensor(prod, lam[:, :, 0, :], lam[:, :, 1, :], ALU.mult))
    V.tensor_reduce(b.lam_d, prod, AX_X, ALU.add).then_inc(s.lam_dots, 1)
    dve.wait_ge(s.consts_in, 16)

    mean(1)
    dve.wait_ge(s.pow_done, 1)
    diagonal(b.diag[:, 0, :], b.rs).then_inc(s.diag_ready, 1)
    dve.wait_ge(s.row_ready, 1)
    evac_row(Panel(P_U), E_U, b.u[:, 0, :], 0)
    lo(Panel(P_U + RING))
    evac_row(Panel(P_U + 1), E_U + 1, b.u[:, 1, :], 1)
    lo(Panel(P_U + 1 + RING))
    lo(Panel(P_VA + RING))
    dve.wait_ge(s.panel_done, P_VA + 2)
    for t in range(TT):
        ins = V.tensor_scalar(b.va[:, t, :], b.ps[:, 2 + t // 2, 256 * (t % 2):256 * (t % 2) + 256],
                              b.rs[:, t:t + 1], None, ALU.mult)
        if t % 2:
            ins.then_inc(s.evac, 1)
    lo(Panel(P_VA + 1 + RING))
    evac_row(Panel(P_POOL), E_POOL, b.xb[:, 0, 16:], 0)
    lo(Panel(P_POOL + RING))
    dve.wait_ge(s.va_gelu, 1)
    for t in range(TT):
        st.link(V.bn_stats(b.ln_stats[:, 6 * t:6 * t + 6], b.va[:, t, :]))
        st.link(V.bn_aggr(b.ln_mv[:, 2 * t:2 * t + 2], b.ln_stats[:, 6 * t:6 * t + 6]))
    var = b.ln_mv.rearrange("p (t c) -> p t c", c=2)
    V.tensor_scalar(b.ln_var, var[:, :, 1], 1e-5, None, ALU.add).then_inc(s.ln_mean, 1)
    evac_row(Panel(P_POOL + 1), E_POOL + 1, b.xb[:, 1, 16:], 1)
    lo(Panel(P_POOL + 1 + RING))
    dve.wait_ge(s.ln_pow, 1)
    for t in range(TT):
        st.mark(V.tensor_scalar(b.va[:, t, :], b.va[:, t, :], b.ln_mv[:, 2 * t:2 * t + 1], b.ln_rs[:, t:t + 1],
                                ALU.subtract, ALU.mult))
    st.wait()
    st.link(V.tensor_tensor(b.va[:], b.va[:], b.early[:, 256:512].unsqueeze(1).to_broadcast([P, TT, 256]),
                            ALU.mult))
    V.tensor_tensor(b.va[:], b.va[:], b.early[:, 512:768].unsqueeze(1).to_broadcast([P, TT, 256]),
                    ALU.add).then_inc(s.v_normed, 1)

    def wsum(dst, src, shift, parts):
        st.link(V.tensor_tensor(dst[parts, 16:], src[parts, 16:], src[parts, 16 - shift:16 + T - shift], ALU.add))

    every, high, low = slice(0, P), slice(64, P), slice(0, 64)
    x0, x1 = b.xb[:, 0, :], b.xb[:, 1, :]
    dve.wait_ge(s.evac, E_POOL + 2)
    wsum(b.s1, x0, 1, every)
    wsum(b.s2, b.s1, 2, high)
    for parts, src in ((low, b.s1), (high, b.s2)):
        st.mark(V.tensor_tensor(b.pool[parts, 0, :], src[parts, 16:], b.inv[parts, 0, :], ALU.mult))
    st.wait()
    V.tensor_tensor(b.pool[:, 0, :], b.pool[:, 0, :], x0[:, 16:], ALU.subtract).then_inc(s.pooled, 1)
    wsum(b.s1, x1, 1, every)
    wsum(b.s2, b.s1, 2, every)
    wsum(b.s1, b.s2, 4, every)
    wsum(b.s2, b.s1, 8, high)
    for parts, src in ((low, b.s1), (high, b.s2)):
        st.mark(V.tensor_tensor(b.pool[parts, 1, :], src[parts, 16:], b.inv[parts, 1, :], ALU.mult))
    st.wait()
    V.tensor_tensor(b.pool[:, 1, :], b.pool[:, 1, :], x1[:, 16:], ALU.subtract).then_inc(s.pooled, 1)

    dve.wait_ge(s.lam_exps, 1)
    st.link(V.tensor_tensor(b.nlam, b.lam_e[:, 1:2], b.lam_e[:, 0:1], ALU.subtract))
    st.link(V.tensor_scalar(b.nlam, b.nlam, -LAM_INIT, None, ALU.add))

    with dve.Fori(0, 2) as i:
        for u in range(RING):
            e = E_Q + u
            evac_row(Panel(P_Q + u, RING, i), e, b.qk[:, 4 * i + u, :], e % 4)
            lo(Panel(P_Q + u + RING, RING, i))

    for f in range(2):
        dve.wait_ge(s.spatial_done, f + 1)
        dve.wait_ge(s.u_ready, 2)
        y = b.yab[:, f, :]
        st.link(V.tensor_tensor(y.rearrange("p (c t) -> p c t", c=TT),
                                b.ps[:, 4 + f, :].rearrange("p (c t) -> p c t", c=TT),
                                b.early[:, P * f:P * f + P].unsqueeze(1).to_broadcast([P, TT, P]), ALU.add))
        V.tensor_tensor(y, y, b.u[:, f, :], ALU.mult).then_inc(s.yab_written, 1)
    for f in range(2):
        dve.wait_ge(s.poolmm_done, f + 1)
        V.tensor_scalar(b.yab[:, 2 + f, :], b.ps[:, 6 + f, :], col(b, "pool_scale", f), None,
                        ALU.mult).then_inc(s.yab_written, 1)

    for u in range(3):
        dve.wait_ge(s.panel_done, P_V + u + 1)
        lo(Panel(P_V + u + RING))
    for t in range(TT):
        if t < TT - 1:
            dve.wait_ge(s.v_done, t + 1)
        else:
            dve.wait_ge(s.panel_done, P_V + 4)
        V.tensor_scalar(b.v[:, t, :], bank(E_V + t), b.rs[:, t:t + 1], None, ALU.mult).then_inc(s.evac, 1)
    lo(Panel(P_V + 3 + RING))

    def gate(p, g, half, slot):
        if isinstance(g, int):
            if g >= 2:
                dve.wait_ge(s.gated, g - 1)
        evac_row(p, 0, b.tmp[:, half, :], slot)

    def score_rows(i, c, before, bias, blocks=range(TT)):
        for qb in blocks:
            n = 4 * c + qb
            w = P * (qb + 1)
            dve.wait_ge(s.score_done, 8 * i + 8 * before + n + 1)
            V.memset(b.turn[:, n:n + 1], 0.0)
            V.tensor_tensor_reduce(b.s[:, c, pairs_offset(qb):pairs_offset(qb + 1)],
                                   b.ps[:, 4 + n % 2, 0:w], bias[:, (TT - 1 - qb) * P:T], 1.0, -3.0e38,
                                   ALU.add, ALU.max, b.mx[:, n:n + 1]).then_inc(s.scored, 1)
        if TT - 1 not in blocks:
            return
        dve.wait_ge(s.scored, 8 * i + 8 * before + 4 * c + 4)
        V.tensor_scalar(b.neg[:, 4 * c:4 * c + 4], b.mx[:, 4 * c:4 * c + 4], -1.0, None,
                        ALU.mult).then_inc(s.negated, 1)

    HEAD_STEPS = 1 + 4 + 2
    with dve.Fori(0, 4) as i:
        st.enter(i, HEAD_STEPS)
        dve.wait_ge(s.qk_hi, 2 * i + 2)
        V.scalar_tensor_tensor(b.ql[:], b.qk[:, i, :], 0.125, f32(b.qh[:]), ALU.mult, ALU.subtract)
        V.tensor_tensor(b.kl[:], b.qk[:, 4 + i, :], f32(b.kh[:]), ALU.subtract).then_inc(s.qk_ready, 1)
        dve.wait_ge(s.v_hi, i + 1)
        V.tensor_tensor(b.vl[:], b.v[:, :, bass.ds(P * i, P)], f32(b.vh[:]), ALU.subtract).then_inc(s.v_ready, 1)
        for u in range(4):
            if u >= 2:
                dve.wait_ge(s.gated, 4 * i + u - 1)
            evac_row(Panel(P_GATE + u, RING, i), 0, b.tmp[:, u % 2, :], (E_GATE + u) % 4)
            if u == 0:
                dve.wait_ge(s.bias_in, 16 * i + 16)
                score_rows(i, 0, 0, b.bias, (0, 1))
            if u not in (1, 2):
                lo(Panel(P_GATE + u + RING, RING, i))
            if u == 0:
                score_rows(i, 0, 0, b.bias, (2, 3))
                score_rows(i, 1, 0, b.bias, (0, 1))
            if u == 1:
                score_rows(i, 1, 0, b.bias, (2, 3))
            if u == 1:
                dve.wait_ge(s.exped, 8 * i + 4)
                st.link(V.reciprocal(b.rec[:, 0:4], b.sums[:, 0:4]))
                for qb in range(TT):
                    sc = b.s[:, 0, pairs_offset(qb):pairs_offset(qb + 1)]
                    st.mark(V.tensor_scalar(sc, sc, b.rec[:, qb:qb + 1], None, ALU.mult))
                dve.wait_ge(s.exped, 8 * i + 8)
                st.link(V.reciprocal(b.rec[:, 4:8], b.sums[:, 4:8]))
                st.link(V.tensor_scalar(b.rec[:, 4:8], b.rec[:, 4:8], b.nlam, None, ALU.mult))
                for qb in range(TT):
                    c0 = b.s[:, 0, pairs_offset(qb):pairs_offset(qb + 1)]
                    c1 = b.s[:, 1, pairs_offset(qb):pairs_offset(qb + 1)]
                    V.scalar_tensor_tensor(c0, c1, b.rec[:, 4 + qb:5 + qb], c0, ALU.mult,
                                           ALU.add).then_inc(s.blended, 1)
                lo(Panel(P_GATE + u + RING, RING, i))
            if u == 2:
                for kb in range(TT):
                    if kb == 2:
                        lo(Panel(P_GATE + u + RING, RING, i))
                    w = (TT - kb) * P
                    at = turned_offset(kb)
                    dve.wait_ge(s.turned_hi, 4 * i + kb + 1)
                    V.tensor_tensor(b.tl[:, at:at + w], b.ps[:, 5 + kb % 2, 0:w], f32(b.th[:, at:at + w]),
                                    ALU.subtract).then_inc(s.turned_ready, 1)
        dve.wait_ge(s.pv_done, i + 1)
        V.tensor_copy(b.o[:, i, :], b.ps[:, 4, :]).then_inc(s.o_evac, 1)
        dve.wait_ge(s.gated, 4 * i + 4)
    st.leave(4)

    for u in range(8):
        gate(Panel(P_GATE + 16 + u), 16 + u, u % 2, (E_GATE + 16 + u) % 4)
        lo(Panel(P_GATE + 16 + u + RING))
        if u == 1:
            dve.wait_ge(s.ocol_done, 4)
            V.tensor_scalar(b.omean, b.ps[:, 7, 0:16], 1.0 / P, 1e-5, ALU.mult, ALU.add).then_inc(s.omean_ready, 1)
            for k in range(4):
                dve.wait_ge(s.yab_hi, k + 1)
                V.tensor_tensor(b.yabl[:, k, :], b.yab[:, k, :], f32(b.yabh[:, k, :]),
                                ALU.subtract).then_inc(s.yab_ready, 1)
        if 3 <= u < 7:
            h = u - 3
            dve.wait_ge(s.orow_done, h + 1)
            V.tensor_tensor(b.o[:, h, :], b.o[:, h, :], b.ps[:, 4 + h, :], ALU.mult).then_inc(s.o_normed, 1)
        if 2 <= u < 6:
            h = u - 2
            if h == 0:
                dve.wait_ge(s.opow_done, 1)
            if h >= 2:
                dve.wait_ge(s.orow_done, h - 1)
            diagonal(b.diag[:, h % 2, :], b.ors[:, 4 * h:4 * h + 4]).then_inc(s.odiag_ready, 1)
        if 3 <= u < 7:
            h = u - 3
            dve.wait_ge(s.yc_hi, h + 1)
            dve.wait_ge(s.o_normed, h + 1)
            V.scalar_tensor_tensor(b.ycl[:, h, :], b.o[:, h, :], b.subln, f32(b.ych[:, h, :]),
                                   ALU.mult, ALU.subtract).then_inc(s.yc_ready, 1)

    with dve.Fori(0, 2) as i:
        st.enter(i, 4)
        for u in range(4):
            j = 4 * i + u
            p = Panel(P_PROJ + u, RING, i)
            dve.wait_ge(s.gated, 24)
            dve.wait_ge(s.panel_done, p.index + 1)

            def branch(r, gates, dst):
                V.scalar_tensor_tensor(dst, gates, 1.0, b.ps[:, 4 * (u % 2) + r, :], ALU.add,
                                       ALU.mult).then_inc(s.evac, 1)
            branch(0, b.ga[:, j, :], b.tmp[:, 0, :])
            branch(1, b.ga[:, 8 + j, :], b.tmp[:, 1, :])
            branch(2, b.gatec[:, j, :], b.sumsq[:])
            dve.wait_ge(s.evac, E_PROJ + 12 * i + 3 * u + 2)
            st.link(V.tensor_tensor(b.tmp[:, 0, :], b.tmp[:, 0, :], b.tmp[:, 1, :], ALU.add))
            dve.wait_ge(s.evac, E_PROJ + 12 * i + 3 * u + 3)
            V.tensor_tensor(b.tmp[:, 0, :], b.tmp[:, 0, :], b.sumsq[:], ALU.add).then_inc(s.m_summed, 1)
            lo(Panel(P_PROJ + u + RING, RING, i))
            dve.wait_ge(s.m_hi, j + 1)
            dve.wait_ge(s.m_summed, j + 1)
            V.scalar_tensor_tensor(b.ml[:, j, :], b.tmp[:, 0, :], 0.5, f32(b.mh[:, j, :]), ALU.mult,
                                   ALU.subtract).then_inc(s.m_ready, 1)
            dve.wait_ge(s.m_ready, j + 1)
    st.leave(2)

    def residual_loop(p0, e0, name, norm):
        V.memset(b.sumsq[:], 0.0).then_inc(s.sums, 1)
        with dve.Fori(0, 2) as i:
            for u in range(4):
                k = 4 * i + u
                p = Panel(p0 + u, RING, i)
                dve.wait_ge(s.panel_done, p.index + 1)
                V.tensor_tensor(b.x[:, k, :], b.x[:, k, :], b.ps[:, (e0 + u) % 4, :], ALU.add).then_inc(s.evac, 1)
                lo(p.plus(RING))
                dve.wait_ge(s.evac, e0 + k + 1)
                x_rest(k, name, 8 * norm + k + 1)
                x_sum(u % 2, 8 * norm + k + 1, 9 * norm + 1 + k)

    residual_loop(P_WOUT, E_WOUT, "ffn_norm_g", 1)

    for a in range(2):
        st.link(V.memset(b.gb[:, a, 0:2], 0.0))
    mean(2)
    dve.wait_ge(s.pow_done, 2)
    diagonal(b.diag[:, 0, :], b.rs).then_inc(s.diag_ready, 1)
    dve.wait_ge(s.row_ready, 2)
    with dve.Fori(0, FT1 // 2) as i:
        st.enter(i, 2)
        for a in range(2):
            j = 2 * i + a
            gate_p, up_p = Panel(P_UP + 2 * a, RING, i), Panel(P_UP + 2 * a + 1, RING, i)
            evac_row(gate_p, 0, b.gb[:, a, 2:], (E_UP + 2 * a) % 4)
            if a == 1:
                act_rest(nc, dve, s, b, 2 * i, 0)
            lo(gate_p.plus(RING))
            dve.wait_ge(s.tapped, j + 1)
            dve.wait_ge(s.evac, E_UP + 4 * i + 2 * a + 1)
            st.link(V.scalar_tensor_tensor(b.cb[:, a, :], b.gb[:, a, 1:T + 1], col(b, "conv1", j), b.cb[:, a, :],
                                           ALU.mult, ALU.add))
            V.scalar_tensor_tensor(b.cb[:, a, :], b.gb[:, a, 0:T], col(b, "conv0", j), b.cb[:, a, :],
                                   ALU.mult, ALU.add).then_inc(s.conved, 1)
            evac_row(up_p, 0, b.tmp[:, a, :], (E_UP + 2 * a + 1) % 4)
            lo(up_p.plus(RING))
            dve.wait_ge(s.gelued, j + 1)
            dve.wait_ge(s.evac, E_UP + 4 * i + 2 * a + 2)
            V.tensor_tensor(b.tmp[:, a, :], b.tmp[:, a, :], b.cb[:, a, :], ALU.mult).then_inc(s.acted, 1)
            if a == 1:
                act_rest(nc, dve, s, b, 2 * i + 1, 1)
    st.leave(FT1 // 2)

    V.memset(b.sumsq[:], 0.0).then_inc(s.sums, 1)
    V.memset(b.sum2[:], 0.0).then_inc(s.sums2, 1)
    with dve.Fori(0, 2) as i:
        for c in range(4):
            k = 4 * i + c
            for m in range(3):
                p = Panel(P_DOWN + 3 * c + m, 12, i)
                dve.wait_ge(s.panel_done, p.index + 1)
                if m == 2:
                    V.tensor_tensor(b.x[:, k, :], b.x[:, k, :], b.ps[:, (E_DOWN + c) % 4, :],
                                    ALU.add).then_inc(s.evac, 1)
                lo(p.plus(RING))
            dve.wait_ge(s.evac, E_DOWN + k + 1)
            x_rest(k, "gg", 16 + k + 1)
            x_sum(c % 2, 16 + k + 1, 18 + 1 + k)
            dve.wait_ge(s.x_second, k + 1)
            dve.wait_ge(s.sums2, k + 1)
            V.tensor_tensor(b.sum2[:], b.sum2[:], b.sq2[:, c % 2, :], ALU.add).then_inc(s.sums2, 1)

    block2_vector(nc, dve, s, b, st, lo, evac_row, mean, diagonal, x_rest, x_sum, residual_loop,
                  score_rows)


def act_rest(nc, dve, s, b, j, half):
    dve.wait_ge(s.act_hi, j + 1)
    dve.wait_ge(s.acted, j + 1)
    nc.vector.tensor_tensor(b.al[:, j, :], b.tmp[:, half, :], f32(b.ah[:, j, :]),
                            ALU.subtract).then_inc(s.act_ready, 1)


def gpsimd_program(nc, pool, s, b):
    G = nc.gpsimd
    G.memset(b.lines[:, :, T:LINE], NEG).then_inc(s.lines_set, 1)
    pool.wait_ge(s.early_in, 64)
    G.affine_select(out=b.ws[:], in_=b.ws[:], compare_op=ALU.is_ge, fill=0.0, base=0,
                    pattern=[[0, 4], [1, P]], channel_multiplier=-1).then_inc(s.ws_masked, 1)

    def power(n):
        pool.wait_ge(s.mean_ready, n)
        G.tensor_tensor(b.rs, b.mean, b.expo[:, 0:4], ALU.pow).then_inc(s.pow_done, 1)

    power(1)
    pool.wait_ge(s.ln_mean, 1)
    G.tensor_tensor(b.ln_rs, b.ln_var, b.expo[:, 0:4], ALU.pow).then_inc(s.ln_pow, 1)
    pool.wait_ge(s.omean_ready, 1)
    G.tensor_tensor(b.ors, b.omean, b.expo, ALU.pow).then_inc(s.opow_done, 1)
    power(2)
    pool.wait_ge(s.mean_ready, 3)
    G.tensor_tensor(b.rsa, b.mean, b.expo[:, 0:4], ALU.pow).then_inc(s.pow_a, 1)
    pool.wait_ge(s.mean_b, 1)
    G.tensor_tensor(b.rs, b.mean, b.expo[:, 0:4], ALU.pow).then_inc(s.pow_done, 1)
    pool.wait_ge(s.mmean_ready, 1)
    G.tensor_tensor(b.mrs, b.mmean, b.expo[:, 0:MT], ALU.pow).then_inc(s.mpow_done, 1)
    pool.wait_ge(s.pv_done, 12)
    pool.wait_ge(s.v_ready, 8)
    pool.wait_ge(s.turned_ready, 48)
    G.memset(b.qe[:], 0.0).then_inc(s.a_cleared, 1)
    G.memset(b.a[:], 0.0).then_inc(s.a_cleared, 1)
    pool.wait_ge(s.panel_done, P_VG + 4)
    G.memset(b.ke[:], 0.0).then_inc(s.ke_cleared, 1)
    for p in range(P_XV + RING, P_WOUT2 + RING):
        pool.wait_ge(s.hi_ready, p + 1)
        pool.wait_ge(s.lo_ready, p)
        G.tensor_tensor(b.wl[:, p % RING, :], b.stage[:, p % RING, :], f32(b.wh[:, p % RING, :]),
                        ALU.subtract).then_inc(s.lo_ready, 1)
    pool.wait_ge(s.gmean_ready, 1)
    G.tensor_tensor(b.grs, b.gmean, b.expo, ALU.pow).then_inc(s.gpow_done, 1)
    for n in (4, 5, 6):
        power(n)


def tensor_program(nc, pe, s, b):
    MM = nc.tensor.matmul

    def three(out, wh, wl, xh, xl, start, stop):
        MM(out, wh, xh, start=start, stop=False, skip_group_check=True)
        MM(out, wh, xl, start=False, stop=False, skip_group_check=True)
        return MM(out, wl, xh, start=False, stop=stop, skip_group_check=True)

    def begin(p, e):
        pe.wait_ge(s.lo_ready, p.index + 1)
        if e is not None:
            pe.wait_ge(s.evac, e - 3)

    def w(p, a, n=P):
        return b.wh[:, p.slot, a:a + n], b.wl[:, p.slot, a:a + n]

    def features(p, e, slot, xh=None, xl=None, tiles=range(KT), last=KT, width=T, ready=None, between=None):
        xh, xl = (b.hh, b.hl) if xh is None else (xh, xl)
        begin(p, e)
        for n, k in enumerate(tiles):
            for step in (between or {}).get(n, ()):
                step()
            if ready:
                ready(k)
            wh, wl = w(p, P * n)
            ins = three(b.ps[:, slot, 0:width], wh, wl, xh[:, k, 0:width], xl[:, k, 0:width], k == 0, k == last - 1)
        ins.then_inc(s.panel_done, 1)

    def column_sums(n, sums):
        pe.wait_ge(s.sums, sums)
        if n > 1:
            pe.wait_ge(s.row_ready, n - 1)
        for t in range(TT):
            ins = MM(b.ps[:, 7, t:t + 1], b.sumsq[:, P * t:P * t + P], b.ones[:, 0:1], start=True, stop=True)
        ins.then_inc(s.col_done, 1)

    def row(n):
        pe.wait_ge(s.diag_ready, n)
        MM(b.ps[:, 7, :], b.ones, b.diag[:, 0, :], start=True, stop=True).then_inc(s.row_done, 1)

    def x_ready(base):
        return lambda k: pe.wait_ge(s.h_ready, base + k + 1)

    features(Panel(P_U), None, 0, ready=x_ready(0))
    features(Panel(P_U + 1), None, 1)
    pe.wait_ge(s.consts_in, 16)
    column_sums(1, 9)
    for m in range(2):
        p = Panel(P_VA + m)
        begin(p, None)
        for k in range(4 * m, 4 * m + 4):
            if k == 3:
                row(1)
            wh, wl = w(p, 256 * (k - 4 * m), 256)
            for t in range(TT):
                tok = slice(P * t, P * t + P)
                ins = three(b.ps[:, 2 + t // 2, 256 * (t % 2):256 * (t % 2) + 256],
                            b.hh[:, k, tok], b.hl[:, k, tok], wh, wl, k == 0 and t % 2 == 0, k == KT - 1)
        ins.then_inc(s.panel_done, 1)
    for u in range(2):
        features(Panel(P_POOL + u), E_POOL + u, u)
    pe.wait_ge(s.line_in, 32)
    for h in range(12):
        if h >= 2:
            pe.wait_ge(s.line_copied, h - 1)
        MM(b.ps[:, 4 + h % 2, :], b.tables[0:NB, P * h:P * h + P], b.onehot[0:NB, :], start=True,
           stop=True).then_inc(s.line_done, 1)

    with pe.Fori(0, 2) as i:
        for u in range(RING):
            features(Panel(P_Q + u, RING, i), E_Q + u + RING * i, (E_Q + u) % 4)

    pe.wait_ge(s.v_normed, 1)
    pe.wait_ge(s.ws_masked, 1)
    pe.wait_ge(s.line_copied, 12)
    for f in range(2):
        for c in range(TT):
            for g in range(2):
                ins = MM(b.ps[64 * g:64 * g + 64, 4 + f, P * c:P * c + P],
                         b.va[:, c, 64 * (2 * f + g):64 * (2 * f + g) + 64], b.ws[:, 2 * f + g, :],
                         start=True, stop=True)
        ins.then_inc(s.spatial_done, 1)
    pe.wait_ge(s.pooled, 2)
    for g in range(2):
        part = slice(64 * g, 64 * g + 64)
        for f in range(2):
            ins = MM(b.ps[part, 6 + f, :], b.poolw[part, f, :], b.pool[part, f, :], start=True, stop=True)
            if g:
                ins.then_inc(s.poolmm_done, 1)

    def tokens(first, e0, done, wait_banks=True):
        for m in range(4):
            p = Panel(first + m)
            begin(p, None)
            for t in range(TT):
                if m == 0:
                    pe.wait_ge(s.evac, e0 + t - 3)
                for n in range(2):
                    k = 2 * m + n
                    wh, wl = w(p, 512 * n, 512)
                    tok = slice(P * t, P * t + P)
                    ins = three(b.ps[:, (e0 + t) % 4, :], b.hh[:, k, tok], b.hl[:, k, tok], wh, wl,
                                k == 0, k == KT - 1)
                if m == 3 and t < TT - 1:
                    ins.then_inc(done, 1)
            ins.then_inc(s.panel_done, 1)

    tokens(P_V, E_V, s.v_done)

    def score(i, n):
        part = slice(64 * (n // TT), 64 * (n // TT) + 64)
        qb = n % TT
        if n >= 2:
            pe.wait_ge(s.scored, 8 * i + n - 1)
        width = P * (qb + 1)
        tok = slice(P * qb, P * qb + P)
        three(b.ps[:, 4 + n % 2, 0:width], b.qh[part, tok], b.ql[part, tok], b.kh[part, 0:width],
              b.kl[part, 0:width], True, True).then_inc(s.score_done, 1)

    def turn(n, kb, c=0):
        if kb == 0:
            pe.wait_ge(s.blended, 4 * n + 4)
        if kb >= 2:
            pe.wait_ge(s.turned_ready, 4 * n + kb - 1)
        for qb in range(kb, TT):
            at = pairs_offset(qb) + P * kb
            ins = nc.tensor.transpose(b.ps[:, 5 + kb % 2, P * (qb - kb):P * (qb - kb) + P],
                                      b.s[:, c, at:at + P], b.ident)
        ins.then_inc(s.turned, 1)

    def values(n, pair, bank):
        pe.wait_ge(s.v_ready, pair + 1)
        for kb in range(TT):
            pe.wait_ge(s.turned_ready, 4 * n + kb + 1)
            at, width = turned_offset(kb), (TT - kb) * P
            ins = three(b.ps[:, bank, kb * P:T], b.vh[:, kb, :], b.vl[:, kb, :], b.th[:, at:at + width],
                        b.tl[:, at:at + width], kb == 0, kb == TT - 1)
        ins.then_inc(s.pv_done, 1)

    with pe.Fori(0, 4) as i:
        def sc(n):
            return lambda: score(i, n)

        def tn(kb):
            return lambda: turn(i, kb)

        between = {1: {1: [sc(2)], 2: [sc(3)], 4: [sc(4)], 5: [sc(5)], 6: [sc(6)], 7: [sc(7)]},
                   3: {3: [tn(0), tn(1)], 5: [tn(2)], 6: [tn(3)]}}
        for u in range(4):
            features(Panel(P_GATE + u, RING, i), E_GATE + u + RING * i, (E_GATE + u) % 4, between=between.get(u))
            if u == 0:
                pe.wait_ge(s.qk_ready, i + 1)
                pe.wait_ge(s.yab_written, 4)
                score(i, 0)
                score(i, 1)
        values(i, i, 4)

    for u in range(8):
        p = Panel(P_GATE + 16 + u)

        def head_row(h):
            pe.wait_ge(s.odiag_ready, h + 1)
            MM(b.ps[:, 4 + h, :], b.ones, b.diag[:, h % 2, :], start=True, stop=True).then_inc(s.orow_done, 1)

        features(p, E_GATE + 16 + u, (E_GATE + 16 + u) % 4,
                 between={5: [lambda: head_row(u - 3)]} if 3 <= u < 7 else None)
        if u < 2:
            for h in (2 * u, 2 * u + 1):
                pe.wait_ge(s.o_squared, h + 1)
                for t in range(TT):
                    ins = MM(b.ps[:, 7, 4 * h + t:4 * h + t + 1], b.osq[:, h % 2, P * t:P * t + P],
                             b.ones[:, 0:1], start=True, stop=True)
                ins.then_inc(s.ocol_done, 1)

    pe.wait_ge(s.yab_ready, 4)
    pe.wait_ge(s.yc_ready, 4)
    with pe.Fori(0, 2) as i:
        for u in range(4):
            p = Panel(P_PROJ + u, RING, i)
            begin(p, None)
            n = 0
            for r, (xh, xl, ks) in enumerate(((b.yabh, b.yabl, (0, 1)), (b.yabh, b.yabl, (2, 3)),
                                              (b.ych, b.ycl, (0, 1, 2, 3)))):
                if r == 0:
                    pe.wait_ge(s.evac, E_PROJ + 3 * (u - 1) + 12 * i if u else E_PROJ - 3 + 12 * i)
                    if u == 0:
                        pe.wait_ge(s.evac, E_PROJ)
                for k in ks:
                    wh, wl = w(p, P * n)
                    ins = three(b.ps[:, 4 * (u % 2) + r, :], wh, wl, xh[:, k, :], xl[:, k, :], k == ks[0],
                                k == ks[-1])
                    n += 1
            ins.then_inc(s.panel_done, 1)

    def four_chunks(p0, e0, xh, xl, ready, between):
        for half in range(2):
            for u in range(4):
                p = Panel(p0 + u)
                if half == 0:
                    begin(p, e0 + u)
                if (half, u) in between:
                    between[half, u]()
                for k in range(4 * half, 4 * half + 4):
                    if u == 0:
                        ready(k)
                    wh, wl = w(p, P * k)
                    ins = three(b.ps[:, (e0 + u) % 4, :], wh, wl, xh[:, k, :], xl[:, k, :], k == 0, k == KT - 1)
                if half:
                    ins.then_inc(s.panel_done, 1)

    def second_chunks(p0, e0, xh, xl):
        for u in range(4, 8):
            features(Panel(p0 + u), e0 + u, (e0 + u) % 4, xh=xh, xl=xl)

    four_chunks(P_WOUT, E_WOUT, b.mh, b.ml, lambda k: pe.wait_ge(s.m_ready, k + 1), {})
    second_chunks(P_WOUT, E_WOUT, b.mh, b.ml)

    def up(i, first):
        for u in range(4):
            features(Panel(P_UP + u, RING, i), E_UP + u + RING * i, (E_UP + u) % 4,
                     ready=x_ready(8) if first and u == 0 else None,
                     between={1: [lambda: row(2)]} if first and u == 2 else None)
            if first and u == 0:
                column_sums(2, 18)

    up(0, True)
    with pe.Fori(1, FT1 // 2) as i:
        up(i, False)

    with pe.Fori(0, 2) as i:
        for c in range(4):
            first = 0
            for m, n in enumerate(DOWN1):
                p = Panel(P_DOWN + 3 * c + m, 12, i)
                ready = (lambda k: pe.wait_ge(s.act_ready, k + 1)) if c == 0 else None
                features(p, E_DOWN + c + 4 * i if m == 0 else None, (E_DOWN + c) % 4, xh=b.ah, xl=b.al,
                         tiles=range(first, first + n), last=FT1, ready=ready)
                first += n

    block2_tensor(nc, pe, s, b, MM, three, begin, w, features, column_sums, row, x_ready, tokens, score, turn,
                  values, four_chunks, second_chunks)



def level_views(ap, size):
    v = ap.rearrange("p (n w) -> p n w", w=2 * size)
    return v, v[:, :, 0:size], v[:, :, size:2 * size]


def block2_scalar(nc, act, s, b, dram, scratch, A, AR, hi, row, x_parts, x_square, residual_loop):
    hi(Panel(P_QA + RING))
    act.dma_start(b.mem[:], dram["mem"]).then_inc(s.mem_in, 16)
    hi(Panel(P_QA + 1 + RING))
    row(3)
    act.wait_ge(s.rowa_done, 1)
    A(b.rowa[:], b.ps[:, 6, :], ACT.Copy).then_inc(s.rowa_ready, 1)
    hi(Panel(P_QA + 2 + RING))
    act.wait_ge(s.mem_in, 16)
    act.wait_ge(s.sums2, 9)
    A(b.kx[:], b.mem[:], ACT.Square).then_inc(s.mem_sq, 1)
    hi(Panel(P_QA + 3 + RING))
    act.wait_ge(s.mem_scaled, 1)
    A(b.memh[:], b.mem[:], ACT.Copy).then_inc(s.mem_hi, 1)
    for u in range(3):
        hi(Panel(P_KA + u + RING))
    act.wait_ge(s.mrow_done, 1)
    A(b.mrow[:], b.ps[:, 5, 0:M], ACT.Copy).then_inc(s.mrow_ready, 1)
    hi(Panel(P_KA + 3 + RING))
    for u in range(3):
        hi(Panel(P_VA2 + u + RING))

    def pair_parts(i):
        act.wait_ge(s.scored, 8 * i + 32)
        act.dma_start(b.bias2[:], bias_tiles(scratch, 4 + 2 * i)).then_inc(s.bias_in, 16)
        act.wait_ge(s.score_done, 8 * i + 32)
        act.wait_ge(s.evac, E_KA + 4)
        AR(b.qh[:], b.qk[:, i, :], ACT.Copy, scale=0.125).then_inc(s.qk_hi, 1)
        AR(b.kh[:], b.qk[:, 4 + i, :], ACT.Copy).then_inc(s.qk_hi, 1)

    def pair_body(i, last):
        def exps(c):
            act.wait_ge(s.negated, 2 * i + 8 + c + 1)
            for qb in range(TT):
                n = 4 * c + qb
                sc = b.s[:, c, pairs_offset(qb):pairs_offset(qb + 1)]
                A(sc, sc, ACT.Exp, bias=b.neg[:, n:n + 1], accum_out=b.sums[:, n:n + 1]).then_inc(s.exped, 1)

        def turned(c, blocks):
            act.wait_ge(s.pv_done, 2 * i + 4 + c)
            for kb in blocks:
                act.wait_ge(s.turned, 8 * i + 16 + 4 * c + kb + 1)
                w = (TT - kb) * P
                A(b.th[:, turned_offset(kb):turned_offset(kb) + w], b.ps[:, 5 + kb % 2, 0:w],
                  ACT.Copy).then_inc(s.turned_hi, 1)

        exps(0)
        act.wait_ge(s.evac, E_VA2 + 4)
        act.wait_ge(s.pv_done, 2 * i + 4)
        AR(b.vh[:], b.v[:, :, bass.ds(P * i, P)] if last is False else b.v[:, :, P * i:P * i + P],
           ACT.Copy).then_inc(s.v_hi, 1)
        exps(1)
        turned(0, (0, 1))
        hi(Panel(P_PAIRS + RING, RING, i))
        turned(0, (2, 3))
        hi(Panel(P_PAIRS + 1 + RING, RING, i))
        turned(1, (0, 1))
        act.wait_ge(s.silued, i + 1)
        act.wait_ge(s.evac, 4 * i + E_PAIRS + 2)
        AR(b.tmp[:, 0, :], b.rg[:, i, :], ACT.Tanh, scale=0.5).then_inc(s.gated, 1)
        turned(1, (2, 3))
        if not last:
            pair_parts(i + 1)
        hi(Panel(P_PAIRS + 2 + RING, RING, i))
        hi(Panel(P_PAIRS + 3 + RING, RING, i))

    pair_parts(0)
    hi(Panel(P_VA2 + 3 + RING))
    with act.Fori(0, 3) as i:
        pair_body(i, False)
    pair_body(3, True)

    act.wait_ge(s.score_done, 64)
    act.wait_ge(s.pv_done, 12)
    act.wait_ge(s.turned_ready, 48)
    act.dma_start(b.masks[:], dram["late"].rearrange("p (l q) -> p l q", q=P)).then_inc(s.late_in, 16)
    act.dma_start(b.wgu[0:16, :], dram["wgu"]).then_inc(s.late_in, 16)
    hi(Panel(P_GLR + RING))
    for r in range(2):
        act.wait_ge(s.logit_done, r + 1)
        A(b.la[:, r, :], b.ps[:, 6 + r, :], ACT.Abs, bias=col(b, "b_gate2", r)).then_inc(s.logit_abs, 1)
    act.wait_ge(s.logit_abs, 2)
    A(b.la[:], b.la[:], ACT.Exp, scale=-1.0).then_inc(s.act_steps, 1)
    act.wait_ge(s.act_steps, 1)
    A(b.la[:], b.la[:], ACT.Ln, bias=b.ones[:, 0:1]).then_inc(s.soft_ready, 1)
    hi(Panel(P_VG + RING))
    act.wait_ge(s.b_ready, 2)
    run = b.b[:].rearrange("p r t -> p (r t)")
    A(b.ebl, run[:, CHUNK - 1::CHUNK], ACT.Exp, scale=1.0 / 16).then_inc(s.last_exped, 1)
    hi(Panel(P_VG + 1 + RING))
    act.wait_ge(s.kd_shift, 1)
    A(b.diag[:], b.diag[:], ACT.Exp, scale=1.0 / 16).then_inc(s.kd_exped, 1)
    hi(Panel(P_VG + 2 + RING))
    hi(Panel(P_VG + 3 + RING))
    A(b.qb[:].rearrange("p r t -> p (r t)"), run, ACT.Exp, scale=1.0 / 16).then_inc(s.b_exped, 1)
    act.wait_ge(s.kd_turned, 1)
    A(b.kdt[:], b.ps[:, 4:6, :].rearrange("p r (t k) -> p r t k", t=TT), ACT.Copy).then_inc(s.kd_copied, 1)
    for n, size in enumerate(LEVELS):
        act.wait_ge(s.shifted, n + 1)
        _, first, second = level_views(b.ee[:, n % 2, :], size)
        A(second, second, ACT.Exp, scale=1.0 / 16).then_inc(s.level_exped, 1)
        A(first, first, ACT.Exp, scale=-1.0 / 16).then_inc(s.level_exped, 1)
        if n != 1:
            hi(Panel(P_XV + max(n - 1, 0) + RING))
    for m in (6, 7):
        hi(Panel(P_XV + m + RING))

    act.wait_ge(s.level_ready, len(LEVELS))
    act.wait_ge(s.o_evac, 12)
    for k in range(4):
        A(b.yh2[:, k, :], b.oa[:, k, :], ACT.Copy).then_inc(s.y_hi, 1)
    for n, h in enumerate(HEAD_ORDER):
        act.wait_ge(s.og_done, n + 1)
        A(b.gsq[:, h, :], b.ps[:, 4 + h, :], ACT.Square).then_inc(s.og_squared, 1)
    for h in range(4):
        act.wait_ge(s.og_normed, h + 1)
        A(b.yh2[:, 4 + h, :], b.og[:, h, :], ACT.Copy, scale=b.half_gn).then_inc(s.y_hi, 1)

    residual_loop(P_WOUT2, E_WOUT2, "norm_xattn", 3)

    def key_parts(h):
        if h:
            act.wait_ge(s.xscore_done, 4 * h)
        A(b.kxh[:], b.kx[:, 2 * h:2 * h + 2, :], ACT.Copy).then_inc(s.xk_hi, 1)

    def value_parts(h):
        if h:
            act.wait_ge(s.xpv_done, 2 * h)
        else:
            act.wait_ge(s.evac, E_XV + 4)
        A(b.vxh[:], b.vx[:, :, 256 * h:256 * h + 256], ACT.Copy).then_inc(s.xv_hi, 1)

    def xq(j):
        act.wait_ge(s.evac, E_XQ + j + 1)
        if j >= 2:
            act.wait_ge(s.xscore_done, 4 * (j // 2))
        A(b.qxh[:, j % 2, :], b.tmp[:, j % 2, :], ACT.Copy, scale=XSCALE).then_inc(s.xq_hi, 1)

    def exps(h):
        act.wait_ge(s.xneg, h + 1)
        if h:
            act.wait_ge(s.xturned, 2 * h)
        for qb in range(TT):
            A(b.xs[:, qb, :], b.ps[:, 4 + qb // 2, M * (qb % 2):M * (qb % 2) + M], ACT.Exp,
              bias=b.neg[:, qb:qb + 1], accum_out=b.sums[:, qb:qb + 1]).then_inc(s.xexped, 1)

    def turned_parts(h):
        if h:
            act.wait_ge(s.xpv_done, 2 * h)
        for mt in range(MT):
            act.wait_ge(s.xturned, 2 * h + mt + 1)
            A(b.xth[:, mt, :], b.ps[:, 6 + mt, :], ACT.Copy).then_inc(s.xturned_hi, 1)

    def out_parts(h):
        for d in range(2):
            act.wait_ge(s.xpv_done, 2 * h + d + 1)
            A(b.oxh[:, 2 * h + d, :], b.ps[:, 6 + d, :], ACT.Copy).then_inc(s.ox_hi, 1)

    act.wait_ge(s.panel_done, P_XQ + 1)
    for j in range(8):
        h = j // 2
        if j % 2 == 0 and h:
            if h >= 2:
                out_parts(h - 2)
            exps(h - 1)
            if h >= 2:
                value_parts(h - 1)
        if j % 2 and h:
            turned_parts(h - 1)
        hi(Panel(P_XQ + j + RING))
        if j == 0:
            row(4)
            key_parts(0)
            value_parts(0)
        elif j % 2 == 0:
            key_parts(h)
        xq(j)
    out_parts(2)
    exps(3)
    value_parts(3)
    turned_parts(3)
    out_parts(3)

    residual_loop(P_XO, E_XO, "norm_mlp", 4)

    def up_body(p0, i, first, base):
        for u in range(4):
            hi(Panel(p0 + u + RING, RING, i))
            if first and u == 0:
                row(5)
            act.wait_ge(s.acted2, base + 4 * i + u + 1)
            AR(b.ah2[:, 4 * i + u, :], b.tmp[:, u % 2, :], ACT.Copy).then_inc(s.act2_hi, 1)

    def down_loop(p0, e0, last):
        if last:
            act.wait_ge(s.sums, 46)
        def body(i):
            for c in range(4):
                k = 4 * i + c
                for m in range(2):
                    hi(Panel(p0 + 2 * c + m + RING, 8, i))
                if last:
                    act.wait_ge(s.sums, 45 + k)
                    act.wait_ge(s.evac, e0 + k + 1)
                    x_square(k, c % 2)

        if last:
            body(0)
            body(1)
        else:
            with act.Fori(0, 2) as i:
                body(i)

    up_body(P_UP_A, 0, True, 0)
    with act.Fori(1, FH // 4) as i:
        up_body(P_UP_A, i, False, 0)
    down_loop(P_DOWN_A, E_DOWN_A, False)
    with act.Fori(0, FH // 4) as i:
        up_body(P_UP_B, i, False, FH)
    down_loop(P_DOWN_B, E_DOWN_B, True)


def block2_vector(nc, dve, s, b, st, lo, evac_row, mean, diagonal, x_rest, x_sum, residual_loop, score_rows):
    V = nc.vector

    def bank(e):
        return b.ps[:, e % 4, :]

    def evac_tokens(first, e0, base, dst, beside=()):
        for u in range(3):
            dve.wait_ge(s.panel_done, first + u + 1)
            lo(Panel(first + u + RING))
            if beside:
                beside[u]()
        for t in range(TT):
            if t < TT - 1:
                dve.wait_ge(s.v_done, base + t + 1)
            else:
                dve.wait_ge(s.panel_done, first + 4)
            V.tensor_scalar(dst[:, t, :], bank(e0 + t), b.rs[:, t:t + 1], None, ALU.mult).then_inc(s.evac, 1)

    mean(3)
    V.tensor_scalar(b.sq_a, b.ps[:, 7, 4:8], 1.0 / D, None, ALU.mult).then_inc(s.steps, 1)
    st.n += 1
    lo(Panel(P_QA + RING))
    dve.wait_ge(s.pow_a, 1)
    st.wait()
    st.link(V.tensor_tensor(b.mean, b.rsa, b.sq_a, ALU.mult))
    st.link(V.tensor_tensor(b.mean, b.mean, b.rsa, ALU.mult))
    V.tensor_scalar(b.mean, b.mean, 1e-6, None, ALU.add).then_inc(s.mean_b, 1)
    diagonal(b.diag[:, 1, :], b.rsa).then_inc(s.diag_a, 1)
    dve.wait_ge(s.pow_done, 3)
    st.link(V.tensor_tensor(b.rs, b.rs, b.rsa, ALU.mult))
    diagonal(b.diag[:, 0, :], b.rs).then_inc(s.diag_ready, 1)
    lo(Panel(P_QA + 1 + RING))
    dve.wait_ge(s.row_ready, 3)
    for u in range(8):
        evac_row(Panel(P_QA + u), 0, b.qk[:, u, :], (E_QA + u) % 4)
        if u >= 2:
            lo(Panel(P_QA + u + RING))
        if u == 3:
            dve.wait_ge(s.mem_sq, 1)
            V.tensor_reduce(b.msum[:], b.kx[:].rearrange("p k m -> p m k"), AX_X, ALU.add).then_inc(s.mem_sums, 1)
            g = b.vec[:, VEC["norm_mem"]:VEC["norm_mem"] + KT]
            V.tensor_tensor(b.mem[:], b.mem[:], g.unsqueeze(2).to_broadcast([P, KT, M]),
                            ALU.mult).then_inc(s.mem_scaled, 1)
        if u == 5:
            dve.wait_ge(s.mcol_done, 1)
            V.tensor_scalar(b.mmean, b.ps[:, 5, 0:MT], 1.0 / D, 1e-6, ALU.mult, ALU.add).then_inc(s.mmean_ready, 1)
            dve.wait_ge(s.mem_hi, 1)
            dve.wait_ge(s.mem_scaled, 1)
            V.tensor_tensor(b.meml[:], b.mem[:], f32(b.memh[:]), ALU.subtract).then_inc(s.mem_ready, 1)
            dve.wait_ge(s.mpow_done, 1)
            dve.wait_ge(s.rowa_done, 1)
            V.tensor_tensor(b.diag[:, 1, 0:M].rearrange("p (a q) -> p a q", a=MT),
                            b.ident.unsqueeze(1).to_broadcast([P, MT, P]),
                            b.mrs.unsqueeze(2).to_broadcast([P, MT, P]), ALU.mult).then_inc(s.mdiag_ready, 1)
    V.tensor_scalar(b.half_gn, col(b, "g_norm", 0), 0.5, None, ALU.mult).then_inc(s.silued, 1)

    PAIR_STEPS = 2

    def pair_parts(i):
        dve.wait_ge(s.qk_hi, 2 * i + 10)
        V.scalar_tensor_tensor(b.ql[:], b.qk[:, i, :], 0.125, f32(b.qh[:]), ALU.mult, ALU.subtract)
        V.tensor_tensor(b.kl[:], b.qk[:, 4 + i, :], f32(b.kh[:]), ALU.subtract).then_inc(s.qk_ready, 1)

    def pair_body(i, last):
        def normalise(c):
            dve.wait_ge(s.exped, 8 * i + 32 + 4 * c + 4)
            st.link(V.reciprocal(b.rec[:, 4 * c:4 * c + 4], b.sums[:, 4 * c:4 * c + 4]))
            for qb in range(TT):
                sc = b.s[:, c, pairs_offset(qb):pairs_offset(qb + 1)]
                V.tensor_scalar(sc, sc, b.rec[:, 4 * c + qb:4 * c + qb + 1], None, ALU.mult).then_inc(s.blended, 1)

        def turned_rest(c, blocks):
            for kb in blocks:
                w = (TT - kb) * P
                at = turned_offset(kb)
                dve.wait_ge(s.turned_hi, 8 * i + 16 + 4 * c + kb + 1)
                V.tensor_tensor(b.tl[:, at:at + w], b.ps[:, 5 + kb % 2, 0:w], f32(b.th[:, at:at + w]),
                                ALU.subtract).then_inc(s.turned_ready, 1)

        def out(c):
            dve.wait_ge(s.pv_done, 2 * i + 4 + c + 1)
            part = slice(64 * c, 64 * c + 64)
            V.tensor_copy(b.oa[part, i, :], b.ps[part, 7 if c else 4, :]).then_inc(s.o_evac, 1)

        def evac(u):
            p = Panel(P_PAIRS + u, RING, i)
            slot = (E_PAIRS + u) % 4
            if u == 0:
                evac_row(p, 0, b.zg[:, i, :], slot)
            elif u == 1:
                evac_row(p, 0, b.rg[:, i, :], slot)
            else:
                dve.wait_ge(s.panel_done, p.index + 1)
                V.tensor_tensor(b.kx[:, 2 * i + u - 2, :], b.ps[:, slot, 0:M], b.mrow[:],
                                ALU.mult).then_inc(s.evac, 1)

        dve.wait_ge(s.bias_in, 16 * i + 80)
        score_rows(i, 0, 4, b.bias2[:, 0, :], (0, 1))
        lo(Panel(P_PAIRS - 1 + RING, RING, i))
        score_rows(i, 0, 4, b.bias2[:, 0, :], (2, 3))
        score_rows(i, 1, 4, b.bias2[:, 1, :], (0, 1))
        normalise(0)
        score_rows(i, 1, 4, b.bias2[:, 1, :], (2, 3))
        evac(0)
        dve.wait_ge(s.v_hi, i + 5)
        v = b.v[:, :, P * i:P * i + P] if last else b.v[:, :, bass.ds(P * i, P)]
        V.tensor_tensor(b.vl[:], v, f32(b.vh[:]), ALU.subtract).then_inc(s.v_ready, 1)
        turned_rest(0, (0, 1))
        lo(Panel(P_PAIRS + RING, RING, i))
        turned_rest(0, (2, 3))
        normalise(1)
        evac(1)
        out(0)
        turned_rest(1, (0, 1))
        lo(Panel(P_PAIRS + 1 + RING, RING, i))
        turned_rest(1, (2, 3))
        if not last:
            pair_parts(i + 1)
        evac(2)
        lo(Panel(P_PAIRS + 2 + RING, RING, i))
        dve.wait_ge(s.gated, i + 25)
        dve.wait_ge(s.evac, 4 * i + E_PAIRS + 2)
        V.scalar_tensor_tensor(b.rg[:, i, :], b.tmp[:, 0, :], 1.0, b.rg[:, i, :], ALU.add,
                               ALU.mult).then_inc(s.silued, 1)
        out(1)
        evac(3)
        if last:
            lo(Panel(P_PAIRS + 3 + RING, RING, i))

    evac_tokens(P_VA2, E_VA2, 3, b.v, (lambda: None, lambda: None, lambda: pair_parts(0)))
    dve.wait_ge(s.mrow_ready, 1)
    with dve.Fori(0, 3) as i:
        st.enter(i, PAIR_STEPS)
        pair_body(i, False)
    st.leave(3)
    pair_body(3, True)

    dve.wait_ge(s.evac, E_PAIRS + 16)
    V.tensor_scalar(b.zg[:, 0:2, :], b.zg[:, 0:2, :], 0.125, None, ALU.mult).then_inc(s.q_scaled, 1)
    dve.wait_ge(s.score_done, 64)
    st.link(V.memset(b.reset[:], 1.0))
    st.mark(V.memset(b.reset[:, 0::CHUNK], 0.0))
    evac_row(Panel(P_GLR), 0, b.glr[:], E_GLR % 4)
    lo(Panel(P_GLR + RING))
    for r in range(2):
        dve.wait_ge(s.logit_abs, r + 1)
        st.mark(V.tensor_scalar(b.b[:, r, :], b.ps[:, 6 + r, :], col(b, "b_gate2", r), 0.0, ALU.add, ALU.min))
    q = b.zg[:, 0:2, :].rearrange("p r t -> p (r t)")
    k = b.zg[:, 2:4, :].rearrange("p r t -> p (r t)")
    run = b.b[:].rearrange("p r t -> p (r t)")
    qb, kd = (ap.rearrange("p r t -> p (r t)") for ap in (b.qb[:], b.diag[:]))

    def running_sums():
        dve.wait_ge(s.soft_ready, 1)
        st.wait()
        st.link(V.tensor_tensor(b.b[:], b.b[:], b.la[:], ALU.subtract))
        for r in range(2):
            V.tensor_tensor_scan(b.b[:, r, :], b.reset[:], b.b[:, r, :], 0.0, ALU.mult,
                                 ALU.add).then_inc(s.b_ready, 1)

    def key_decay():
        dve.wait_ge(s.b_ready, 2)
        dve.wait_ge(s.mrow_done, 1)
        chunks = run.rearrange("p (c t) -> p c t", t=CHUNK)
        V.tensor_tensor(kd.rearrange("p (c t) -> p c t", t=CHUNK),
                        chunks[:, :, CHUNK - 1:CHUNK].to_broadcast([P, 2 * NC, CHUNK]), chunks,
                        ALU.subtract).then_inc(s.kd_shift, 1)
        normed_x((0, 1, 2, 3))

    def decayed_keys():
        dve.wait_ge(s.kd_exped, 1)
        V.tensor_tensor(kd, kd, k, ALU.mult).then_inc(s.kd_ready, 1)
        dve.wait_ge(s.silued, 5)
        dve.wait_ge(s.q_scaled, 1)
        V.tensor_tensor(b.tmp[:].rearrange("p r t -> p (r t)"), q, k, ALU.mult).then_inc(s.qk_product, 1)

    def normed_x(chunks):
        dve.wait_ge(s.rowa_ready, 1)
        for c in chunks:
            st.mark(V.scalar_tensor_tensor(b.x[:, c, :], b.x[:, c, :], col(b, "final_norm_g", c), b.rowa[:],
                                           ALU.mult, ALU.mult))

    evac_tokens(P_VG, E_VG, 6, b.vg, (running_sums, key_decay, decayed_keys))
    lo(Panel(P_VG + 3 + RING))
    dve.wait_ge(s.late_in, 32)
    dve.wait_ge(s.a_cleared, 2)
    for h in range(4):
        dve.wait_ge(s.level_done, h + 1)
        V.copy_predicated(b.a[:, h // 2, :, h % 2, :],
                          b.masks[:, 0, :].bitcast(U32).unsqueeze(1).to_broadcast([P, TT, P]),
                          b.ps[:, 4 + h, :].rearrange("p (t q) -> p t q", t=TT)).then_inc(s.level_taken, 1)
    dve.wait_ge(s.b_exped, 1)
    dve.wait_ge(s.q_scaled, 1)
    V.tensor_tensor(qb, qb, q, ALU.mult).then_inc(s.qb_ready, 1)

    def xv_slot(m):
        dve.wait_ge(s.panel_done, P_XV + m + 1)
        if m % 4 == 3:
            for t in range(MT):
                V.tensor_scalar(b.vx[:, t, 512 * (m // 4):512 * (m // 4) + 512], bank(E_XV + 2 * (m // 4) + t),
                                b.mrs[:, t:t + 1], None, ALU.mult).then_inc(s.evac, 1)

    def shift(n):
        if n >= 2:
            dve.wait_ge(s.level_ready, n - 1)
        v, _, _ = level_views(run, LEVELS[n])
        d, _, _ = level_views(b.ee[:, n % 2, :], LEVELS[n])
        ref = v[:, :, LEVELS[n] - 1:LEVELS[n]].to_broadcast([P, T // LEVELS[n], 2 * LEVELS[n]])
        V.tensor_tensor(d, v, ref, ALU.subtract).then_inc(s.shifted, 1)

    def apply(n):
        level = n + 1
        dve.wait_ge(s.level_exped, 2 * n + 2)
        if level >= 3:
            dve.wait_ge(s.level_done, 4 + 2 * (level - 2))
        _, e1, e2 = level_views(b.ee[:, n % 2, :], LEVELS[n])
        _, _, q2 = level_views(q, LEVELS[n])
        _, k1, _ = level_views(k, LEVELS[n])
        _, ke1, _ = level_views(b.ke[:, level % 2, :], LEVELS[n])
        for a in range(2):
            part = slice(64 * a, 64 * a + 64)
            dst = b.qe[part, level % 2, :, a, :]
            if LEVELS[n] < 64:
                dst = dst.rearrange("p c (n w) -> p c n w", w=LEVELS[n])
                src = [v[part].rearrange("p (c n) w -> p c n w", c=2 * TT) for v in (q2, e2)]
            else:
                src = [q2[part], e2[part]]
            st.mark(V.tensor_tensor(dst, src[0], src[1], ALU.mult))
        st.wait()
        V.tensor_tensor(ke1, k1, e1, ALU.mult).then_inc(s.level_ready, 1)

    def take(level):
        size = LEVELS[level - 1]
        mask = b.masks[:, level, :].bitcast(U32).rearrange("p (n w) -> p n w", w=2 * size)[:, :, size:]
        for r in range(2):
            dve.wait_ge(s.level_done, 4 + 2 * (level - 1) + r + 1)
            dve.wait_ge(s.level_taken, 2 * level + r + 1 if level > 1 else 4)
            dst = b.a[:, r, :, :, :].rearrange("p t a (n w) -> p (t a) n w", w=2 * size)
            src = b.ps[:, (4 if level % 2 else 6) + r, :].rearrange("p (c n w) -> p c n w", c=2 * TT, w=size)
            V.copy_predicated(dst[:, :, :, size:], mask.unsqueeze(1).to_broadcast([P, 2 * TT, 64 // size, size]),
                              src).then_inc(s.level_taken, 1)

    shift(0)
    xv_slot(0)
    shift(1)
    dve.wait_ge(s.ke_cleared, 1)
    apply(0)
    dve.wait_ge(s.last_exped, 1)
    for c in range(NC - 1):
        for r in range(2):
            dve.wait_ge(s.updates_done, r + 1)
            upd = b.ps[:, 4 + r, P * c:P * c + P]
            if c == 0:
                ins = V.tensor_copy(b.states[:, r, 1, :], upd)
            else:
                dve.wait_ge(s.states_ready, 2 * c - 1 + r)
                ins = V.scalar_tensor_tensor(b.states[:, r, c + 1, :], b.states[:, r, c, :],
                                             b.ebl[:, NC * r + c:NC * r + c + 1], upd, ALU.mult, ALU.add)
            ins.then_inc(s.states_ready, 1)
    for n in range(len(LEVELS)):
        if n:
            apply(n)
        if n + 2 < len(LEVELS):
            shift(n + 2)
        if n:
            take(n)
        xv_slot(1 + n)
    take(len(LEVELS))

    for k in range(4):
        dve.wait_ge(s.y_hi, k + 1)
        V.tensor_tensor(b.yl2[:, k, :], b.oa[:, k, :], f32(b.yh2[:, k, :]), ALU.subtract).then_inc(s.y_ready, 1)
    normed_x((4, 5, 6, 7))
    for n, h in enumerate(HEAD_ORDER):
        dve.wait_ge(s.og_squared, n + 1)
        V.tensor_tensor(b.og[:, h, :], b.ps[:, 4 + h, :], b.rg[:, h, :], ALU.mult).then_inc(s.og_evac, 1)
    dve.wait_ge(s.gcol_done, 4)
    V.tensor_scalar(b.gmean, b.ps[:, 6, 0:16], 1.0 / P, 1e-6, ALU.mult, ALU.add).then_inc(s.gmean_ready, 1)
    dve.wait_ge(s.gpow_done, 1)
    for h in range(4):
        if h >= 2:
            dve.wait_ge(s.grow_done, h - 1)
        diagonal(b.diag[:, h % 2, :], b.grs[:, 4 * h:4 * h + 4]).then_inc(s.gdiag_ready, 1)
    for h in range(4):
        dve.wait_ge(s.grow_done, h + 1)
        dve.wait_ge(s.og_evac, 4)
        V.tensor_tensor(b.og[:, h, :], b.og[:, h, :], b.ps[:, 4 + h, :], ALU.mult).then_inc(s.og_normed, 1)
    for h in range(4):
        dve.wait_ge(s.y_hi, 4 + h + 1)
        V.scalar_tensor_tensor(b.yl2[:, 4 + h, :], b.og[:, h, :], b.half_gn, f32(b.yh2[:, 4 + h, :]),
                               ALU.mult, ALU.subtract).then_inc(s.y_ready, 1)

    dve.wait_ge(s.lo_ready, P_WOUT2 + RING)
    residual_loop(P_WOUT2, E_WOUT2, "norm_xattn", 3)

    def norm_row(n):
        mean(n)
        dve.wait_ge(s.pow_done, n)
        diagonal(b.diag[:, 0, :], b.rs).then_inc(s.diag_ready, 1)

    def key_rest(h):
        dve.wait_ge(s.xk_hi, h + 1)
        V.tensor_tensor(b.kxl[:], b.kx[:, 2 * h:2 * h + 2, :], f32(b.kxh[:]), ALU.subtract).then_inc(s.xk_ready, 1)

    def value_rest(h):
        dve.wait_ge(s.xv_hi, h + 1)
        V.tensor_tensor(b.vxl[:], b.vx[:, :, 256 * h:256 * h + 256], f32(b.vxh[:]), ALU.subtract).then_inc(
            s.xv_ready, 1)

    def q_chunk(j):
        if j >= 2:
            dve.wait_ge(s.xq_ready, j - 1)
        evac_row(Panel(P_XQ + j), 0, b.tmp[:, j % 2, :], (E_XQ + j) % 4)

    def q_rest(j):
        dve.wait_ge(s.xq_hi, j + 1)
        dve.wait_ge(s.evac, E_XQ + j + 1)
        V.scalar_tensor_tensor(b.qxl[:, j % 2, :], b.tmp[:, j % 2, :], XSCALE, f32(b.qxh[:, j % 2, :]),
                               ALU.mult, ALU.subtract).then_inc(s.xq_ready, 1)

    def maxima(h):
        for half in range(2):
            dve.wait_ge(s.xscore_done, 4 * h + 2 * half + 2)
            if h:
                dve.wait_ge(s.xneg, h)
            st.mark(V.tensor_reduce(b.mx[:, 2 * half:2 * half + 2],
                                    b.ps[:, 4 + half, :].rearrange("p (a m) -> p a m", a=2), AX_X, ALU.max))
        st.wait()
        V.tensor_scalar(b.neg[:, 0:4], b.mx[:, 0:4], -1.0, None, ALU.mult).then_inc(s.xneg, 1)

    def normalise_x(h):
        dve.wait_ge(s.xexped, 4 * h + 4)
        st.link(V.reciprocal(b.rec[:, 0:4], b.sums[:, 0:4]))
        for qb in range(TT):
            V.tensor_scalar(b.xs[:, qb, :], b.xs[:, qb, :], b.rec[:, qb:qb + 1], None,
                            ALU.mult).then_inc(s.xblended, 1)

    def turned_rest_x(h):
        for mt in range(MT):
            dve.wait_ge(s.xturned_hi, 2 * h + mt + 1)
            V.tensor_tensor(b.xtl[:, mt, :], b.ps[:, 6 + mt, :], f32(b.xth[:, mt, :]),
                            ALU.subtract).then_inc(s.xturned_ready, 1)

    def out_rest(h):
        for d in range(2):
            dve.wait_ge(s.ox_hi, 2 * h + d + 1)
            V.tensor_tensor(b.oxl[:, 2 * h + d, :], b.ps[:, 6 + d, :], f32(b.oxh[:, 2 * h + d, :]),
                            ALU.subtract).then_inc(s.ox_ready, 1)

    norm_row(4)
    dve.wait_ge(s.row_ready, 4)
    for j in range(8):
        h = j // 2
        if j % 2 == 0 and h:
            if h >= 2:
                out_rest(h - 2)
            maxima(h - 1)
            if h >= 2:
                value_rest(h - 1)
            normalise_x(h - 1)
        if j % 2 and h:
            turned_rest_x(h - 1)
        q_chunk(j)
        if j == 0:
            lo(Panel(P_XQ + j + RING))
            key_rest(0)
            value_rest(0)
        elif j % 2 == 0:
            key_rest(h)
        q_rest(j)
        if j:
            lo(Panel(P_XQ + j + RING))
    out_rest(2)
    maxima(3)
    value_rest(3)
    normalise_x(3)
    turned_rest_x(3)
    out_rest(3)

    residual_loop(P_XO, E_XO, "norm_mlp", 4)

    def rest(j, half, base):
        dve.wait_ge(s.act2_hi, base + j + 1)
        dve.wait_ge(s.acted2, base + j + 1)
        V.tensor_tensor(b.al2[:, j, :], b.tmp[:, half, :], f32(b.ah2[:, j, :]), ALU.subtract).then_inc(
            s.act2_ready, 1)

    def up_body(p0, e0, i, base):
        for u in range(4):
            j = 4 * i + u
            evac_row(Panel(p0 + u, RING, i), 0, b.tmp[:, u % 2, :], (e0 + u) % 4)
            lo(Panel(p0 + u + RING, RING, i))
            dve.wait_ge(s.evac, e0 + j + 1)
            V.scalar_tensor_tensor(b.tmp[:, u % 2, :], b.tmp[:, u % 2, :], 0.0, b.tmp[:, u % 2, :], ALU.max,
                                   ALU.mult).then_inc(s.acted2, 1)
            rest(j, u % 2, base)

    def down_loop(p0, e0, last):
        def body(i):
            for c in range(4):
                k = 4 * i + c
                for m in range(2):
                    p = Panel(p0 + 2 * c + m, 8, i)
                    dve.wait_ge(s.panel_done, p.index + 1)
                    if m == 1:
                        V.tensor_tensor(b.x[:, k, :], b.x[:, k, :], b.ps[:, (e0 + c) % 4, :],
                                        ALU.add).then_inc(s.evac, 1)
                    lo(p.plus(RING))
                if last:
                    x_sum(c % 2, 40 + k + 1, 46 + k)

        if last:
            body(0)
            body(1)
        else:
            with dve.Fori(0, 2) as i:
                body(i)

    norm_row(5)
    dve.wait_ge(s.row_ready, 5)
    with dve.Fori(0, FH // 4) as i:
        up_body(P_UP_A, E_UP_A, i, 0)
    down_loop(P_DOWN_A, E_DOWN_A, False)
    with dve.Fori(0, FH // 4) as i:
        up_body(P_UP_B, E_UP_B, i, FH)
    V.memset(b.sumsq[:], 0.0).then_inc(s.sums, 1)
    down_loop(P_DOWN_B, E_DOWN_B, True)

    norm_row(6)
    dve.wait_ge(s.row_done, 6)
    dve.wait_ge(s.evac, E_END)
    for k in range(KT):
        V.scalar_tensor_tensor(b.x[:, k, :], b.x[:, k, :], col(b, "norm_final", k), b.ps[:, 7, :], ALU.mult,
                               ALU.mult).then_inc(s.final_scaled, 1)


def block2_tensor(nc, pe, s, b, MM, three, begin, w, features, column_sums, row, x_ready, tokens, score, turn,
                  values, four_chunks, second_chunks):
    def norm_rows():
        row(3)
        pe.wait_ge(s.diag_a, 1)
        MM(b.ps[:, 6, :], b.ones, b.diag[:, 1, :], start=True, stop=True).then_inc(s.rowa_done, 1)

    def memory_row():
        pe.wait_ge(s.mdiag_ready, 1)
        MM(b.ps[:, 5, 0:M], b.ones, b.diag[:, 1, 0:M], start=True, stop=True).then_inc(s.mrow_done, 1)

    for u in range(8):
        features(Panel(P_QA + u), E_QA + u, (E_QA + u) % 4, ready=x_ready(16) if u == 0 else None,
                 between={3: {1: [norm_rows]}, 7: {4: [memory_row]}}.get(u))
        if u == 0:
            pe.wait_ge(s.sums2, 9)
            pe.wait_ge(s.row_ready, 2)
            for t in range(TT):
                MM(b.ps[:, 7, 4 + t:5 + t], b.sum2[:, P * t:P * t + P], b.ones[:, 0:1], start=True, stop=True)
            column_sums(3, 27)
        if u == 4:
            pe.wait_ge(s.mem_sums, 1)
            for t in range(MT):
                ins = MM(b.ps[:, 5, t:t + 1], b.msum[:, P * t:P * t + P], b.ones[:, 0:1], start=True, stop=True)
            ins.then_inc(s.mcol_done, 1)
    tokens(P_VA2, E_VA2, s.v_done)

    pe.wait_ge(s.mem_ready, 1)
    pe.wait_ge(s.mrow_ready, 1)
    pe.wait_ge(s.rowa_ready, 1)

    def pair_body(i):
        def sc(n):
            return lambda: score(4 + i, n)

        def tn(c, kb):
            return lambda: turn(4 + 2 * i + c, kb, c)

        def start():
            pe.wait_ge(s.qk_ready, i + 5)
            pe.wait_ge(s.o_evac, 2 * i + 3)

        def first_values():
            values(4 + 2 * i, 4 + i, 4)

        def all_scored():
            pe.wait_ge(s.scored, 8 * i + 40)

        def second_values():
            pe.wait_ge(s.o_evac, 2 * i + 4)
            values(5 + 2 * i, 4 + i, 7)

        between = ({0: [start, sc(0), sc(1)], 1: [sc(2)], 2: [sc(3)], 3: [sc(4)], 4: [sc(5)], 6: [sc(6)], 7: [sc(7)]},
                   {2: [all_scored, tn(0, 0), tn(0, 1)], 4: [tn(0, 2)], 5: [tn(0, 3)], 7: [first_values]},
                   {2: [tn(1, 0), tn(1, 1)], 6: [tn(1, 2)]},
                   {0: [tn(1, 3)], 4: [second_values]})
        for u in range(4):
            moving = {} if u < 2 else {"xh": b.memh, "xl": b.meml, "width": M}
            features(Panel(P_PAIRS + u, RING, i), E_PAIRS + u + RING * i, (E_PAIRS + u) % 4,
                     between=between[u], **moving)

    with pe.Fori(0, 3) as i:
        pair_body(i)
    pair_body(3)

    features(Panel(P_GLR), E_GLR, E_GLR % 4)
    pe.wait_ge(s.late_in, 32)
    pe.wait_ge(s.evac, E_GLR + 1)
    pe.wait_ge(s.turned_ready, 48)
    pe.wait_ge(s.o_evac, 12)
    for r in range(2):
        MM(b.ps[:, 6 + r, :], b.wgu[0:16, P * r:P * r + P], b.glr[0:16, :], start=True,
           stop=True).then_inc(s.logit_done, 1)
    tokens(P_VG, E_VG, s.v_done)
    pe.wait_ge(s.qk_product, 1)
    pe.wait_ge(s.b_ready, 2)
    for h in range(4):
        part = slice(64 * (h % 2), 64 * (h % 2) + 64)
        MM(b.ps[:, 4 + h, :], b.ones[part, :], b.tmp[part, h // 2, :], start=True, stop=True).then_inc(s.level_done, 1)

    def xv(m):
        p = Panel(P_XV + m)
        begin(p, None)
        half = m // 4
        for t in range(MT):
            e = E_XV + 2 * half + t
            if m % 4 == 0:
                pe.wait_ge(s.evac, e - 3)
            for n in range(2):
                k = 2 * (m % 4) + n
                wh, wl = w(p, 512 * n, 512)
                tok = slice(P * t, P * t + P)
                ins = three(b.ps[:, e % 4, :], b.memh[:, k, tok], b.meml[:, k, tok], wh, wl, k == 0, k == KT - 1)
        ins.then_inc(s.panel_done, 1)

    xv(0)
    pe.wait_ge(s.kd_ready, 1)
    pe.wait_ge(s.level_taken, 4)
    for r in range(2):
        for t in range(TT):
            ins = nc.tensor.transpose(b.ps[:, 4 + r, P * t:P * t + P], b.diag[:, r, P * t:P * t + P], b.ident)
    ins.then_inc(s.kd_turned, 1)
    xv(1)
    pe.wait_ge(s.kd_copied, 1)
    for r in range(2):
        for c in range(NC - 1):
            for a in range(2):
                head = 2 * r + a
                ins = MM(b.ps[64 * a:64 * a + 64, 4 + r, P * c:P * c + P], b.kdt[:, r, c, 64 * a:64 * a + 64],
                         b.vg[:, c, P * head:P * head + P], start=True, stop=True, skip_group_check=True)
        ins.then_inc(s.updates_done, 1)
    for level in range(1, len(LEVELS) + 1):
        pe.wait_ge(s.level_ready, level)
        for r in range(2):
            if level == 1:
                pe.wait_ge(s.states_ready, 2 * (NC - 1))
            elif level >= 3:
                pe.wait_ge(s.level_taken, 4 + 2 * (level - 3) + r + 1)
            for n in range(TT):
                c = TT * r + n
                ins = MM(b.ps[:, (4 if level % 2 else 6) + r, P * n:P * n + P], b.ke[:, level % 2, P * c:P * c + P],
                         b.qe[:, level % 2, c, :, :], start=True, stop=True)
            ins.then_inc(s.level_done, 1)
        if level < len(LEVELS):
            xv(1 + level)
    pe.wait_ge(s.qb_ready, 1)

    def from_states(h):
        r, part = h // 2, slice(64 * (h % 2), 64 * (h % 2) + 64)
        for c in range(1, NC):
            tok = slice(CHUNK * c, CHUNK * c + CHUNK)
            MM(b.ps[:, 4 + h, tok], b.states[part, r, c, :], b.qb[part, r, tok], start=c == 1,
               stop=False, skip_group_check=True)

    def within(h):
        for t in range(TT):
            tok = slice(P * t, P * t + P)
            ins = MM(b.ps[:, 4 + h, tok], b.vg[:, t, P * h:P * h + P], b.a[:, h // 2, t, h % 2, :], start=False,
                     stop=t == TT - 1, skip_group_check=True)
        ins.then_inc(s.og_done, 1)

    pe.wait_ge(s.level_taken, 4 + 2 * len(LEVELS) - 2)
    from_states(2)
    from_states(3)
    pe.wait_ge(s.level_taken, 4 + 2 * len(LEVELS))
    within(2)
    within(3)
    for h in (0, 1):
        from_states(h)
        within(h)

    def gated_columns():
        for n, h in enumerate(HEAD_ORDER):
            pe.wait_ge(s.og_squared, n + 1)
            if n == 0:
                pe.wait_ge(s.og_evac, 1)
            for t in range(TT):
                ins = MM(b.ps[:, 6, 4 * h + t:4 * h + t + 1], b.gsq[:, h, P * t:P * t + P], b.ones[:, 0:1],
                         start=True, stop=True)
            ins.then_inc(s.gcol_done, 1)

    def gated_rows():
        for h in range(4):
            pe.wait_ge(s.gdiag_ready, h + 1)
            pe.wait_ge(s.og_evac, 4)
            MM(b.ps[:, 4 + h, :], b.ones, b.diag[:, h % 2, :], start=True, stop=True).then_inc(s.grow_done, 1)

    four_chunks(P_WOUT2, E_WOUT2, b.yh2, b.yl2, lambda k: pe.wait_ge(s.y_ready, k + 1),
                {(0, 1): gated_columns, (0, 3): gated_rows})
    second_chunks(P_WOUT2, E_WOUT2, b.yh2, b.yl2)

    def xscores(h):
        pe.wait_ge(s.xk_ready, h + 1)
        pe.wait_ge(s.xq_ready, 2 * h + 2)
        if h:
            pe.wait_ge(s.xexped, 4 * h)
        for qb in range(TT):
            tok = slice(P * qb, P * qb + P)
            for d in range(2):
                ins = three(b.ps[:, 4 + qb // 2, M * (qb % 2):M * (qb % 2) + M], b.qxh[:, d, tok], b.qxl[:, d, tok],
                            b.kxh[:, d, :], b.kxl[:, d, :], d == 0, d == 1)
            ins.then_inc(s.xscore_done, 1)

    def xturn(h):
        pe.wait_ge(s.xblended, 4 * h + 4)
        if h:
            pe.wait_ge(s.ox_ready, 2 * h)
        for mt in range(MT):
            for qb in range(TT):
                ins = nc.tensor.transpose(b.ps[:, 6 + mt, P * qb:P * qb + P], b.xs[:, qb, P * mt:P * mt + P], b.ident)
            ins.then_inc(s.xturned, 1)

    def xvalues(h):
        pe.wait_ge(s.xturned_ready, 2 * h + 2)
        pe.wait_ge(s.xv_ready, h + 1)
        for d in range(2):
            for mt in range(MT):
                ins = three(b.ps[:, 6 + d, :], b.vxh[:, mt, P * d:P * d + P], b.vxl[:, mt, P * d:P * d + P],
                            b.xth[:, mt, :], b.xtl[:, mt, :], mt == 0, mt == MT - 1)
            ins.then_inc(s.xpv_done, 1)

    for j in range(8):
        h = j // 2
        between = {}
        if j == 1:
            between = {4: [lambda: row(4)]}
        elif j % 2 and h:
            between = {5: [lambda: xturn(h - 1)]}
        elif h:
            between = {5: [lambda: xscores(h - 1)]}
            if h >= 2:
                between[2] = [lambda: xvalues(h - 2)]
        features(Panel(P_XQ + j), E_XQ + j, (E_XQ + j) % 4, ready=x_ready(24) if j == 0 else None, between=between)
        if j == 0:
            column_sums(4, 36)

    four_chunks(P_XO, E_XO, b.oxh, b.oxl, lambda k: pe.wait_ge(s.ox_ready, k + 1),
                {(0, 0): lambda: xvalues(2), (0, 1): lambda: xscores(3), (0, 3): lambda: xturn(3),
                 (1, 0): lambda: xvalues(3)})
    second_chunks(P_XO, E_XO, b.oxh, b.oxl)

    def up_body(p0, e0, i, first):
        for u in range(4):
            features(Panel(p0 + u, RING, i), e0 + u + RING * i, (e0 + u) % 4,
                     ready=x_ready(32) if first and u == 0 else None,
                     between={1: [lambda: row(5)]} if first and u == 2 else None)
            if first and u == 0:
                column_sums(5, 45)

    def down_loop(p0, e0, base):
        with pe.Fori(0, 2) as i:
            for c in range(4):
                for m in range(2):
                    features(Panel(p0 + 2 * c + m, 8, i), e0 + c + 4 * i if m == 0 else None, (e0 + c) % 4,
                             xh=b.ah2, xl=b.al2, tiles=range(KT * m, KT * m + KT), last=FH,
                             ready=(lambda k: pe.wait_ge(s.act2_ready, base + k + 1)) if c == 0 else None)

    up_body(P_UP_A, E_UP_A, 0, True)
    with pe.Fori(1, FH // 4) as i:
        up_body(P_UP_A, E_UP_A, i, False)
    down_loop(P_DOWN_A, E_DOWN_A, 0)
    with pe.Fori(0, FH // 4) as i:
        up_body(P_UP_B, E_UP_B, i, False)
    down_loop(P_DOWN_B, E_DOWN_B, FH)
    column_sums(6, 54)
    row(6)


def tiles(w):
    return w.reshape(-1, P, w.shape[1])


def chunk_panels(w):
    k, n = w.shape
    return w.reshape(k // P, P, n // P, P).transpose(2, 1, 0, 3).reshape(n // P, P, -1)


def row_panels(w):
    k, n = w.shape
    return w.reshape(k * n // (P * D), D // n, P, n).transpose(0, 2, 1, 3).reshape(-1, P, D)


def down_panels(w, parts):
    per = chunk_panels(w).reshape(w.shape[1] // P, P, -1, P)
    out = np.zeros((per.shape[0], len(parts), P, KT, P), w.dtype)
    at = 0
    for m, n in enumerate(parts):
        out[:, m, :, :n] = per[:, :, at:at + n]
        at += n
    return out.reshape(-1, P, D)


def vector(v):
    return v.reshape(-1, P).T


def shape_constants():
    consts = np.stack([np.eye(P, dtype=np.float32), np.ones((P, P), np.float32)], 1)
    windows = np.repeat(np.array([2, 4, 8, 16]), 64).reshape(2, P).T
    t = np.arange(T)
    inv = (1.0 / np.minimum(t[None, None] + 1, windows[:, :, None])).astype(np.float32)
    rel = T - 1 - np.arange(T)
    large = 16 + (np.log(np.maximum(rel, 1) / 16) / np.log(8) * 16).astype(int)
    bucket = np.where(rel < 16, rel, np.minimum(large, NB - 1))
    onehot = (bucket[None] == np.arange(NB)[:, None]).astype(np.float32)
    return consts, inv, onehot


def level_masks():
    j, i = np.arange(P)[:, None], np.arange(P)[None]
    masks = [j == i]
    for n in LEVELS:
        masks.append((j // (2 * n) == i // (2 * n)) & (j // n % 2 == 0) & (i // n % 2 == 1))
    return np.stack(masks, 1).astype(np.float32)


def layout(a):
    w_in, gate, up = a["w_in"][0], a["w_gate"][0], a["w_up"][0]
    gate_up = np.stack([chunk_panels(up[:, :FF1]), chunk_panels(up[:, FF1:])], 1).reshape(-1, P, D)
    projections = np.concatenate([a["proj_a"][0], a["proj_b"][0], a["proj_c"][0]], 0)
    stream = [chunk_panels(w_in[:, 0:256]), row_panels(w_in[:, 256:512]), chunk_panels(w_in[:, 512:768]),
              chunk_panels(w_in[:, 768:1792]), row_panels(w_in[:, 1792:2304]), chunk_panels(gate),
              chunk_panels(projections), chunk_panels(a["w_out"][0]), gate_up, down_panels(a["w_down"][0], DOWN1)]
    w2, xkv = a["w_in_2"][0], a["w_xkv_2"][0]
    glr = chunk_panels(w2[:, 2560:2560 + P])
    qk_g = chunk_panels(w2[:, 1536:2048])
    r_g = chunk_panels(w2[:, 2576:3088])
    xk = chunk_panels(xkv[:, 0:D])
    pairs = np.stack([qk_g, r_g, xk[0::2], xk[1::2]], 1).reshape(-1, P, D)
    w_up2, w_down2 = a["w_up_2"][0], a["w_down_2"][0]
    half = FF2 // 2
    stream += [chunk_panels(w2[:, 0:1024]), row_panels(w2[:, 1024:1536]), pairs, glr,
               row_panels(w2[:, 2048:2560]), row_panels(xkv[:, D:D + 512]), row_panels(xkv[:, D + 512:2 * D]), chunk_panels(a["w_out_2"][0]),
               chunk_panels(a["w_xq_2"][0]), chunk_panels(a["w_xo_2"][0])]
    for n in range(2):
        stream += [chunk_panels(w_up2[:, half * n:half * n + half]),
                   down_panels(w_down2[half * n:half * n + half], (KT, KT))]
    vec = [a["attn_norm_g"][0], a["b_gate"][0], a["ffn_norm_g"][0], a["conv_w"][0, 0], a["conv_w"][0, 1],
           a["conv_w"][0, 2], a["conv_b"][0], a["final_norm_g"], a["diff_subln_g"][0], a["pool_scale"][0],
           a["norm_mix_2"][0], a["b_gate_2"][0], a["g_norm_2"][0], a["norm_xattn_2"][0], a["norm_mem_2"][0],
           a["norm_mlp_2"][0], a["norm_final_2"]]
    consts, inv, onehot = shape_constants()
    sgu_b = np.repeat(a["sgu_b"][0].reshape(2, 2, P), 64, axis=1).transpose(1, 0, 2).reshape(P, 256)
    wide = np.concatenate([a["sgu_ln_g"][0], a["sgu_ln_b"][0], a["diff_lam"][0].reshape(-1)])
    early = np.concatenate([sgu_b, np.broadcast_to(wide, (P, wide.size))], 1)
    tables = np.concatenate([a["rel_bias"], a["rp_table_2"]], 1)
    return {
        "stream": np.concatenate(stream, 0),
        "late": np.concatenate([level_masks().reshape(P, -1)], 1),
        "wgu": a["w_gate_up_2"][0],
        "mem": a["mem_2"][0].T.reshape(KT, P, M).transpose(1, 0, 2),
        "x": a["x"][0].T.reshape(KT, P, T).transpose(1, 0, 2),
        "vec": np.concatenate([vector(v) for v in vec], 1),
        "consts": consts, "inv_count": inv, "onehot": onehot, "early": early,
        "tables": np.repeat(tables, P, axis=1),
        "sgu_w": a["sgu_w"][0].transpose(2, 0, 1),
        "pool_w": a["pool_w"][0].reshape(2, P, 64).transpose(1, 0, 2),
    }


def kernel(**inputs):
    import concourse.bacc as bacc
    from concourse.bass_utils import run_bass_kernel_spmd

    arrays = {f"{k}_dram": np.ascontiguousarray(v) for k, v in layout({k: np.asarray(v) for k, v in inputs.items()}).items()}
    nc = bacc.Bacc("TRN2", target_bir_lowering=False, num_devices=1, dynamic_dma_scratch_size=1024)
    dram = {k[:-5]: nc.dram_tensor(k, v.shape, mybir.dt.from_np(v.dtype), kind="ExternalInput").ap()
            for k, v in arrays.items()}
    out = nc.dram_tensor("out_dram", (D, T), F32, kind="ExternalOutput").ap()
    build(nc, dram, out)
    got = run_bass_kernel_spmd(nc, [arrays], core_ids=[0]).results[0]["out_dram"]
    return np.ascontiguousarray(got.T).reshape(1, T, D)
```
